# Optimizing a Trainium2 kernel written in Bass

```python
import jax, jax.numpy as jnp
from jax import lax
import numpy as np

D_MODEL = 1024
BATCH = 1
SEQ = 256
DEPTH = 1
DEC_BATCH = 8
DEC_SEQ = 4
PAST_LEN = 256
PAGE_SIZE = 128

HEAD_DIM = 64
H_A = 8
HKV_A = 1
G_A = H_A // HKV_A
H_IDX = 8
D_IDX = 64
TOPK_A_MAX = 256
H_B = 8
HKV_B = 2
G_B = H_B // HKV_B
MOBA_BLOCK = 256
TOPK_B = 3
D_FF = 2752
ROPE_THETA = 10000.0
EPS = 1e-6
Q_BLOCK = 128

W_QA = H_A * HEAD_DIM
W_KA = HKV_A * HEAD_DIM
W_VA = HKV_A * HEAD_DIM
W_QI = H_IDX * D_IDX
W_KI = D_IDX
W_WI = H_IDX
W_QB = H_B * HEAD_DIM
W_KB = HKV_B * HEAD_DIM
W_VB = HKV_B * HEAD_DIM
N_IN = W_QA + W_KA + W_VA + W_QI + W_KI + W_WI + W_QB + W_KB + W_VB + 2 * D_MODEL

kernel_name = "hybrid_dsa_moba_macaron_step"

def rms_norm(x, g):
    xf = x.astype(jnp.float32)
    y = xf * lax.rsqrt(jnp.mean(xf * xf, axis=-1, keepdims=True) + EPS)
    return (y * g.astype(jnp.float32)).astype(x.dtype)

def rope(x, pos):
    half = x.shape[-1] // 2
    inv = ROPE_THETA ** (-jnp.arange(half, dtype=jnp.float32) / half)
    ang = pos.astype(jnp.float32)[:, None] * inv[None, :]
    cos = jnp.cos(ang)[:, None, :]
    sin = jnp.sin(ang)[:, None, :]
    xf = x.astype(jnp.float32)
    x1, x2 = xf[..., :half], xf[..., half:]
    return jnp.concatenate([x1 * cos - x2 * sin, x2 * cos + x1 * sin], axis=-1).astype(x.dtype)

def swiglu(x, w_in, w_out):
    hu = x @ w_in
    g, u = hu[..., :D_FF], hu[..., D_FF:]
    return (jax.nn.silu(g) * u) @ w_out

def split_cols(z):
    sizes = (W_QA, W_KA, W_VA, W_QI, W_KI, W_WI, W_QB, W_KB, W_VB, D_MODEL, D_MODEL)
    outs, start = [], 0
    for s in sizes:
        outs.append(z[..., start:start + s])
        start += s
    return outs

def project(h, pos, w_in, q_norm_a, k_norm_a, q_norm_b, k_norm_b, gate_bias):
    b, t, _ = h.shape
    qa, ka, va, qi, ki, wi, qb, kb, vb, ga, gb = split_cols(h @ w_in)
    return {
        "qa": rope(rms_norm(qa.reshape(b, t, H_A, HEAD_DIM), q_norm_a), pos),
        "ka": rope(rms_norm(ka.reshape(b, t, HKV_A, HEAD_DIM), k_norm_a), pos),
        "va": va.reshape(b, t, HKV_A, HEAD_DIM),
        "qi": rope(qi.reshape(b, t, H_IDX, D_IDX), pos),
        "ki": rope(ki.reshape(b, t, 1, D_IDX), pos).reshape(b, t, D_IDX),
        "wi": wi * (H_IDX ** -0.5),
        "qb": rope(rms_norm(qb.reshape(b, t, H_B, HEAD_DIM), q_norm_b), pos),
        "kb": rope(rms_norm(kb.reshape(b, t, HKV_B, HEAD_DIM), k_norm_b), pos),
        "vb": vb.reshape(b, t, HKV_B, HEAD_DIM),
        "ga": ga + gate_bias[:D_MODEL],
        "gb": gb + gate_bias[D_MODEL:],
    }

def dsa_attend(qa, qi, wi, pos, ka, va, ki, k_sel):
    n_q = qa.shape[0]
    n_keys = ka.shape[0]
    s = jnp.einsum('qhd,sd->qhs', qi.astype(jnp.float32), ki.astype(jnp.float32)) * (D_IDX ** -0.5)
    score = jnp.einsum('qh,qhs->qs', wi.astype(jnp.float32), jax.nn.relu(s))
    key_pos = jnp.arange(n_keys)
    score = jnp.where(key_pos[None, :] <= pos[:, None], score, -jnp.inf)
    _, sel = lax.top_k(score, k_sel)
    valid = sel <= pos[:, None]
    ks = ka[sel]
    vs = va[sel]
    qg = qa.reshape(n_q, HKV_A, G_A, HEAD_DIM)
    logits = jnp.einsum('qngd,qknd->qngk', qg, ks).astype(jnp.float32) * (HEAD_DIM ** -0.5)
    logits = jnp.where(valid[:, None, None, :], logits, -jnp.inf)
    p = jax.nn.softmax(logits, axis=-1).astype(vs.dtype)
    return jnp.einsum('qngk,qknd->qngd', p, vs).reshape(n_q, H_A * HEAD_DIM)

def moba_attend(qb, pos, kb_blocks, vb_blocks, kb_mean):
    n_q = qb.shape[0]
    n_blk = kb_blocks.shape[0]
    qg = qb.reshape(n_q, HKV_B, G_B, HEAD_DIM)
    own = pos // MOBA_BLOCK
    gate = jnp.einsum('qngd,jnd->qngj', qg.astype(jnp.float32), kb_mean)
    past = jnp.arange(n_blk)[None, :] < own[:, None]
    gate = jnp.where(past[:, None, None, :], gate, -jnp.inf)
    n_top = min(TOPK_B, n_blk)
    _, sel = lax.top_k(gate, n_top)
    sel_ok = sel < own[:, None, None, None]
    own_b = jnp.broadcast_to(own[:, None, None, None], sel.shape[:-1] + (1,))
    blocks = jnp.concatenate([sel, own_b.astype(sel.dtype)], axis=-1)
    blk_ok = jnp.concatenate([sel_ok, jnp.ones(own_b.shape, dtype=bool)], axis=-1)
    kvh = jnp.arange(HKV_B)[None, :, None, None]
    ks = kb_blocks.transpose(2, 0, 1, 3)[kvh, blocks]
    vs = vb_blocks.transpose(2, 0, 1, 3)[kvh, blocks]
    key_pos = blocks[..., None] * MOBA_BLOCK + jnp.arange(MOBA_BLOCK)
    mask = blk_ok[..., None] & (key_pos <= pos[:, None, None, None, None])
    logits = jnp.einsum('qngd,qngjkd->qngjk', qg, ks).astype(jnp.float32) * (HEAD_DIM ** -0.5)
    logits = jnp.where(mask, logits, -jnp.inf)
    shp = logits.shape
    p = jax.nn.softmax(logits.reshape(shp[:3] + (-1,)), axis=-1).reshape(shp).astype(vs.dtype)
    return jnp.einsum('qngjk,qngjkd->qngd', p, vs).reshape(n_q, H_B * HEAD_DIM)

def seq_attend(qa, qi, wi, qb, pos, ka, va, ki, kb, vb, k_sel):
    n_keys = ka.shape[0]
    n_blk = -(-n_keys // MOBA_BLOCK)
    pad = n_blk * MOBA_BLOCK - n_keys
    kb_blocks = jnp.pad(kb, ((0, pad), (0, 0), (0, 0))).reshape(n_blk, MOBA_BLOCK, HKV_B, HEAD_DIM)
    vb_blocks = jnp.pad(vb, ((0, pad), (0, 0), (0, 0))).reshape(n_blk, MOBA_BLOCK, HKV_B, HEAD_DIM)
    kb_mean = jnp.mean(kb_blocks.astype(jnp.float32), axis=1)
    n_q = qa.shape[0]
    qblk = Q_BLOCK if n_q % Q_BLOCK == 0 else n_q
    nqb = n_q // qblk

    def blk(a):
        return a.reshape((nqb, qblk) + a.shape[1:])

    def step(args):
        qa_, qi_, wi_, qb_, pos_ = args
        return (dsa_attend(qa_, qi_, wi_, pos_, ka, va, ki, k_sel),
                moba_attend(qb_, pos_, kb_blocks, vb_blocks, kb_mean))

    oa, ob = lax.map(step, (blk(qa), blk(qi), blk(wi), blk(qb), blk(pos)))
    return oa.reshape(n_q, H_A * HEAD_DIM), ob.reshape(n_q, H_B * HEAD_DIM)

def mix_group(t, ka, va, ki, kb, vb, pos, k_sel):
    def per_seq(args):
        qa, qi, wi, qb, ka_, va_, ki_, kb_, vb_ = args
        return seq_attend(qa, qi, wi, qb, pos, ka_, va_, ki_, kb_, vb_, k_sel)
    return lax.map(per_seq, (t["qa"], t["qi"], t["wi"], t["qb"], ka, va, ki, kb, vb))

def merge(t, oa, ob, w_up_a, w_up_b, w_out):
    m = jax.nn.sigmoid(t["ga"]) * (oa @ w_up_a) + jax.nn.sigmoid(t["gb"]) * (ob @ w_up_b)
    return m @ w_out

def gather_pages(pool, page_table):
    g = pool[page_table]
    return g.reshape((page_table.shape[0], -1) + pool.shape[2:])

def setup_inputs(seed: int = 0) -> dict:
    key = jax.random.key(seed)
    ks = jax.random.split(key, 32)
    n_pages = PAST_LEN // PAGE_SIZE
    n_used = DEC_BATCH * n_pages
    n_pool = n_used + n_used // 4

    def nrm(k, shape, scale=1.0):
        return jax.random.normal(k, shape, jnp.float32) * scale

    def gain(k, shape):
        return 1.0 + 0.01 * jax.random.normal(k, shape, jnp.float32)

    page_table = jax.random.permutation(ks[7], n_pool)[:n_used].reshape(DEC_BATCH, n_pages).astype(jnp.int32)
    return {
        "x_prompt": nrm(ks[0], (BATCH, SEQ, D_MODEL)),
        "x_sample": nrm(ks[1], (DEC_BATCH, DEC_SEQ, D_MODEL)),
        "cache_k_a": nrm(ks[2], (DEPTH, n_pool, PAGE_SIZE, HKV_A, HEAD_DIM)),
        "cache_v_a": nrm(ks[3], (DEPTH, n_pool, PAGE_SIZE, HKV_A, HEAD_DIM)),
        "cache_kidx_a": nrm(ks[4], (DEPTH, n_pool, PAGE_SIZE, D_IDX)),
        "cache_k_b": nrm(ks[5], (DEPTH, n_pool, PAGE_SIZE, HKV_B, HEAD_DIM)),
        "cache_v_b": nrm(ks[6], (DEPTH, n_pool, PAGE_SIZE, HKV_B, HEAD_DIM)),
        "page_table": page_table,
        "ffn1_norm": gain(ks[8], (DEPTH, D_MODEL)),
        "ffn1_w_in": nrm(ks[9], (DEPTH, D_MODEL, 2 * D_FF), D_MODEL ** -0.5),
        "ffn1_w_out": nrm(ks[10], (DEPTH, D_FF, D_MODEL), D_FF ** -0.5),
        "mix_norm": gain(ks[11], (DEPTH, D_MODEL)),
        "w_in": nrm(ks[12], (DEPTH, D_MODEL, N_IN), D_MODEL ** -0.5),
        "q_norm_a": gain(ks[13], (DEPTH, HEAD_DIM)),
        "k_norm_a": gain(ks[14], (DEPTH, HEAD_DIM)),
        "q_norm_b": gain(ks[15], (DEPTH, HEAD_DIM)),
        "k_norm_b": gain(ks[16], (DEPTH, HEAD_DIM)),
        "gate_bias": nrm(ks[17], (DEPTH, 2 * D_MODEL), 0.01),
        "w_up_a": nrm(ks[18], (DEPTH, H_A * HEAD_DIM, D_MODEL), (H_A * HEAD_DIM) ** -0.5),
        "w_up_b": nrm(ks[19], (DEPTH, H_B * HEAD_DIM, D_MODEL), (H_B * HEAD_DIM) ** -0.5),
        "w_out": nrm(ks[20], (DEPTH, D_MODEL, D_MODEL), D_MODEL ** -0.5),
        "ffn2_norm": gain(ks[21], (DEPTH, D_MODEL)),
        "ffn2_w_in": nrm(ks[22], (DEPTH, D_MODEL, 2 * D_FF), D_MODEL ** -0.5),
        "ffn2_w_out": nrm(ks[23], (DEPTH, D_FF, D_MODEL), D_FF ** -0.5),
    }

def reference(x_prompt, x_sample, cache_k_a, cache_v_a, cache_kidx_a, cache_k_b, cache_v_b, page_table,
              ffn1_norm, ffn1_w_in, ffn1_w_out, mix_norm, w_in, q_norm_a, k_norm_a, q_norm_b, k_norm_b,
              gate_bias, w_up_a, w_up_b, w_out, ffn2_norm, ffn2_w_in, ffn2_w_out):
    seq = x_prompt.shape[1]
    n_new = x_sample.shape[1]
    past_len = page_table.shape[1] * cache_k_a.shape[2]
    pos_p = jnp.arange(seq, dtype=jnp.int32)
    pos_s = past_len + jnp.arange(n_new, dtype=jnp.int32)
    k_sel_p = min(TOPK_A_MAX, seq // 4)
    k_sel_s = min(TOPK_A_MAX, (past_len + n_new) // 4)

    names = ("ka", "va", "ki", "kb", "vb")
    rows_p = {n: [] for n in names}
    rows_s = {n: [] for n in names}
    xp, xs = x_prompt, x_sample
    for l in range(DEPTH):
        xp = xp + 0.5 * swiglu(rms_norm(xp, ffn1_norm[l]), ffn1_w_in[l], ffn1_w_out[l])
        xs = xs + 0.5 * swiglu(rms_norm(xs, ffn1_norm[l]), ffn1_w_in[l], ffn1_w_out[l])

        tp = project(rms_norm(xp, mix_norm[l]), pos_p, w_in[l], q_norm_a[l], k_norm_a[l],
                     q_norm_b[l], k_norm_b[l], gate_bias[l])
        ts = project(rms_norm(xs, mix_norm[l]), pos_s, w_in[l], q_norm_a[l], k_norm_a[l],
                     q_norm_b[l], k_norm_b[l], gate_bias[l])

        oa, ob = mix_group(tp, tp["ka"], tp["va"], tp["ki"], tp["kb"], tp["vb"], pos_p, k_sel_p)
        xp = xp + merge(tp, oa, ob, w_up_a[l], w_up_b[l], w_out[l])

        def with_past(pool, new):
            return jnp.concatenate([gather_pages(pool[l], page_table).astype(new.dtype), new], axis=1)

        oa, ob = mix_group(ts, with_past(cache_k_a, ts["ka"]), with_past(cache_v_a, ts["va"]),
                           with_past(cache_kidx_a, ts["ki"]), with_past(cache_k_b, ts["kb"]),
                           with_past(cache_v_b, ts["vb"]), pos_s, k_sel_s)
        xs = xs + merge(ts, oa, ob, w_up_a[l], w_up_b[l], w_out[l])

        xp = xp + 0.5 * swiglu(rms_norm(xp, ffn2_norm[l]), ffn2_w_in[l], ffn2_w_out[l])
        xs = xs + 0.5 * swiglu(rms_norm(xs, ffn2_norm[l]), ffn2_w_in[l], ffn2_w_out[l])

        for n in names:
            rows_p[n].append(tp[n])
            rows_s[n].append(ts[n])

    return (xp, xs,
            jnp.stack(rows_p["ka"]), jnp.stack(rows_p["va"]), jnp.stack(rows_p["ki"]),
            jnp.stack(rows_p["kb"]), jnp.stack(rows_p["vb"]),
            jnp.stack(rows_s["ka"]), jnp.stack(rows_s["va"]), jnp.stack(rows_s["ki"]),
            jnp.stack(rows_s["kb"]), jnp.stack(rows_s["vb"]))


_drawn_inputs = setup_inputs


def setup_inputs(seed=0):
    import zlib

    import numpy as np

    out = dict(_drawn_inputs(seed))
    spreads = {}
    factors = {'ffn1_norm': 7.722,
     'mix_norm': 4.898,
     'q_norm_a': 52.953,
     'k_norm_a': 32.371,
     'q_norm_b': 56.998,
     'k_norm_b': 22.032,
     'gate_bias': 64.0,
     'ffn2_norm': 42.088}
    for name, (base, spread) in spreads.items():
        noise = np.random.default_rng([zlib.crc32(name.encode()), seed]).standard_normal(out[name].shape)
        drawn = base * np.exp(spread * noise) if base else spread * noise
        out[name] = __import__('jax').numpy.asarray(drawn.astype(out[name].dtype))
    for name, factor in factors.items():
        out[name] = (out[name] * factor).astype(out[name].dtype)
    return out
```

```python
from contextlib import ExitStack

import numpy as np

import concourse.bass as bass
from concourse import mybir

F32 = mybir.dt.float32
F32R = mybir.dt.float32r
BF16 = mybir.dt.bfloat16
I32 = mybir.dt.int32
ALU = mybir.AluOpType
ACT = mybir.ActivationFunctionType
AX = mybir.AxisListType.X

P = 128
EPS = 1e-6
ROPE_THETA = 10000.0
NEG = -float(2.0 ** 100)
TAKEN = -3.0e38
TAKEN_LIMIT = -2.0e38

NP_TOK, N_SEQ, N_NEW = 256, 8, 4
NS_TOK = N_SEQ * N_NEW
N = NP_TOK + NS_TOK
PAST = 256
PAGE = 128
NPG = PAST // PAGE
HD = 64
HEADS = 8
TOPK_PROMPT = NP_TOK // 4
TOPK_SAMPLE = (PAST + N_NEW) // 4
NK_S = PAST + NS_TOK
D = 1024
KB = D // P
DFF = 2752
FB = -(-DFF // P)
FTAIL = DFF - (FB - 1) * P
TC = 256
NR, NU = 3, 4
AHEAD = NU

C_COS, C_SIN = 0, N
C_SWAP = 2 * N
C_ID, C_BLK, C_ONE = C_SWAP + P, C_SWAP + 2 * P, C_SWAP + 3 * P
C_CAUSAL = C_ONE + P
C_MASKS = C_CAUSAL + 2 * P
C_EXP = C_MASKS + NK_S
C_EXPT = C_EXP + 2 * P
C_HSEL = C_EXPT + 2 * NS_TOK
C_ALL = C_HSEL + HEADS


def shape_constants():
    c = np.zeros((P, C_ALL), np.float32)
    half = HD // 2
    inv = (np.float32(ROPE_THETA) ** (-np.arange(half, dtype=np.float32) / np.float32(half))).astype(np.float32)
    pos = np.concatenate([np.arange(NP_TOK), np.tile(PAST + np.arange(N_NEW), N_SEQ)]).astype(np.float32)
    ang = (pos[None, :] * inv[:, None]).astype(np.float32)
    c[:, C_COS:C_COS + N] = np.tile(np.cos(ang), (4, 1))
    c[:, C_SIN:C_SIN + N] = np.tile(np.concatenate([-np.sin(ang), np.sin(ang)]), (2, 1))
    p = np.arange(P)
    c[p ^ half, C_SWAP + p] = 1.0
    c[p, C_ID + p] = 1.0
    c[:, C_BLK:C_BLK + P] = (p[:, None] // HD == p[None, :] // HD) / HD
    c[:, C_ONE:C_ONE + P] = 1.0 / D
    keys = np.arange(2 * P)
    c[:, C_CAUSAL:C_CAUSAL + 2 * P] = np.where(keys[None, :] <= P + p[:, None], 0.0, NEG)
    b, t = np.arange(NS_TOK) // N_NEW, np.arange(NS_TOK) % N_NEW
    c[:NS_TOK, C_MASKS + PAST:C_MASKS + NK_S] = np.where(
        (b[:, None] == b[None, :]) & (t[None, :] <= t[:, None]), 0.0, NEG)
    rb, rh, rt = p // 32, p % 32 // N_NEW, p % N_NEW
    for g in range(2):
        e = (b[:, None] == 4 * g + rb[None, :]) & (t[:, None] == rt[None, :])
        c[:NS_TOK, C_EXP + g * P:C_EXP + (g + 1) * P] = e
        c[:, C_EXPT + g * NS_TOK:C_EXPT + (g + 1) * NS_TOK] = e.T
    c[:, C_HSEL:C_HSEL + HEADS] = rh[:, None] == np.arange(HEADS)[None, :]
    return c


def weight_plan():
    tiles, units, first = [], [], {}

    def ffn(f):
        first[f"G{f}"] = len(tiles), len(units)
        w = f"ffn{f}_w_in"
        for t in range(FB // 2):
            width = min(TC, DFF - TC * t)
            n = len(tiles)
            for c0 in (0, DFF):
                tiles.append([(0, P, 0, KB, 0, width, w, 0, c0 + TC * t)])
            for m in range(2):
                for g in range(2):
                    units.append((n + g, m * P, min(P, width - m * P), KB))
        first[f"D{f}"] = len(tiles), len(units)
        w = f"ffn{f}_w_out"
        for c in range(D // TC):
            for k0 in range(0, FB, KB):
                kb = min(KB, FB - k0)
                n = len(tiles)
                full = kb - (k0 + kb == FB)
                tiles.append([(0, P, 0, full, 0, TC, w, k0 * P, c * TC)])
                if full < kb:
                    tiles[-1].append((0, FTAIL, full, 1, 0, TC, w, (FB - 1) * P, c * TC))
                units.extend((n, m * P, P, kb) for m in range(2))

    def one(*cols):
        tiles.append([(0, P, 0, KB, a, w, "w_in", 0, s) for a, w, s in cols])

    ffn(1)
    first["P"] = len(tiles), len(units)
    wqa, wk, wq = 0, HD, HEADS * HD
    ka, va = wq, wq + wk
    qi = va + wk
    ki = qi + wq
    wi = ki + wk
    qb = wi + HEADS
    kb_ = qb + wq
    vb = kb_ + 2 * HD
    ga = vb + 2 * HD
    one((0, TC, qi))
    one((0, TC, qi + TC))
    one((0, HD, ka), (HD, HD, ka), (2 * HD, HD, ki), (3 * HD, HD, ki))
    one((0, TC, kb_))
    qbh = [((s * HD), HD, qb + (m + 4 * s) * HD) for m in range(4) for s in range(2)]
    at = lambda m, a: [(a + qbh[2 * m + s][0], HD, qbh[2 * m + s][2]) for s in range(2)]
    one((0, HD, va), (HD, HEADS, wi), *at(0, P))
    one(*at(1, 0), *at(2, P))
    one(*at(3, 0), (P, P, wqa))
    one((0, TC, wqa + P))
    one((0, P, wqa + 3 * P), (P, P, ga))
    for g in range(7):
        one((0, TC, ga + P + g * TC))
    one((0, P, ga + 15 * P))
    base = first["P"][0]
    for u in range(33):
        units.append((base + u // 2, (u % 2) * P, HD + HEADS if u == 8 else P, KB))
    first["U"] = len(tiles), len(units)
    for c in range(D // TC):
        n = len(tiles)
        tiles.append([(0, P, 0, 4, 0, TC, "w_up_a", 0, c * TC)]
                     + [(s * HD, HD, 4, 4, 0, TC, "w_up_b", s * 4 * HD, c * TC) for s in range(2)])
        units.extend((n, m * P, P, KB) for m in range(2))
    first["O"] = len(tiles), len(units)
    for c in range(D // TC):
        n = len(tiles)
        tiles.append([(0, P, 0, KB, 0, TC, "w_out", 0, c * TC)])
        units.extend((n, m * P, P, KB) for m in range(2))
    ffn(2)
    return tiles, units, first


U_QI, U_KA, U_KI, U_KB, U_VB, U_VW, U_QB, U_QA, U_GATE, U_END = 0, 4, 5, 6, 7, 8, 9, 13, 17, 33
NORMED = [U_KA, U_KB] + list(range(U_QB, U_QA + 4))
ROTATED = [u for u in range(U_GATE) if u not in (U_VB, U_VW)]
GAIN_OF = {U_KA: 41, U_KB: 43} | {u: 42 for u in range(U_QB, U_QB + 4)} | {u: 40 for u in range(U_QA, U_QA + 4)}
GAIN_ROWS = 44

IDX, MOBA, DSA = 0, 1, 2
N_STEPS = 24
FIRST_STEP_SLOT = 12
STEP_OF_SLOT = {u: u - FIRST_STEP_SLOT for u in range(FIRST_STEP_SLOT, U_END)}
TOK_SLOT, WCOL_SLOT = 10, 11
CHORE_STEP, CHORES_PER_STEP = 5, 2


def step_kind(m):
    kind, a = divmod(m, 8)
    return (kind, 1, a) if a < 4 else (kind, 0, a - 4) if a < 6 else (kind, 2, a - 6)


def step_heads(form, i):
    return (i // 2, [2 * (i % 2), 2 * (i % 2) + 1], 2 * P) if form == 1 else (i, [0, 1, 2, 3], P)


def out_group(m):
    kind, form, i = step_kind(m)
    g = (kind - 1) * 3 + {1: 0, 0: 1, 2: 2}[form]
    return g, i == {1: 3, 0: 1, 2: 1}[form]


def build(nc, a, o):
    tiles, units, first = weight_plan()
    landed, total = [], [0] * NR
    for n, t in enumerate(tiles):
        total[n % NR] += 16 * len(t)
        landed.append(total[n % NR])
    tile_split = [0] * len(tiles)
    for v, u in enumerate(units):
        tile_split[u[0]] = v + 1

    ctx = ExitStack()
    with ctx:
        sems = {}

        def sem(name):
            sems[name] = ctx.enter_context(nc.semaphore(name))
            return sems[name]

        here = [-(-nc.sbuf_base // 128) * 128]

        def sb(name, shape, dt=F32, at=None):
            size = int(np.prod(shape[1:])) * (2 if dt == BF16 else 4)
            where = here[0] if at is None else at
            t = nc.alloc_sbuf_tensor_at(name, shape, dt, offset=where)
            if at is None:
                here[0] += -(-size // 32) * 32
            return t, where

        def new(name, shape, dt=F32):
            return sb(name, shape, dt)[0]

        raw = new("raw", [P, NR, KB, TC])
        whi = new("whi", [P, NU, KB, P], F32R)
        wlo = new("wlo", [P, NU, KB, P], F32R)
        x = new("x", [P, KB, N])
        nhi = new("nhi", [P, KB, N], F32R)
        nlo = new("nlo", [P, KB, N], F32R)
        hhi, at_h = sb("hhi", [P, FB, N], F32R)
        hlo = new("hlo", [P, FB, N], F32R)
        blk = lambda i: at_h + i * N * 4
        xtok, _ = sb("xtok", [P, 3, D], at=at_h)
        qi, _ = sb("qi", [P, 4, N], at=blk(0))
        qb, _ = sb("qb", [P, 4, N], at=blk(4))
        qa, _ = sb("qa", [P, 4, N], at=blk(8))
        bhi, _ = sb("bhi", [P, 4, N], F32R, at=blk(0))
        blo, _ = sb("blo", [P, 4, N], F32R, at=blk(12))
        ahi, _ = sb("ahi", [P, 4, N], F32R, at=blk(4))
        alo, _ = sb("alo", [P, 4, N], F32R, at=blk(16))
        gates, _ = sb("gates", [P, 16, N], at=blk(20))
        kv, _ = sb("kv", [P, 5, N], at=blk(36))
        kt, at_kt = sb("kt", [P, 3, N_SEQ, PAST])
        ytok, _ = sb("ytok", [P, 3, D], at=at_kt)
        va_pg = new("va_pg", [P, N_SEQ * NPG, HD])
        vb_pg = new("vb_pg", [P, N_SEQ * NPG, P])
        cst = new("cst", [P, C_ALL])
        idb = new("idb", [P, P], BF16)
        causalb = new("causalb", [P, 2 * P], BF16)
        masksb = new("masksb", [NS_TOK, NK_S], BF16)
        expb = new("expb", [NS_TOK, 2 * P], BF16)
        rows = new("rows", [GAIN_ROWS, P])
        gains = new("gains", [P, GAIN_ROWS])
        ptab = new("ptab", [1, N_SEQ * NPG], I32)
        tmp = new("tmp", [P, 2, 1, N])
        act_tmp = new("act_tmp", [P, 2, 1, N])
        rms, sq_block, ssq = act_tmp[:, 0, 0, :], act_tmp[:, 0, 0, :], act_tmp[:, 1, 0, :]
        eps_col = new("eps_col", [P, 4])
        kraw, at_att = sb("kraw", [P, 3, N_SEQ * NPG, P])
        end_kraw = here[0]
        here[0] = at_att
        roots = new("roots", [P, 2, N])
        tok = new("tok", [P, 3, 456])
        probs = new("probs", [P, 2, 512])
        probsT = new("probsT", [P, 2, 512])
        qz = new("qz", [P, 3, 2 * P])
        acc1 = new("acc1", [P, 2 * P])
        acc0 = new("acc0", [P, P])
        acc_s = new("acc_s", [NS_TOK, NK_S])
        best = new("best", [P, 8])
        sel1 = new("sel1", [P, 2 * P], BF16)
        sel0 = new("sel0", [P, P], BF16)
        sel_s = new("sel_s", [NS_TOK, NK_S], BF16)
        nmax = new("nmax", [P, 4 * N_STEPS])
        rsum = new("rsum", [P, 4 * N_STEPS])
        rinv = new("rinv", [P, 4 * N_STEPS])
        wi_p = new("wi_p", [P, 2, HEADS])
        wsel = new("wsel", [P, 2, HEADS])
        wcol = new("wcol", [P, 2])
        wexp = new("wexp", [P, 2, NS_TOK])
        va2 = new("va2", [NS_TOK, P])
        assert here[0] <= nc.sbuf_usable_end and end_kraw <= nc.sbuf_usable_end, (here, end_kraw, nc.sbuf_usable_end)
        ps = [ctx.enter_context(nc.psum_tensor(f"ps{i}", [P, 512], F32)) for i in range(8)]
        zloc = ([qi[:, i, :] for i in range(4)] + [kv[:, i, :] for i in range(5)]
                + [qb[:, i, :] for i in range(4)] + [qa[:, i, :] for i in range(4)])
        KT_OF = {IDX: 0, MOBA: 1, DSA: 2}
        Q_OF = {IDX: qi, MOBA: qb, DSA: qa}
        K_OF = {IDX: kv[:, 1, :], MOBA: kv[:, 2, :], DSA: kv[:, 0, :]}
        c_ = lambda at, n, rows_=P: cst[0:rows_, at:at + n]

        raw_in = [sem(f"raw_in{i}") for i in range(NR)]
        (const_in, x_in, rows_in, ptab_in, pages_in, out_done, gains_T, gains_ready, scaled_gains, masks_ready,
         xT_done, x_ready, squares_ready, ms_done, root_ready, rstd_ready, scaled, n_hi, n_lo,
         w_hi, w_lo, unit_done, silu_done, pair_free, h_hi, h_lo, down_evac, keysT_done, keysT_act, keysT_dve,
         z_ready, zsq_ready, zms_done, zroot_ready, zn_ready, swapped, z_final, tok_T, tok_ready, wexp_ps, wexp_ready,
         qz_ready, qz_zero, logits_done, max_done, soft_done, idx_acc, score_ps, score_ready, sel_ready, rinv_ready,
         probs_ready, probsT_done, probsT_ready, pv_done, out_hi, out_lo, va2_ready, sig_ready, m_scaled, m_hi, m_lo,
         o_evac, yT_done, y_ready, dve_chain, act_chain, pool_chain, wi_ready) = [sem(s) for s in (
             "const_in x_in rows_in ptab_in pages_in out_done gains_T gains_ready scaled_gains masks_ready "
             "xT_done x_ready squares_ready ms_done root_ready rstd_ready scaled n_hi n_lo "
             "w_hi w_lo unit_done silu_done pair_free h_hi h_lo down_evac keysT_done keysT_act keysT_dve "
             "z_ready zsq_ready zms_done zroot_ready zn_ready swapped z_final tok_T tok_ready wexp_ps wexp_ready "
             "qz_ready qz_zero logits_done max_done soft_done idx_acc score_ps score_ready sel_ready rinv_ready "
             "probs_ready probsT_done probsT_ready pv_done out_hi out_lo va2_ready sig_ready m_scaled m_hi m_lo "
             "o_evac yT_done y_ready dve_chain act_chain pool_chain wi_ready").split()]

        LOOP_TILES, LOOP_UNITS, LOOP_PAIRS = 6, 12, 6
        G_LOOPS = FB // 2 // 3
        D_LOOPS = D // TC // 2
        BANKS_FREE = 3
        DOWN_FREE = 3

        def landed_per_turn(n):
            return landed[n + LOOP_TILES] - landed[n]

        def index_among(u, those):
            return those.index(u)

        def sample_columns(ap, kind, s):
            order = "p (b s m t) -> p s m b t" if kind == MOBA else "p (b m s t) -> p s m b t"
            return ap.rearrange(order, b=N_SEQ, m=4, s=2, t=N_NEW)[:, s]

        def out_views(t, bank, kind, form):
            if form < 2:
                return [(t[:, :, form * P:(form + 1) * P], bank[:, :].rearrange("p (m q) -> p m q", m=4))]
            halves = [slice(s * HD, (s + 1) * HD) for s in range(2)]
            return [(t[h, :, NP_TOK:N].rearrange("p m (b t) -> p m b t", t=N_NEW),
                     sample_columns(bank[h, 0:2 * P], kind, s)) for s, h in enumerate(halves)]

        block = ctx.enter_context(nc.Block())

        @block.sync
        def _(sp):
            def load(n, it=None, turns=1):
                if n >= NR:
                    free = max(tile_split[n - NR + LOOP_TILES * i] - LOOP_UNITS * i for i in range(turns))
                    free = free if it is None else free + LOOP_UNITS * it
                    sp.wait_ge(w_hi, free)
                    sp.wait_ge(w_lo, free)
                for p0, np_, k0, nk, c0, w, name, r0, s0 in tiles[n]:
                    src = a[name][r0:r0 + nk * np_, :]
                    if it is None:
                        src = src[:, s0:s0 + w]
                    else:
                        step = tiles[n + LOOP_TILES][0][8] - tiles[n][0][8]
                        src = src[:, bass.ds(it * step + s0, w)]
                    sp.dma_start(raw[p0:p0 + np_, n % NR, k0:k0 + nk, c0:c0 + w],
                                 src.rearrange("(k p) c -> p k c", p=np_)).then_inc(raw_in[n % NR], 16)

            for f in (1, 2):
                g0, d0 = first[f"G{f}"][0], first[f"D{f}"][0]
                for n in range(LOOP_TILES):
                    load(g0 + n)
                with sp.Fori(0, G_LOOPS - 1) as it:
                    for n in range(LOOP_TILES):
                        load(g0 + LOOP_TILES + n, it, G_LOOPS - 1)
                for n in range(G_LOOPS * LOOP_TILES, 2 * (FB // 2)):
                    load(g0 + n)
                with sp.Fori(0, D_LOOPS) as it:
                    for n in range(LOOP_TILES):
                        load(d0 + n, it, D_LOOPS)
                if f == 1:
                    for n in range(first["P"][0], first["G2"][0]):
                        load(n)
            sp.wait_ge(y_ready, KB)
            sp.dma_start(o["y_prompt"].rearrange("b (t p) d -> p (b t) d", p=P), ytok[:, 0:2, :]).then_inc(out_done, 16)
            sp.dma_start(o["y_sample"].rearrange("b t d -> (b t) d"), ytok[0:NS_TOK, 2, :]).then_inc(out_done, 16)
            sp.wait_ge(out_done, 16 * 12)

        @block.gpsimd
        def _(pool):
            nc.gpsimd.dma_start(ptab[:], a["page_table"].rearrange("a b -> (a b)")[None, :]).then_inc(ptab_in, 16)
            pool.wait_ge(ptab_in, 16)
            n_pool = a["cache_k_a"].shape[1]
            flat = {n: a[n].rearrange("l n p h d -> (l n) p (h d)") for n in
                    ("cache_k_a", "cache_v_a", "cache_k_b", "cache_v_b")}
            flat["cache_kidx_a"] = a["cache_kidx_a"].rearrange("l n p d -> (l n) p d")
            with pool.Fori(0, N_SEQ * NPG) as i:
                page = pool.value_load(ptab[0:1, bass.ds(i, 1)], min_val=0, max_val=n_pool - 1)
                for name, dst in (("cache_kidx_a", kraw[:, 0, bass.ds(i, 1), 0:HD]),
                                  ("cache_kidx_a", kraw[:, 0, bass.ds(i, 1), HD:P]),
                                  ("cache_k_b", kraw[:, 1, bass.ds(i, 1), :]),
                                  ("cache_k_a", kraw[:, 2, bass.ds(i, 1), 0:HD]),
                                  ("cache_k_a", kraw[:, 2, bass.ds(i, 1), HD:P]),
                                  ("cache_v_a", va_pg[:, bass.ds(i, 1), :]),
                                  ("cache_v_b", vb_pg[:, bass.ds(i, 1), :])):
                    nc.gpsimd.dma_start(dst, flat[name][bass.ds(page, 1), :, :].rearrange("o p d -> p o d"))\
                        .then_inc(pages_in, 16)

            chained = [0]

            def link(ins):
                chained[0] += 1
                ins.then_inc(pool_chain, 1)
                pool.wait_ge(pool_chain, chained[0])

            def squares(r, ready, base):
                for k in range(KB):
                    pool.wait_ge(ready, base + k + 1)
                    link(nc.gpsimd.tensor_tensor(sq_block if k else ssq, x[:, k, :], x[:, k, :], ALU.mult))
                    if k:
                        ins = nc.gpsimd.tensor_tensor(ssq, ssq, sq_block, ALU.add)
                        if k < KB - 1:
                            link(ins)
                        else:
                            ins.then_inc(squares_ready, 1)

            squares(0, x_ready, 0)
            squares(1, down_evac, DOWN_FREE)
            pool.wait_ge(keysT_done, 12)
            nc.gpsimd.memset(qz[:], 0.0).then_inc(qz_zero, 1)
            pool.wait_ge(qz_zero, 1)
            for kind, last in ((IDX, U_QI + 3), (MOBA, U_QB + 3), (DSA, U_QA + 3)):
                pool.wait_ge(z_final, index_among(last, ROTATED) + 1)
                for s in range(2):
                    lo = slice(s * HD, (s + 1) * HD)
                    dst = sample_columns(qz[lo, kind, :], kind, s)
                    src = Q_OF[kind][lo, :, NP_TOK:N].rearrange("p m (b t) -> p m b t", t=N_NEW)
                    nc.gpsimd.tensor_copy(dst, src).then_inc(qz_ready, 1)
                    pool.wait_ge(qz_ready, 2 * kind + s + 1)
            pool.wait_ge(tok_ready, 3)
            for s in range(2):
                nc.gpsimd.tensor_copy(va2[:, s * HD:(s + 1) * HD], tok[0:NS_TOK, 2, 384:448]).then_inc(va2_ready, 1)
                pool.wait_ge(va2_ready, s + 1)
            for m in range(8, N_STEPS):
                kind, form, i = step_kind(m)
                nh, w = {1: (2, 2 * P), 0: (4, P), 2: (1, NK_S)}[form]
                pool.wait_ge(rinv_ready, m - 7)
                pool.wait_ge(soft_done, m + 1)
                pv = probs[:, m % 2, 0:nh * w].rearrange("p (h k) -> p h k", h=nh)
                r = rinv[:, 4 * m:4 * m + nh].unsqueeze(2).to_broadcast([P, nh, w])
                nc.gpsimd.tensor_tensor(pv, pv, r, ALU.mult).then_inc(probs_ready, 1)
            squares(2, o_evac, 0)

        @block.scalar
        def _(act):
            for name, at in (("ffn1_norm", 0), ("mix_norm", 8), ("ffn2_norm", 16)):
                act.dma_start(rows[at:at + 8, :], a[name].rearrange("l (k p) -> (l k) p", p=P)).then_inc(rows_in, 16)
            act.dma_start(rows[24:40, :], a["gate_bias"].rearrange("l (k p) -> (l k) p", p=P)).then_inc(rows_in, 16)
            for i, name in enumerate(("q_norm_a", "k_norm_a", "q_norm_b", "k_norm_b")):
                for s in range(2):
                    act.dma_start(rows[40 + i:41 + i, s * HD:(s + 1) * HD], a[name]).then_inc(rows_in, 16)
            act.dma_start(xtok[:, 0:2, :], a["x_prompt"].rearrange("b (t p) d -> p (b t) d", p=P)).then_inc(x_in, 16)
            act.dma_start(xtok[0:NS_TOK, 2, :], a["x_sample"].rearrange("b t d -> (b t) d")).then_inc(x_in, 16)
            act.dma_start(cst[:], a["constants"]).then_inc(const_in, 16)

            def split_hi(v, it=0):
                n, c0, w, nk = units[v]
                step = 0 if isinstance(it, int) else landed_per_turn(n)
                act.wait_ge(raw_in[n % NR], landed[n] + step * it)
                if v >= NU:
                    act.wait_ge(unit_done, v - NU + 1 + LOOP_UNITS * it)
                nc.scalar.activation(whi[:, v % NU, 0:nk, 0:w], raw[:, n % NR, 0:nk, c0:c0 + w], ACT.Copy)\
                    .then_inc(w_hi, 1)

            for v in range(AHEAD):
                split_hi(v)
            for k in range(KB):
                act.wait_ge(xT_done, k + 1)
                nc.scalar.activation(x[:, k, :], ps[k % 4][:, 0:N], ACT.Copy).then_inc(x_ready, 1)

            def root(r):
                act.wait_ge(ms_done, r + 1)
                nc.scalar.activation(rms, ps[0][:, 0:N], ACT.Sqrt, bias=eps_col[:, 0:1]).then_inc(root_ready, 1)

            def norm_hi(r):
                for k in range(KB):
                    act.wait_ge(scaled, KB * r + k + 1)
                    nc.scalar.activation(nhi[:, k, :], tmp[:, k % 2, 0, :], ACT.Copy).then_inc(n_hi, 1)

            act.wait_ge(masks_ready, 1)
            root(0)
            norm_hi(0)

            def pair(f, p, it=0):
                v = first[f"G{f}"][1] + 2 * p + 1
                gp = (f - 1) * FB + p
                w = units[v][2]
                act.wait_ge(unit_done, v + 1 + LOOP_UNITS * it)
                act.wait_ge(pair_free, gp + 2 + LOOP_PAIRS * it)
                nc.scalar.activation(act_tmp[0:w, p % 2, 0, :], ps[2 * (p % 3)][0:w, 0:N], ACT.Silu).then_inc(silu_done, 1)
                split_hi(v - 1 + AHEAD, it)
                split_hi(v + AHEAD, it)
                act.wait_ge(pair_free, gp + 1 + BANKS_FREE + LOOP_PAIRS * it)
                at = slice(p, p + 1) if isinstance(it, int) else bass.ds(LOOP_PAIRS * it + p, 1)
                nc.scalar.activation(hhi[0:w, at, :], tmp[0:w, p % 2, :, :], ACT.Copy).then_inc(h_hi, 1)

            def gate_up(f):
                with act.Fori(0, G_LOOPS) as it:
                    for p in range(LOOP_PAIRS):
                        pair(f, p, it)
                for p in range(G_LOOPS * LOOP_PAIRS, FB):
                    pair(f, p)

            def down_turn(f, it, ahead=True):
                v0 = first[f"D{f}"][1]
                for j in range(LOOP_UNITS):
                    if v0 + j + AHEAD < len(units) or not isinstance(it, int):
                        split_hi(v0 + j + AHEAD, it)

            gate_up(1)
            with act.Fori(0, D_LOOPS) as it:
                down_turn(1, it)
            for g in range(0, 12, 2):
                act.wait_ge(keysT_done, g + 1)
                dst = kt[:, g // 4, :, :].rearrange("p b k -> p (b k)")[:, (g % 4) * 512:(g % 4 + 1) * 512]
                nc.scalar.activation(dst, ps[1 + g % 3][:, :], ACT.Copy).then_inc(keysT_act, 1)
            root(1)
            norm_hi(1)

            vp = first["P"][1]

            def attend(m):
                if m < N_STEPS:
                    kind, form, i = step_kind(m)
                    nh, w = {1: (2, 2 * P), 0: (4, P), 2: (1, NK_S)}[form]
                    if m >= 2:
                        k2, f2, i2 = step_kind(m - 2)
                        if k2 != IDX:
                            act.wait_ge(probsT_done, m - 2 - 8 + 1)
                        elif f2 != 2:
                            act.wait_ge(idx_acc, m - 2 + 1)
                        else:
                            act.wait_ge(score_ps, i2 + 1)
                    act.wait_ge(logits_done, m + 1)
                    if kind == IDX:
                        nc.scalar.activation(probs[:, m % 2, 0:nh * w], ps[m % 2][:, 0:nh * w], ACT.Relu).then_inc(soft_done, 1)
                    else:
                        act.wait_ge(max_done, m - 7)
                        for h in range(nh):
                            ins = nc.scalar.activation(probs[:, m % 2, h * w:(h + 1) * w], ps[m % 2][:, h * w:(h + 1) * w],
                                                       ACT.Exp, bias=nmax[:, 4 * m + h:4 * m + h + 1],
                                                       accum_out=rsum[:, 4 * m + h:4 * m + h + 1])
                        ins.then_inc(soft_done, 1)
                if 8 <= m - 1 < N_STEPS:
                    n = m - 1 - 8
                    act.wait_ge(probsT_done, n + 1)
                    if n >= 2:
                        act.wait_ge(pv_done, n - 1)
                    if step_kind(m - 1)[1] == 2:
                        nc.scalar.activation(probsT[:, n % 2, 0:256], ps[2 + n % 2][:, 0:256], ACT.Copy)
                        nc.scalar.activation(probsT[0:NS_TOK, n % 2, 256:384], ps[2 + n % 2][0:NS_TOK, 256:384],
                                             ACT.Copy).then_inc(probsT_ready, 1)
                    else:
                        nc.scalar.activation(probsT[:, n % 2, :], ps[2 + n % 2][:, :], ACT.Copy).then_inc(probsT_ready, 1)
                if 8 <= m - 2 < N_STEPS and out_group(m - 2)[1]:
                    g = out_group(m - 2)[0]
                    kind, form, _ = step_kind(m - 2)
                    act.wait_ge(pv_done, m - 2 - 8 + 1)
                    dst_t = bhi if kind == MOBA else ahi
                    for dst, src in out_views(dst_t, ps[4 + g % 2], kind, form):
                        ins = nc.scalar.activation(dst, src, ACT.Copy)
                    ins.then_inc(out_hi, 1)

            for u in range(U_END):
                if u in STEP_OF_SLOT:
                    attend(STEP_OF_SLOT[u])
                act.wait_ge(unit_done, vp + u + 1)
                bank = ps[6 + u % 2]
                if u < U_GATE:
                    w = units[vp + u][2]
                    nc.scalar.activation(zloc[u][0:w], bank[0:w, 0:N], ACT.Copy).then_inc(z_ready, 1)
                else:
                    j = u - U_GATE
                    nc.scalar.activation(gates[:, j, :], bank[:, 0:N], ACT.Identity, bias=gains[:, 24 + j:25 + j]).then_inc(z_ready, 1)
                if u in NORMED:
                    i = index_among(u, NORMED)
                    if i >= 2:
                        act.wait_ge(zms_done, i - 1)
                    nc.scalar.activation(act_tmp[:, i % 2, 0, :], bank[:, 0:N], ACT.Square).then_inc(zsq_ready, 1)
                if u - 1 in NORMED:
                    i = index_among(u - 1, NORMED)
                    act.wait_ge(zms_done, i + 1)
                    if i >= 2:
                        act.wait_ge(zn_ready, i - 1)
                    nc.scalar.activation(roots[:, i % 2, :], ps[5][:, 0:N], ACT.Sqrt, bias=eps_col[:, 0:1]).then_inc(zroot_ready, 1)
                split_hi(vp + u + AHEAD)
                if u == TOK_SLOT:
                    for t in range(3):
                        r = P if t < 2 else NS_TOK
                        act.wait_ge(tok_T, t + 1)
                        nc.scalar.activation(tok[0:r, t, :], ps[(2, 3, 0)[t]][0:r, 0:456], ACT.Copy).then_inc(tok_ready, 1)
                    act.wait_ge(tok_ready, 3)
                    for name, c0, w in (("k_a", 0, 64), ("kidx", 64, 64), ("k_b", 128, 128), ("v_b", 256, 128), ("v_a", 384, 64)):
                        act.dma_start(o[f"new_{name}_p"], tok[:, 0:2, c0:c0 + w]).then_inc(out_done, 16)
                        act.dma_start(o[f"new_{name}_s"], tok[0:NS_TOK, 2, c0:c0 + w]).then_inc(out_done, 16)
            for m in range(U_END - FIRST_STEP_SLOT, N_STEPS + 2):
                attend(m)
            act.wait_ge(z_ready, U_END)
            for i in range(4):
                nc.scalar.activation(gates[:, 4 * i:4 * i + 4, :], gates[:, 4 * i:4 * i + 4, :], ACT.Sigmoid).then_inc(sig_ready, 1)
            vu = first["U"][1]
            for j in range(8):
                split_hi(vu + j + AHEAD)
                act.wait_ge(m_scaled, j + 1)
                nc.scalar.activation(nhi[:, j, :], tmp[:, j % 2, 0, :], ACT.Copy).then_inc(m_hi, 1)
            vo = first["O"][1]
            for j in range(8):
                split_hi(vo + j + AHEAD)
            root(2)
            norm_hi(2)
            gate_up(2)
            vd = first["D2"][1]
            for j in range(2 * LOOP_UNITS):
                if vd + j + AHEAD < len(units):
                    split_hi(vd + j + AHEAD)

        @block.vector
        def _(dve):
            chained = [0]

            def link(ins):
                chained[0] += 1
                ins.then_inc(dve_chain, 1)
                dve.wait_ge(dve_chain, chained[0])

            def split_lo(v, it=0):
                n, c0, w, nk = units[v]
                dve.wait_ge(w_hi, v + 1 + LOOP_UNITS * it)
                nc.vector.tensor_tensor(wlo[:, v % NU, 0:nk, 0:w], raw[:, n % NR, 0:nk, c0:c0 + w],
                                        whi[:, v % NU, 0:nk, 0:w].bitcast(F32), ALU.subtract).then_inc(w_lo, 1)

            nc.vector.memset(eps_col[:, 0:1], EPS).then_inc(masks_ready, 1)
            nc.vector.memset(eps_col[:, 1:2], 0.0).then_inc(pair_free, BANKS_FREE)
            nc.vector.memset(eps_col[:, 2:3], 0.0).then_inc(down_evac, DOWN_FREE)
            dve.wait_ge(gains_T, 1)
            nc.vector.tensor_copy(gains[:], ps[4][:, 0:GAIN_ROWS]).then_inc(gains_ready, 1)
            dve.wait_ge(gains_ready, 1)
            for c in (40, 42):
                nc.vector.tensor_scalar(gains[:, c:c + 1], gains[:, c:c + 1], HD ** -0.5, None, ALU.mult).then_inc(scaled_gains, 1)
            dve.wait_ge(const_in, 16)
            nc.vector.tensor_copy(idb[:], c_(C_ID, P)).then_inc(masks_ready, 1)
            nc.vector.tensor_copy(causalb[:], c_(C_CAUSAL, 2 * P)).then_inc(masks_ready, 1)
            nc.vector.tensor_copy(masksb[:], c_(C_MASKS, NK_S, NS_TOK)).then_inc(masks_ready, 1)
            nc.vector.tensor_copy(expb[:], c_(C_EXP, 2 * P, NS_TOK)).then_inc(masks_ready, 1)
            for v in range(AHEAD):
                split_lo(v)

            def norm(r, g0):
                dve.wait_ge(root_ready, r + 1)
                link(nc.vector.reciprocal(rms, rms))

                def lo(k):
                    dve.wait_ge(n_hi, KB * r + k + 1)
                    nc.vector.tensor_tensor(nlo[:, k, :], tmp[:, k % 2, 0, :], nhi[:, k, :].bitcast(F32),
                                            ALU.subtract).then_inc(n_lo, 1)

                for k in range(KB):
                    if k >= 2:
                        dve.wait_ge(n_lo, KB * r + k - 1)
                    nc.vector.scalar_tensor_tensor(tmp[:, k % 2, 0, :], x[:, k, :], gains[:, g0 + k:g0 + k + 1],
                                                   rms, ALU.mult, ALU.mult).then_inc(scaled, 1)
                    if k:
                        lo(k - 1)
                lo(KB - 1)

            norm(0, 0)

            def pair(f, p, it=0):
                v = first[f"G{f}"][1] + 2 * p + 1
                gp = (f - 1) * FB + p
                w = units[v][2]
                dve.wait_ge(silu_done, gp + 1 + LOOP_PAIRS * it)
                nc.vector.tensor_tensor(tmp[0:w, p % 2, 0, :], act_tmp[0:w, p % 2, 0, :], ps[2 * (p % 3) + 1][0:w, 0:N],
                                        ALU.mult).then_inc(pair_free, 1)
                split_lo(v - 1 + AHEAD, it)
                split_lo(v + AHEAD, it)
                dve.wait_ge(h_hi, gp + 1 + LOOP_PAIRS * it)
                at = slice(p, p + 1) if isinstance(it, int) else bass.ds(LOOP_PAIRS * it + p, 1)
                nc.vector.tensor_tensor(hlo[0:w, at, :], tmp[0:w, p % 2, :, :], hhi[0:w, at, :].bitcast(F32),
                                        ALU.subtract).then_inc(h_lo, 1)

            def gate_up(f):
                with dve.Fori(0, G_LOOPS) as it:
                    for p in range(LOOP_PAIRS):
                        pair(f, p, it)
                for p in range(G_LOOPS * LOOP_PAIRS, FB):
                    pair(f, p)

            def down_turn(f, it, q0=0):
                v0 = first[f"D{f}"][1] + 6 * q0
                for j in range(LOOP_UNITS):
                    q, i = divmod(j, 6)
                    if i >= 4:
                        m = i - 4
                        dve.wait_ge(unit_done, v0 + j + 1 + LOOP_UNITS * it)
                        k = 2 * (q0 + q) + m
                        xk = x[:, k:k + 1, :] if isinstance(it, int) else x[:, bass.ds(4 * it + k, 1), :]
                        bank = ps[(6, 4)[q % 2] + m]
                        nc.vector.scalar_tensor_tensor(xk, bank[:, 0:N].unsqueeze(1), 0.5, xk, ALU.mult, ALU.add)\
                            .then_inc(down_evac, 1)
                    if v0 + j + AHEAD < len(units):
                        split_lo(v0 + j + AHEAD, it)

            gate_up(1)
            with dve.Fori(0, D_LOOPS) as it:
                down_turn(1, it)
            for g in range(1, 12, 2):
                dve.wait_ge(keysT_done, g + 1)
                dst = kt[:, g // 4, :, :].rearrange("p b k -> p (b k)")[:, (g % 4) * 512:(g % 4 + 1) * 512]
                nc.vector.tensor_copy(dst, ps[1 + g % 3][:, :]).then_inc(keysT_dve, 1)
            norm(1, 8)

            vp = first["P"][1]

            def top_k(work, rounds, final, mask, kind_final):
                r = work.shape[0]

                def one_round(n):
                    link(nc.vector.max(best[0:r, :], work[:]))
                    if n == rounds - 1 and kind_final:
                        link(nc.vector.memset(best[0:r, kind_final:8], TAKEN))
                    link(nc.vector.match_replace(work[:], best[0:r, :], work[:], TAKEN))

                def finish():
                    link(nc.vector.tensor_scalar(work[:], work[:], TAKEN_LIMIT, NEG, ALU.is_gt, ALU.mult))
                    nc.vector.tensor_tensor(final[:], work[:], mask, ALU.add).then_inc(sel_ready, 1)

                return [lambda n=n: one_round(n) for n in range(rounds)] + [finish]

            chores = (top_k(acc1, TOPK_PROMPT // 8, sel1, c_(C_CAUSAL, 2 * P), 0)
                      + top_k(acc0, TOPK_PROMPT // 8, sel0, c_(C_CAUSAL + P, P), 0)
                      + top_k(acc_s, -(-TOPK_SAMPLE // 8), sel_s, c_(C_MASKS, NK_S, NS_TOK), TOPK_SAMPLE % 8))

            def attend(m):
                if 8 <= m < N_STEPS:
                    kind, form, i = step_kind(m)
                    nh, w = {1: (2, 2 * P), 0: (4, P), 2: (1, NK_S)}[form]
                    dve.wait_ge(logits_done, m + 1)
                    nc.vector.tensor_reduce(nmax[:, 4 * m:4 * m + nh], ps[m % 2][:, 0:nh * w].rearrange("p (h k) -> p h k", h=nh),
                                            AX, ALU.max, negate=True).then_inc(max_done, 1)
                if m == 8:
                    dve.wait_ge(score_ps, 2)
                    nc.vector.tensor_tensor(acc_s[:], ps[3][0:NS_TOK, 0:NK_S], c_(C_MASKS, NK_S, NS_TOK), ALU.add)\
                        .then_inc(score_ready, 1)
                    dve.wait_ge(score_ready, 1)
                if 8 <= m - 2 < N_STEPS and out_group(m - 2)[1]:
                    g = out_group(m - 2)[0]
                    kind, form, _ = step_kind(m - 2)
                    dve.wait_ge(out_hi, g + 1)
                    lo_t, hi_t = (blo, bhi) if kind == MOBA else (alo, ahi)
                    for (dst, src), (hi, _) in zip(out_views(lo_t, ps[4 + g % 2], kind, form),
                                                   out_views(hi_t, ps[4 + g % 2], kind, form)):
                        ins = nc.vector.tensor_tensor(dst, src, hi.bitcast(F32), ALU.subtract)
                    ins.then_inc(out_lo, 1)

            def attend_late(m):
                if m < 6:
                    kind, form, i = step_kind(m)
                    half, blocks, w = step_heads(form, i)
                    acc = acc1 if form == 1 else acc0
                    mask = c_(C_CAUSAL, 2 * P) if form == 1 else c_(C_CAUSAL + P, P)
                    dve.wait_ge(soft_done, m + 1)
                    for j, b in enumerate(blocks):
                        h = 2 * b + half
                        ins = nc.vector.scalar_tensor_tensor(
                            acc[:], probs[:, m % 2, j * w:(j + 1) * w], wi_p[:, form, h:h + 1],
                            mask if i == 0 and j == 0 else acc[:], ALU.mult, ALU.add)
                        if j == len(blocks) - 1:
                            ins.then_inc(idx_acc, 1)
                            dve.wait_ge(idx_acc, m + 1)
                        else:
                            link(ins)
                if 8 <= m < N_STEPS:
                    nh = {1: 2, 0: 4, 2: 1}[step_kind(m)[1]]
                    dve.wait_ge(soft_done, m + 1)
                    nc.vector.reciprocal(rinv[:, 4 * m:4 * m + nh], rsum[:, 4 * m:4 * m + nh]).then_inc(rinv_ready, 1)
                if m >= CHORE_STEP:
                    for _ in range(CHORES_PER_STEP):
                        if chores and (m >= 8 or len(chores) > TOPK_SAMPLE // 8 + 2):
                            chores.pop(0)()

            for u in range(U_END):
                if u in STEP_OF_SLOT:
                    attend(STEP_OF_SLOT[u])
                if u - 1 in NORMED:
                    i = index_among(u - 1, NORMED)
                    g = GAIN_OF[u - 1]
                    dve.wait_ge(zroot_ready, i + 1)
                    link(nc.vector.reciprocal(roots[:, i % 2, :], roots[:, i % 2, :]))
                    if i == 0:
                        dve.wait_ge(scaled_gains, 2)
                    nc.vector.scalar_tensor_tensor(zloc[u - 1], zloc[u - 1], gains[:, g:g + 1], roots[:, i % 2, :],
                                                   ALU.mult, ALU.mult).then_inc(zn_ready, 1)
                if u - 2 in ROTATED:
                    i = index_among(u - 2, ROTATED)
                    z = zloc[u - 2]
                    dve.wait_ge(swapped, i + 1)
                    nc.vector.tensor_tensor(tmp[:, 0, 0, :], ps[4][:, 0:N], c_(C_SIN, N), ALU.mult)
                    link(nc.vector.tensor_tensor(z, z, c_(C_COS, N), ALU.mult))
                    nc.vector.tensor_tensor(z, z, tmp[:, 0, 0, :], ALU.add).then_inc(z_final, 1)
                split_lo(vp + u + AHEAD)
                if u == WCOL_SLOT:
                    dve.wait_ge(tok_ready, 3)
                    nc.vector.tensor_scalar(wi_p[:], tok[:, 0:2, 448:456], HEADS ** -0.5, HD ** -0.5,
                                            ALU.mult, ALU.mult).then_inc(wi_ready, 1)
                    dve.wait_ge(wi_ready, 1)
                    dve.wait_ge(wexp_ps, 1)
                    hs = c_(C_HSEL, HEADS).unsqueeze(1).to_broadcast([P, 2, HEADS])
                    link(nc.vector.tensor_tensor(wsel[:], ps[3][:, 0:2 * HEADS].rearrange("p (g h) -> p g h", g=2), hs, ALU.mult))
                    link(nc.vector.tensor_reduce(wcol[:], wsel[:], AX, ALU.add))
                    link(nc.vector.tensor_scalar(wcol[:], wcol[:], HEADS ** -0.5, HD ** -0.5, ALU.mult, ALU.mult))
                    for g in range(2):
                        nc.vector.tensor_scalar(wexp[:, g, :], c_(C_EXPT + g * NS_TOK, NS_TOK), wcol[:, g:g + 1], None,
                                                ALU.mult).then_inc(wexp_ready, 1)
                if u in STEP_OF_SLOT:
                    attend_late(STEP_OF_SLOT[u])
            for m in range(U_END - FIRST_STEP_SLOT, N_STEPS + 2):
                attend(m)
                attend_late(m)
            assert not chores

            vu = first["U"][1]

            def merged_lo(j):
                dve.wait_ge(m_hi, j + 1)
                nc.vector.tensor_tensor(nlo[:, j, :], tmp[:, j % 2, 0, :], nhi[:, j, :].bitcast(F32), ALU.subtract).then_inc(m_lo, 1)

            for j in range(8):
                dve.wait_ge(unit_done, vu + j + 1)
                dve.wait_ge(sig_ready, 3 + j // 4)
                ba, bb = (ps[6], ps[7]) if j % 2 == 0 else (ps[0], ps[1])
                nc.vector.tensor_tensor(gates[:, j, :], gates[:, j, :], ba[:, 0:N], ALU.mult)
                link(nc.vector.tensor_tensor(gates[:, 8 + j, :], gates[:, 8 + j, :], bb[:, 0:N], ALU.mult))
                nc.vector.tensor_tensor(tmp[:, j % 2, 0, :], gates[:, j, :], gates[:, 8 + j, :], ALU.add).then_inc(m_scaled, 1)
                split_lo(vu + j + AHEAD)
                merged_lo(j)
            vo = first["O"][1]
            for j in range(8):
                dve.wait_ge(unit_done, vo + j + 1)
                nc.vector.tensor_tensor(x[:, j, :], ps[2 + j % 2][:, 0:N], x[:, j, :], ALU.add).then_inc(o_evac, 1)
                split_lo(vo + j + AHEAD)
            norm(2, 16)
            gate_up(2)

            def y_out(k):
                dve.wait_ge(yT_done, k + 1)
                bank = ps[k % 2]
                nc.vector.tensor_copy(ytok[:, 0:2, k * P:(k + 1) * P], bank[:, 0:2 * P].rearrange("p (t c) -> p t c", t=2))
                nc.vector.tensor_copy(ytok[0:NS_TOK, 2, k * P:(k + 1) * P], bank[0:NS_TOK, 2 * P:3 * P]).then_inc(y_ready, 1)

            for turn in range(D_LOOPS):
                down_turn(2, 0, 2 * turn)
                if turn == 0:
                    for k in range(2):
                        y_out(k)
            for k in range(2, KB):
                y_out(k)

        @block.tensor
        def _(pe):
            def unit(v, out, xs, it=0, kl=None, start=True, stop=True, wait_x=None, done=True):
                n, c0, w, nk = units[v]
                pe.wait_ge(w_lo, v + 1 + LOOP_UNITS * it)
                ks = range(nk) if kl is None else kl
                for i, k in enumerate(ks):
                    if wait_x:
                        wait_x(k)
                    hi, lo, r = xs(k)
                    h, l = whi[0:r, v % NU, k, 0:w], wlo[0:r, v % NU, k, 0:w]
                    nc.tensor.matmul(out[0:w, 0:N], h, hi, start=start and i == 0, stop=False)
                    nc.tensor.matmul(out[0:w, 0:N], h, lo, start=False, stop=False)
                    ins = nc.tensor.matmul(out[0:w, 0:N], l, hi, start=False, stop=stop and i == len(ks) - 1)
                if done:
                    ins.then_inc(unit_done, 1)

            ident = c_(C_ID, P)
            pe.wait_ge(const_in, 16)
            pe.wait_ge(rows_in, 16 * 12)
            nc.tensor.transpose(ps[4][:, 0:GAIN_ROWS], rows[:], cst[0:GAIN_ROWS, C_ID:C_ID + GAIN_ROWS]).then_inc(gains_T, 1)
            pe.wait_ge(x_in, 32)
            for k in range(KB):
                if k >= 4:
                    pe.wait_ge(x_ready, k - 3)
                for t in range(3):
                    r = P if t < 2 else NS_TOK
                    ins = nc.tensor.transpose(ps[k % 4][:, t * P:t * P + r], xtok[0:r, t, k * P:(k + 1) * P],
                                              cst[0:r, C_ID:C_ID + r])
                ins.then_inc(xT_done, 1)

            def mean_square(r):
                pe.wait_ge(squares_ready, r + 1)
                nc.tensor.matmul(ps[0][:, 0:N], c_(C_ONE, P), ssq, start=True, stop=True).then_inc(ms_done, 1)

            normed = lambda k: (nhi[:, k, :], nlo[:, k, :], P)

            def pair(f, p, it=0, r=None):
                v = first[f"G{f}"][1] + 2 * p
                pe.wait_ge(pair_free, (f - 1) * FB + p + 1 + LOOP_PAIRS * it)
                for g in range(2):
                    unit(v + g, ps[2 * (p % 3) + g], normed, it)

            def gate_up(f, r):
                pe.wait_ge(n_lo, KB * (r + 1))
                with pe.Fori(0, G_LOOPS) as it:
                    for p in range(LOOP_PAIRS):
                        pair(f, p, it)
                for p in range(G_LOOPS * LOOP_PAIRS, FB):
                    pair(f, p)
                pe.wait_ge(h_lo, f * FB)

            def down_turn(f, it, q0=0, between=None):
                v = first[f"D{f}"][1] + 6 * q0
                for q in range(2):
                    pe.wait_ge(down_evac, KB * (f - 1) + 2 * (q0 + q) + DOWN_FREE - 2 + 4 * it)
                    for t in range(3):
                        for m in range(2):
                            xs = lambda k, t=t: (hhi[0:FTAIL if KB * t + k == FB - 1 else P, KB * t + k, :],
                                                 hlo[0:FTAIL if KB * t + k == FB - 1 else P, KB * t + k, :],
                                                 FTAIL if KB * t + k == FB - 1 else P)
                            unit(v + 6 * q + 2 * t + m, ps[(6, 4)[q] + m], xs, it, start=t == 0, stop=t == 2)
                    if between:
                        between(q0 + q)

            mean_square(0)
            gate_up(1, 0)
            with pe.Fori(0, D_LOOPS) as it:
                down_turn(1, it)

            pe.wait_ge(pages_in, 16 * 7 * N_SEQ * NPG)
            for g in range(12):
                if g == 6:
                    mean_square(1)
                if g >= 3:
                    pe.wait_ge((keysT_act, keysT_dve)[(g - 3) % 2], (g - 3) // 2 + 1)
                for j in range(4):
                    ins = nc.tensor.transpose(ps[1 + g % 3][:, j * P:(j + 1) * P], kraw[:, g // 4, (g % 4) * 4 + j, :], ident)
                ins.then_inc(keysT_done, 1)

            def attend(m):
                if m < N_STEPS:
                    kind, form, i = step_kind(m)
                    bank = ps[m % 2]
                    if m >= 2:
                        pe.wait_ge(soft_done, m - 1)
                    if m == 0:
                        pe.wait_ge(tok_ready, 3)
                    if i == 0 and form == 1:
                        pe.wait_ge(z_final, index_among({IDX: U_KI, MOBA: U_QB + 3, DSA: U_QA + 3}[kind], ROTATED) + 1)
                    if form == 2 and i == 0:
                        pe.wait_ge(qz_ready, 2 * (kind + 1))
                        pe.wait_ge(keysT_act, 6)
                        pe.wait_ge(keysT_dve, 6)
                    if m == 8:
                        pe.wait_ge(masks_ready, 5)
                    if kind == DSA and i == 0:
                        pe.wait_ge(sel_ready, {1: 1, 0: 2, 2: 3}[form])
                    k_new = K_OF[kind]
                    if form == 2:
                        if kind != IDX:
                            nc.tensor.matmul(bank[:, 0:NK_S], expb[:, i * P:(i + 1) * P],
                                             masksb[:] if kind == MOBA else sel_s[:], start=True, stop=False)
                        for b in range(4):
                            s = 4 * i + b
                            nc.tensor.matmul(bank[32 * b:32 * b + 32, 0:PAST], qz[:, kind, 32 * s:32 * s + 32],
                                             kt[:, KT_OF[kind], s, :], start=kind == IDX, stop=kind == IDX)
                        ins = nc.tensor.matmul(bank[:, PAST:NK_S], qz[:, kind, i * P:(i + 1) * P], k_new[:, NP_TOK:N],
                                               start=kind == IDX, stop=True)
                    else:
                        half, blocks, w = step_heads(form, i)
                        if kind != IDX:
                            mask = ((causalb[:] if kind == MOBA else sel1[:]) if form == 1
                                    else (causalb[:, P:2 * P] if kind == MOBA else sel0[:]))
                            nh = len(blocks)
                            nc.tensor.matmul(bank[:, :].rearrange("p (h k) -> p h k", h=nh), idb[:],
                                             mask.unsqueeze(1).to_broadcast([P, nh, w]), start=True, stop=False)
                        rows_ = slice(half * HD, (half + 1) * HD)
                        for j, b in enumerate(blocks):
                            ins = nc.tensor.matmul(bank[:, j * w:(j + 1) * w], Q_OF[kind][rows_, b, form * P:(form + 1) * P],
                                                   k_new[rows_, 0:w], start=kind == IDX,
                                                   stop=kind == IDX or j == len(blocks) - 1)
                    ins.then_inc(logits_done, 1)
                if m - 1 in (6, 7):
                    g = m - 1 - 6
                    pe.wait_ge(soft_done, m)
                    pe.wait_ge(wexp_ready, 2)
                    nc.tensor.matmul(ps[3][0:NS_TOK, 0:NK_S], wexp[:, g, :], probs[:, (m - 1) % 2, 0:NK_S],
                                     start=g == 0, stop=g == 1).then_inc(score_ps, 1)
                if 8 <= m - 1 < N_STEPS:
                    n = m - 1 - 8
                    form = step_kind(m - 1)[1]
                    pr = probs[:, (m - 1) % 2, :]
                    pe.wait_ge(probs_ready, n + 1)
                    if n >= 2:
                        pe.wait_ge(probsT_ready, n - 1)
                    if n == 1:
                        pe.wait_ge(score_ready, 1)
                    bank = ps[2 + n % 2]
                    if form == 2:
                        for j in range(2):
                            nc.tensor.transpose(bank[:, j * P:(j + 1) * P], pr[:, j * P:(j + 1) * P], ident)
                        ins = nc.tensor.transpose(bank[0:NS_TOK, 2 * P:3 * P], pr[:, PAST:NK_S], ident)
                    else:
                        for j in range(4):
                            ins = nc.tensor.transpose(bank[:, j * P:(j + 1) * P], pr[:, j * P:(j + 1) * P], ident)
                    ins.then_inc(probsT_done, 1)
                if 8 <= m - 2 < N_STEPS:
                    n = m - 2 - 8
                    kind, form, i = step_kind(m - 2)
                    g, _ = out_group(m - 2)
                    bank = ps[4 + g % 2]
                    pe.wait_ge(probsT_ready, n + 1)
                    if i == 0 and g >= 2:
                        pe.wait_ge(out_lo, g - 1)
                    if n == 0:
                        pe.wait_ge(z_final, len(ROTATED))
                    pT = probsT[:, n % 2, :]
                    if form == 2:
                        if kind == DSA and i == 0:
                            pe.wait_ge(va2_ready, 2)
                        v_new = va2[:, :] if kind == DSA else tok[0:NS_TOK, 2, 256:384]
                        cols = slice(i * P, (i + 1) * P)
                        nc.tensor.matmul(bank[:, cols], v_new, pT[0:NS_TOK, 2 * P:3 * P], start=True, stop=False)
                        for b in range(4):
                            for j in range(NPG):
                                pg = (4 * i + b) * NPG + j
                                last = b == 3 and j == NPG - 1
                                rhs = pT[:, j * P + 32 * b:j * P + 32 * b + 32]
                                dst = slice(i * P + 32 * b, i * P + 32 * b + 32)
                                if kind == MOBA:
                                    ins = nc.tensor.matmul(bank[:, dst], vb_pg[:, pg, :], rhs, start=False, stop=last)
                                else:
                                    for s in range(2):
                                        ins = nc.tensor.matmul(bank[s * HD:(s + 1) * HD, dst], va_pg[:, pg, :], rhs,
                                                               start=False, stop=last)
                    else:
                        half, blocks, w = step_heads(form, i)
                        vc = 384 if kind == DSA else 256 + half * HD
                        for j, b in enumerate(blocks):
                            for t in range(w // P):
                                ins = nc.tensor.matmul(bank[half * HD:(half + 1) * HD, b * P:(b + 1) * P],
                                                       tok[:, t, vc:vc + HD], pT[:, (j * (w // P) + t) * P:(j * (w // P) + t + 1) * P],
                                                       start=t == 0, stop=t == w // P - 1)
                    ins.then_inc(pv_done, 1)

            vp = first["P"][1]
            for u in range(U_END):
                if u in STEP_OF_SLOT:
                    attend(STEP_OF_SLOT[u])
                if u >= 2:
                    pe.wait_ge(z_ready, u - 1)
                wait_x = (lambda k: pe.wait_ge(n_lo, KB + k + 1)) if u == 0 else None
                unit(vp + u, ps[6 + u % 2], normed, wait_x=wait_x)
                if u - 1 in NORMED:
                    i = index_among(u - 1, NORMED)
                    pe.wait_ge(zsq_ready, i + 1)
                    if i:
                        pe.wait_ge(zroot_ready, i)
                    nc.tensor.matmul(ps[5][:, 0:N], c_(C_BLK, P), act_tmp[:, i % 2, 0, :], start=True, stop=True).then_inc(zms_done, 1)
                if u - 2 in ROTATED:
                    i = index_among(u - 2, ROTATED)
                    if u - 2 in NORMED:
                        pe.wait_ge(zn_ready, index_among(u - 2, NORMED) + 1)
                    if i:
                        pe.wait_ge(z_final, i)
                    nc.tensor.matmul(ps[4][:, 0:N], c_(C_SWAP, P), zloc[u - 2], start=True, stop=True).then_inc(swapped, 1)
                if u == TOK_SLOT:
                    pe.wait_ge(z_final, index_among(U_KB, ROTATED) + 1)
                    pe.wait_ge(z_ready, U_VW + 1)
                    for t in range(3):
                        r = P if t < 2 else NS_TOK
                        tc_ = slice(t * P, t * P + r)
                        for b, w, c0 in ((0, HD, 0), (1, HD, 64), (2, P, 128), (3, P, 256), (4, HD + HEADS, 384)):
                            ins = nc.tensor.transpose(ps[(2, 3, 0)[t]][0:r, c0:c0 + w], kv[0:w, b, tc_], cst[0:w, C_ID:C_ID + w])
                        ins.then_inc(tok_T, 1)
                if u == WCOL_SLOT:
                    pe.wait_ge(tok_ready, 3)
                    for g in range(2):
                        ins = nc.tensor.matmul(ps[3][:, g * HEADS:(g + 1) * HEADS], c_(C_EXP + g * P, P, NS_TOK),
                                               tok[0:NS_TOK, 2, 448:456], start=True, stop=True)
                    ins.then_inc(wexp_ps, 1)
            for m in range(U_END - FIRST_STEP_SLOT, N_STEPS + 2):
                attend(m)

            vu = first["U"][1]
            pe.wait_ge(out_lo, 6)
            pe.wait_ge(z_ready, U_END)
            for j in range(8):
                ba, bb = (ps[6], ps[7]) if j % 2 == 0 else (ps[0], ps[1])
                if j >= 2:
                    pe.wait_ge(m_scaled, j - 1)
                unit(vu + j, ba, lambda k: (ahi[:, k, :], alo[:, k, :], P), kl=range(4), done=False)
                unit(vu + j, bb, lambda k: (bhi[:, k - 4, :], blo[:, k - 4, :], P), kl=range(4, 8))
            vo = first["O"][1]
            for j in range(8):
                if j >= 2:
                    pe.wait_ge(o_evac, j - 1)
                wait_x = (lambda k: pe.wait_ge(m_lo, k + 1)) if j == 0 else None
                unit(vo + j, ps[2 + j % 2], normed, wait_x=wait_x)
            mean_square(2)
            gate_up(2, 2)

            def y_T(k):
                pe.wait_ge(down_evac, DOWN_FREE + KB + k + 1)
                if k >= 2:
                    pe.wait_ge(y_ready, k - 1)
                for t in range(3):
                    r = P if t < 2 else NS_TOK
                    ins = nc.tensor.transpose(ps[k % 2][0:r, t * P:(t + 1) * P], x[:, k, t * P:t * P + r], ident)
                ins.then_inc(yT_done, 1)

            down_turn(2, 0, 0, between=lambda q: [y_T(k) for k in range(2 * q - 2, 2 * q)] if q else None)
            down_turn(2, 0, 2, between=lambda q: [y_T(k) for k in range(2 * q - 2, 2 * q)])
            for k in range(KB - 2, KB):
                y_T(k)


INPUTS = ("x_prompt x_sample cache_k_a cache_v_a cache_kidx_a cache_k_b cache_v_b page_table ffn1_norm ffn1_w_in "
          "ffn1_w_out mix_norm w_in q_norm_a k_norm_a q_norm_b k_norm_b gate_bias w_up_a w_up_b w_out ffn2_norm "
          "ffn2_w_in ffn2_w_out").split()
LAYER_WEIGHTS = "ffn1_w_in ffn1_w_out w_in w_up_a w_up_b w_out ffn2_w_in ffn2_w_out".split()


def kernel(**inputs):
    import concourse.bacc as bacc
    from concourse.bass_utils import run_bass_kernel_spmd

    nc = bacc.Bacc("TRN2", target_bir_lowering=False, num_devices=1)
    arrays, a = {}, {}
    for name in INPUTS:
        v = np.ascontiguousarray(inputs[name])
        arrays[f"in_{name}"] = v
        a[name] = nc.dram_tensor(f"in_{name}", v.shape, mybir.dt.from_np(v.dtype), kind="ExternalInput").ap()
    for name in LAYER_WEIGHTS:
        a[name] = a[name].rearrange("l r c -> (l r) c")
    arrays["in_constants"] = shape_constants()
    a["constants"] = nc.dram_tensor("in_constants", (P, C_ALL), F32, kind="ExternalInput").ap()
    returned = [("y_prompt", (1, NP_TOK, D)), ("y_sample", (N_SEQ, N_NEW, D))]
    for g, lead in (("p", (1, 1, NP_TOK)), ("s", (1, N_SEQ, N_NEW))):
        returned += [(f"new_k_a_{g}", lead + (1, HD)), (f"new_v_a_{g}", lead + (1, HD)), (f"new_kidx_{g}", lead + (HD,)),
                     (f"new_k_b_{g}", lead + (2, HD)), (f"new_v_b_{g}", lead + (2, HD))]
    o = {}
    for name, shape in returned:
        t = nc.dram_tensor(f"out_{name}", shape, F32, kind="ExternalOutput").ap()
        if name.endswith("_p"):
            t = t.rearrange("l b (t p) d -> p (l b t) d" if len(shape) == 4 else "l b (t p) h d -> p (l b t) (h d)", p=P)
        elif name.endswith("_s"):
            t = t.rearrange("l b t d -> (l b t) d" if len(shape) == 4 else "l b t h d -> (l b t) (h d)")
        o[name] = t
    build(nc, a, o)
    r = run_bass_kernel_spmd(nc, [arrays], core_ids=[0])
    return tuple(r.results[0][f"out_{name}"] for name, _ in returned)
```

```python
from contextlib import ExitStack

import numpy as np

import concourse.bass as bass
from concourse import mybir

F32 = mybir.dt.float32
F32R = mybir.dt.float32r
BF16 = mybir.dt.bfloat16
I32 = mybir.dt.int32
ALU = mybir.AluOpType
ACT = mybir.ActivationFunctionType
AX = mybir.AxisListType.X

P = 128
EPS = 1e-6
ROPE_THETA = 10000.0
NEG = -float(2.0 ** 100)
TAKEN = -3.0e38
TAKEN_LIMIT = -2.0e38

NP_TOK, N_SEQ, N_NEW = 256, 8, 4
NS_TOK = N_SEQ * N_NEW
N = NP_TOK + NS_TOK
PAST = 256
PAGE = 128
NPG = PAST // PAGE
HD = 64
HEADS = 8
TOPK_PROMPT = NP_TOK // 4
TOPK_SAMPLE = (PAST + N_NEW) // 4
NK_S = PAST + NS_TOK
D = 1024
KB = D // P
DFF = 2752
FB = -(-DFF // P)
FTAIL = DFF - (FB - 1) * P
TC = 256
NR, NU = 3, 4
AHEAD = NU

C_ID, C_SWAP, C_BLK, C_ONE = 0, P, 2 * P, 3 * P
C_COS, C_SIN = 4 * P, 4 * P + N
C_CAUSAL = C_SIN + N
C_MASKS = C_CAUSAL + 2 * P
C_EXP = C_MASKS + NK_S
C_EXPT = C_EXP + 2 * P
C_HSEL = C_EXPT + 2 * NS_TOK
C_ALL = C_HSEL + HEADS


def shape_constants():
    c = np.zeros((P, C_ALL), np.float32)
    half = HD // 2
    inv = (np.float32(ROPE_THETA) ** (-np.arange(half, dtype=np.float32) / np.float32(half))).astype(np.float32)
    pos = np.concatenate([np.arange(NP_TOK), np.tile(PAST + np.arange(N_NEW), N_SEQ)]).astype(np.float32)
    ang = (pos[None, :] * inv[:, None]).astype(np.float32)
    c[:, C_COS:C_COS + N] = np.tile(np.cos(ang), (4, 1))
    c[:, C_SIN:C_SIN + N] = np.tile(np.concatenate([-np.sin(ang), np.sin(ang)]), (2, 1))
    p = np.arange(P)
    c[p ^ half, C_SWAP + p] = 1.0
    c[p, C_ID + p] = 1.0
    c[:, C_BLK:C_BLK + P] = (p[:, None] // HD == p[None, :] // HD) / HD
    c[:, C_ONE:C_ONE + P] = 1.0 / D
    keys = np.arange(2 * P)
    c[:, C_CAUSAL:C_CAUSAL + 2 * P] = np.where(keys[None, :] <= P + p[:, None], 0.0, NEG)
    b, t = np.arange(NS_TOK) // N_NEW, np.arange(NS_TOK) % N_NEW
    c[:NS_TOK, C_MASKS + PAST:C_MASKS + NK_S] = np.where(
        (b[:, None] == b[None, :]) & (t[None, :] <= t[:, None]), 0.0, NEG)
    rb, rh, rt = p // 32, p % 32 // N_NEW, p % N_NEW
    for g in range(2):
        e = (b[:, None] == 4 * g + rb[None, :]) & (t[:, None] == rt[None, :])
        c[:NS_TOK, C_EXP + g * P:C_EXP + (g + 1) * P] = e
        c[:, C_EXPT + g * NS_TOK:C_EXPT + (g + 1) * NS_TOK] = e.T
    c[:, C_HSEL:C_HSEL + HEADS] = rh[:, None] == np.arange(HEADS)[None, :]
    return c


def weight_plan():
    tiles, units, first = [], [], {}

    def ffn(f):
        first[f"G{f}"] = len(tiles), len(units)
        w = f"ffn{f}_w_in"
        for t in range(FB // 2):
            width = min(TC, DFF - TC * t)
            n = len(tiles)
            for c0 in (0, DFF):
                tiles.append([(0, P, 0, KB, 0, width, w, 0, c0 + TC * t)])
            for m in range(2):
                for g in range(2):
                    units.append((n + g, m * P, min(P, width - m * P), KB))
        first[f"D{f}"] = len(tiles), len(units)
        w = f"ffn{f}_w_out"
        for c in range(D // TC):
            for k0 in range(0, FB, KB):
                kb = min(KB, FB - k0)
                n = len(tiles)
                full = kb - (k0 + kb == FB)
                tiles.append([(0, P, 0, full, 0, TC, w, k0 * P, c * TC)])
                if full < kb:
                    tiles[-1].append((0, FTAIL, full, 1, 0, TC, w, (FB - 1) * P, c * TC))
                units.extend((n, m * P, P, kb) for m in range(2))

    def one(*cols):
        tiles.append([(0, P, 0, KB, a, w, "w_in", 0, s) for a, w, s in cols])

    ffn(1)
    first["P"] = len(tiles), len(units)
    wqa, wk, wq = 0, HD, HEADS * HD
    ka, va = wq, wq + wk
    qi = va + wk
    ki = qi + wq
    wi = ki + wk
    qb = wi + HEADS
    kb_ = qb + wq
    vb = kb_ + 2 * HD
    ga = vb + 2 * HD
    one((0, TC, qi))
    one((0, TC, qi + TC))
    one((0, HD, ka), (HD, HD, ka), (2 * HD, HD, ki), (3 * HD, HD, ki))
    one((0, TC, kb_))
    qbh = [((s * HD), HD, qb + (m + 4 * s) * HD) for m in range(4) for s in range(2)]
    at = lambda m, a: [(a + qbh[2 * m + s][0], HD, qbh[2 * m + s][2]) for s in range(2)]
    one((0, HD, va), (HD, HEADS, wi), *at(0, P))
    one(*at(1, 0), *at(2, P))
    one(*at(3, 0), (P, P, wqa))
    one((0, TC, wqa + P))
    one((0, P, wqa + 3 * P), (P, P, ga))
    for g in range(7):
        one((0, TC, ga + P + g * TC))
    one((0, P, ga + 15 * P))
    base = first["P"][0]
    for u in range(33):
        units.append((base + u // 2, (u % 2) * P, HD + HEADS if u == 8 else P, KB))
    first["U"] = len(tiles), len(units)
    for c in range(D // TC):
        n = len(tiles)
        tiles.append([(0, P, 0, 4, 0, TC, "w_up_a", 0, c * TC)]
                     + [(s * HD, HD, 4, 4, 0, TC, "w_up_b", s * 4 * HD, c * TC) for s in range(2)])
        units.extend((n, m * P, P, KB) for m in range(2))
    first["O"] = len(tiles), len(units)
    for c in range(D // TC):
        n = len(tiles)
        tiles.append([(0, P, 0, KB, 0, TC, "w_out", 0, c * TC)])
        units.extend((n, m * P, P, KB) for m in range(2))
    ffn(2)
    return tiles, units, first


U_QI, U_KA, U_KI, U_KB, U_VB, U_VW, U_QB, U_QA, U_GATE, U_END = 0, 4, 5, 6, 7, 8, 9, 13, 17, 33
NORMED = [U_KA, U_KB] + list(range(U_QB, U_QA + 4))
LAST_QUERY = {U_QI + 3: 0, U_QB + 3: 1, U_QA + 3: 2}
ROTATED = [u for u in range(U_GATE) if u not in (U_VB, U_VW)]
GAIN_OF = {U_KA: 41, U_KB: 43} | {u: 42 for u in range(U_QB, U_QB + 4)} | {u: 40 for u in range(U_QA, U_QA + 4)}
GAIN_ROWS = 44

IDX, MOBA, DSA = 0, 1, 2
N_STEPS = 24
STEPS_OF_SLOT = {11 + i: [2 * i, 2 * i + 1] for i in range(4)} | {u: [u - 8] for u in range(16, U_END)}
STEPS_AFTER = [U_END - 8]
TOK_SLOT, WCOL_SLOT = 9, 10
CHORE_SLOT, CHORES_PER_SLOT = 14, 2


def step_kind(m):
    kind, a = divmod(m, 8)
    return (kind, 1, a) if a < 4 else (kind, 0, a - 4) if a < 6 else (kind, 2, a - 6)


def step_heads(form, i):
    return (i // 2, [2 * (i % 2), 2 * (i % 2) + 1], 2 * P) if form == 1 else (i, [0, 1, 2, 3], P)


def out_group(m):
    kind, form, i = step_kind(m)
    g = (kind - 1) * 3 + {1: 0, 0: 1, 2: 2}[form]
    return g, i == {1: 3, 0: 1, 2: 1}[form]


def build(nc, a, o):
    tiles, units, first = weight_plan()
    landed, total = [], [0] * NR
    for n, t in enumerate(tiles):
        total[n % NR] += 16 * len(t)
        landed.append(total[n % NR])
    tile_split = [0] * len(tiles)
    for v, u in enumerate(units):
        tile_split[u[0]] = v + 1

    ctx = ExitStack()
    with ctx:
        sems = {}

        def sem(name):
            sems[name] = ctx.enter_context(nc.semaphore(name))
            return sems[name]

        here = [-(-nc.sbuf_base // 128) * 128]

        def sb(name, shape, dt=F32, at=None):
            size = int(np.prod(shape[1:])) * (2 if dt == BF16 else 4)
            where = here[0] if at is None else at
            t = nc.alloc_sbuf_tensor_at(name, shape, dt, offset=where)
            if at is None:
                here[0] += -(-size // 32) * 32
            return t, where

        def new(name, shape, dt=F32):
            return sb(name, shape, dt)[0]

        raw = new("raw", [P, NR, KB, TC])
        whi = new("whi", [P, NU, KB, P], F32R)
        wlo = new("wlo", [P, NU, KB, P], F32R)
        x = new("x", [P, KB, N])
        nhi = new("nhi", [P, KB, N], F32R)
        nlo = new("nlo", [P, KB, N], F32R)
        hhi, at_h = sb("hhi", [P, FB, N], F32R)
        hlo = new("hlo", [P, FB, N], F32R)
        blk = lambda i: at_h + i * N * 4
        xtok, _ = sb("xtok", [P, 3, D], at=at_h)
        qi, _ = sb("qi", [P, 4, N], at=blk(0))
        qb, _ = sb("qb", [P, 4, N], at=blk(4))
        qa, _ = sb("qa", [P, 4, N], at=blk(8))
        bhi, _ = sb("bhi", [P, 4, N], F32R, at=blk(0))
        blo, _ = sb("blo", [P, 4, N], F32R, at=blk(12))
        ahi, _ = sb("ahi", [P, 4, N], F32R, at=blk(4))
        alo, _ = sb("alo", [P, 4, N], F32R, at=blk(16))
        gates, _ = sb("gates", [P, 16, N], at=blk(20))
        kv, _ = sb("kv", [P, 5, N], at=blk(36))
        va2, _ = sb("va2", [NS_TOK, P], at=blk(41))
        masksb, _ = sb("masksb", [NS_TOK, NK_S], BF16, at=blk(42))
        expb, _ = sb("expb", [NS_TOK, 2 * P], BF16, at=blk(43))
        kt, at_kt = sb("kt", [P, 3, N_SEQ, PAST])
        ytok, _ = sb("ytok", [P, 3, D], at=at_kt)
        mhi, _ = sb("mhi", [P, KB, N], F32R, at=blk(36))
        mlo, _ = sb("mlo", [P, KB, N], F32R, at=at_kt)
        va_pg = new("va_pg", [P, N_SEQ * NPG, HD])
        vb_pg = new("vb_pg", [P, N_SEQ * NPG, P])
        cst = new("cst", [P, C_ALL])
        idb = new("idb", [P, P], BF16)
        causalb = new("causalb", [P, 2 * P], BF16)
        gains = new("gains", [P, GAIN_ROWS])
        ptab = new("ptab", [1, N_SEQ * NPG], I32)
        tmp = new("tmp", [P, 2, 1, N])
        act_tmp = new("act_tmp", [P, 2, 1, N])
        rms, sq_block, ssq = act_tmp[:, 0, 0, :], act_tmp[:, 0, 0, :], act_tmp[:, 1, 0, :]
        rstd = new("rstd", [P, N])
        eps_col = new("eps_col", [P, 4])
        kraw, at_att = sb("kraw", [P, 3, N_SEQ * NPG, P])
        end_kraw = here[0]
        here[0] = at_att
        rows, _ = sb("rows", [GAIN_ROWS, P], at=at_att)
        rot_tmp = tmp[:, :, 0, :]
        roots = new("roots", [P, 2, N])
        tok = new("tok", [P, 3, 456])
        probs = new("probs", [P, 2, 512])
        probsT = new("probsT", [P, 2, 512])
        qz = new("qz", [P, 3, 2 * P])
        acc1 = new("acc1", [P, 2 * P])
        acc0 = new("acc0", [P, P])
        acc_s = new("acc_s", [NS_TOK, NK_S])
        best = new("best", [P, 8])
        sel1 = new("sel1", [P, 2 * P], BF16)
        sel0 = new("sel0", [P, P], BF16)
        sel_s = new("sel_s", [NS_TOK, NK_S], BF16)
        nmax = new("nmax", [P, 4 * N_STEPS])
        rsum = new("rsum", [P, 4 * N_STEPS])
        rinv = new("rinv", [P, 4 * N_STEPS])
        wi_p = new("wi_p", [P, 2, HEADS])
        wsel = new("wsel", [P, 2, HEADS])
        wcol = new("wcol", [P, 2])
        wexp = new("wexp", [P, 2, NS_TOK])
        assert here[0] <= nc.sbuf_usable_end and end_kraw <= nc.sbuf_usable_end, (here, end_kraw, nc.sbuf_usable_end)
        ps = [ctx.enter_context(nc.psum_tensor(f"ps{i}", [P, 512], F32)) for i in range(8)]
        zloc = ([qi[:, i, :] for i in range(4)] + [kv[:, i, :] for i in range(5)]
                + [qb[:, i, :] for i in range(4)] + [qa[:, i, :] for i in range(4)])
        KT_OF = {IDX: 0, MOBA: 1, DSA: 2}
        Q_OF = {IDX: qi, MOBA: qb, DSA: qa}
        K_OF = {IDX: kv[:, 1, :], MOBA: kv[:, 2, :], DSA: kv[:, 0, :]}
        c_ = lambda at, n, rows_=P: cst[0:rows_, at:at + n]

        raw_in = [sem(f"raw_in{i}") for i in range(NR)]
        (const_in, consts_in, x_in, rows_in, ptab_in, pages_in, out_done, gains_T, gains_ready, scaled_gains, masks_ready,
         xT_done, x_ready, squares_ready, ms_done, root_ready, rstd_ready, scaled, n_hi, n_lo,
         w_hi, w_lo, unit_done, gate_scaled, up_scaled, silu_done, pair_free, prod_ready, h_hi, h_lo, down_evac, keysT_done, keysT_act, keysT_dve,
         z_ready, zsq_ready, zg_ready, zms_done, zroot_ready, zrstd_ready, zn_ready, swapped, rot_ready, rot_cos, z_final, tok_T, tok_ready, wexp_ps, wexp_ready,
         qz_ready, qz_zero, logits_done, max_done, soft_done, idx_acc, score_ps, score_ready, sel_ready, rinv_ready,
         probs_ready, probsT_done, probsT_ready, pv_done, out_hi, out_lo, va2_ready, sig_ready, m_scaled, m_hi, m_lo,
         o_evac, yT_done, y_ready, dve_chain, act_chain, pool_chain, wi_ready) = [sem(s) for s in (
             "const_in consts_in x_in rows_in ptab_in pages_in out_done gains_T gains_ready scaled_gains masks_ready "
             "xT_done x_ready squares_ready ms_done root_ready rstd_ready scaled n_hi n_lo "
             "w_hi w_lo unit_done gate_scaled up_scaled silu_done pair_free prod_ready h_hi h_lo down_evac keysT_done keysT_act keysT_dve "
             "z_ready zsq_ready zg_ready zms_done zroot_ready zrstd_ready zn_ready swapped rot_ready rot_cos z_final tok_T tok_ready wexp_ps wexp_ready "
             "qz_ready qz_zero logits_done max_done soft_done idx_acc score_ps score_ready sel_ready rinv_ready "
             "probs_ready probsT_done probsT_ready pv_done out_hi out_lo va2_ready sig_ready m_scaled m_hi m_lo "
             "o_evac yT_done y_ready dve_chain act_chain pool_chain wi_ready").split()]

        LOOP_TILES, LOOP_UNITS, LOOP_PAIRS = 6, 12, 6
        G_LOOPS = FB // 2 // 3
        G_HEAD = 2
        D_LOOPS = D // TC // 2
        MS_BANK = (7, 0, 7)
        BANKS_FREE = 3
        DOWN_FREE = 3

        def landed_per_turn(n):
            return landed[n + LOOP_TILES] - landed[n]

        def index_among(u, those):
            return those.index(u)

        def sample_columns(ap, kind, s):
            order = "p (b s m t) -> p s m b t" if kind == MOBA else "p (b m s t) -> p s m b t"
            return ap.rearrange(order, b=N_SEQ, m=4, s=2, t=N_NEW)[:, s]

        def out_views(t, bank, kind, form):
            if form < 2:
                return [(t[:, :, form * P:(form + 1) * P], bank[:, :].rearrange("p (m q) -> p m q", m=4))]
            halves = [slice(s * HD, (s + 1) * HD) for s in range(2)]
            return [(t[h, :, NP_TOK:N].rearrange("p m (b t) -> p m b t", t=N_NEW),
                     sample_columns(bank[h, 0:2 * P], kind, s)) for s, h in enumerate(halves)]

        block = ctx.enter_context(nc.Block())

        @block.sync
        def _(sp):
            def load(n, it=None, turns=1):
                if n >= NR:
                    free = max(tile_split[n - NR + LOOP_TILES * i] - LOOP_UNITS * i for i in range(turns))
                    free = free if it is None else free + LOOP_UNITS * it
                    sp.wait_ge(w_hi, free)
                    sp.wait_ge(w_lo, free)
                for p0, np_, k0, nk, c0, w, name, r0, s0 in tiles[n]:
                    src = a[name][r0:r0 + nk * np_, :]
                    if it is None:
                        src = src[:, s0:s0 + w]
                    else:
                        step = tiles[n + LOOP_TILES][0][8] - tiles[n][0][8]
                        src = src[:, bass.ds(it * step + s0, w)]
                    sp.dma_start(raw[p0:p0 + np_, n % NR, k0:k0 + nk, c0:c0 + w],
                                 src.rearrange("(k p) c -> p k c", p=np_)).then_inc(raw_in[n % NR], 16)

            sp.dma_start(xtok[:, 0:2, :], a["x_prompt"].rearrange("b (t p) d -> p (b t) d", p=P)).then_inc(x_in, 16)
            sp.dma_start(xtok[0:NS_TOK, 2, :], a["x_sample"].rearrange("b t d -> (b t) d")).then_inc(x_in, 16)
            for f in (1, 2):
                g0, d0 = first[f"G{f}"][0], first[f"D{f}"][0]
                for n in range(LOOP_TILES):
                    load(g0 + n)
                with sp.Fori(0, G_LOOPS - 1) as it:
                    for n in range(LOOP_TILES):
                        load(g0 + LOOP_TILES + n, it, G_LOOPS - 1)
                for n in range(G_LOOPS * LOOP_TILES, 2 * (FB // 2)):
                    load(g0 + n)
                with sp.Fori(0, D_LOOPS) as it:
                    for n in range(LOOP_TILES):
                        load(d0 + n, it, D_LOOPS)
                if f == 1:
                    for n in range(first["P"][0], first["G2"][0]):
                        load(n)
            yp, ys = o["y_prompt"].rearrange("b (t p) d -> p (b t) d", p=P), o["y_sample"].rearrange("b t d -> (b t) d")
            for k0, k1 in ((0, 4), (4, 6), (6, KB)):
                sp.wait_ge(y_ready, k1)
                cols = slice(k0 * P, k1 * P)
                sp.dma_start(yp[:, :, cols], ytok[:, 0:2, cols]).then_inc(out_done, 16)
                sp.dma_start(ys[:, cols], ytok[0:NS_TOK, 2, cols]).then_inc(out_done, 16)
            sp.wait_ge(out_done, 16 * 16)

        @block.gpsimd
        def _(pool):
            chained = [0]

            def link(ins):
                chained[0] += 1
                ins.then_inc(pool_chain, 1)
                pool.wait_ge(pool_chain, chained[0])

            def squares(r, ready, base):
                for k in range(KB):
                    pool.wait_ge(ready, base + k + 1)
                    link(nc.gpsimd.tensor_tensor(sq_block if k else ssq, x[:, k, :], x[:, k, :], ALU.mult))
                    if k:
                        ins = nc.gpsimd.tensor_tensor(ssq, ssq, sq_block, ALU.add)
                        if k < KB - 1:
                            link(ins)
                        else:
                            ins.then_inc(squares_ready, 1)

            squares(0, x_ready, 0)
            nc.gpsimd.dma_start(ptab[:], a["page_table"].rearrange("a b -> (a b)")[None, :]).then_inc(ptab_in, 16)
            pool.wait_ge(ptab_in, 16)
            n_pool = a["cache_k_a"].shape[1]
            flat = {n: a[n].rearrange("l n p h d -> (l n) p (h d)") for n in
                    ("cache_k_a", "cache_v_a", "cache_k_b", "cache_v_b")}
            flat["cache_kidx_a"] = a["cache_kidx_a"].rearrange("l n p d -> (l n) p d")
            with pool.Fori(0, N_SEQ * NPG) as i:
                page = pool.value_load(ptab[0:1, bass.ds(i, 1)], min_val=0, max_val=n_pool - 1)
                for name, dst in (("cache_kidx_a", kraw[:, 0, bass.ds(i, 1), 0:HD]),
                                  ("cache_kidx_a", kraw[:, 0, bass.ds(i, 1), HD:P]),
                                  ("cache_k_b", kraw[:, 1, bass.ds(i, 1), :]),
                                  ("cache_k_a", kraw[:, 2, bass.ds(i, 1), 0:HD]),
                                  ("cache_k_a", kraw[:, 2, bass.ds(i, 1), HD:P]),
                                  ("cache_v_a", va_pg[:, bass.ds(i, 1), :]),
                                  ("cache_v_b", vb_pg[:, bass.ds(i, 1), :])):
                    nc.gpsimd.dma_start(dst, flat[name][bass.ds(page, 1), :, :].rearrange("o p d -> p o d"))\
                        .then_inc(pages_in, 16)

            squares(1, down_evac, DOWN_FREE)
            pool.wait_ge(keysT_done, 12)
            nc.gpsimd.memset(qz[:], 0.0).then_inc(qz_zero, 1)
            pool.wait_ge(qz_zero, 1)

            def sample_queries(kind):
                for s in range(2):
                    half = slice(s * HD, (s + 1) * HD)
                    dst = sample_columns(qz[half, kind, :], kind, s)
                    src = Q_OF[kind][half, :, NP_TOK:N].rearrange("p m (b t) -> p m b t", t=N_NEW)
                    nc.gpsimd.tensor_copy(dst, src).then_inc(qz_ready, 1)
                    pool.wait_ge(qz_ready, 2 * kind + s + 1)

            def weigh(m):
                kind, form, i = step_kind(m)
                nh, w = {1: (2, 2 * P), 0: (4, P), 2: (1, NK_S)}[form]
                pool.wait_ge(rinv_ready, m - 7)
                pool.wait_ge(soft_done, m + 1)
                pv = probs[:, m % 2, 0:nh * w].rearrange("p (h k) -> p h k", h=nh)
                r = rinv[:, 4 * m:4 * m + nh].unsqueeze(2).to_broadcast([P, nh, w])
                nc.gpsimd.tensor_tensor(pv, pv, r, ALU.mult).then_inc(probs_ready, 1)

            for u in range(U_END):
                for m in STEPS_OF_SLOT.get(u, []):
                    if 8 <= m < N_STEPS:
                        weigh(m)
                if u - 1 in NORMED:
                    i = index_among(u - 1, NORMED)
                    pool.wait_ge(zg_ready, i + 1)
                    pool.wait_ge(zrstd_ready, i + 1)
                    nc.gpsimd.tensor_tensor(zloc[u - 1], zloc[u - 1], roots[:, i % 2, :], ALU.mult).then_inc(zn_ready, 1)
                if u - 2 in ROTATED:
                    i = index_among(u - 2, ROTATED)
                    z = zloc[u - 2]
                    pool.wait_ge(swapped, i + 1)
                    nc.gpsimd.tensor_tensor(z, z, c_(C_COS, N), ALU.mult).then_inc(rot_cos, 1)
                    pool.wait_ge(rot_cos, i + 1)
                    pool.wait_ge(rot_ready, i + 1)
                    nc.gpsimd.tensor_tensor(z, z, rot_tmp[:, i % 2, :], ALU.add).then_inc(z_final, 1)
                    if u - 2 in LAST_QUERY:
                        pool.wait_ge(z_final, i + 1)
                        sample_queries(LAST_QUERY[u - 2])
                if u == WCOL_SLOT:
                    pool.wait_ge(tok_ready, 3)
                    for s in range(2):
                        nc.gpsimd.tensor_copy(va2[:, s * HD:(s + 1) * HD], tok[0:NS_TOK, 2, 384:448]).then_inc(va2_ready, 1)
                        pool.wait_ge(va2_ready, s + 1)
            squares(2, o_evac, 0)

        @block.scalar
        def _(act):
            act.dma_start(cst[:, 0:P], a["constants"][:, 0:P]).then_inc(const_in, 16)
            for name, at in (("ffn1_norm", 0), ("mix_norm", 8), ("ffn2_norm", 16)):
                act.dma_start(rows[at:at + 8, :], a[name].rearrange("l (k p) -> (l k) p", p=P)).then_inc(rows_in, 16)
            act.dma_start(rows[24:40, :], a["gate_bias"].rearrange("l (k p) -> (l k) p", p=P)).then_inc(rows_in, 16)
            for i, name in enumerate(("q_norm_a", "k_norm_a", "q_norm_b", "k_norm_b")):
                for s in range(2):
                    act.dma_start(rows[40 + i:41 + i, s * HD:(s + 1) * HD], a[name]).then_inc(rows_in, 16)
            act.wait_ge(raw_in[0], 16)
            act.dma_start(cst[:, P:], a["constants"][:, P:]).then_inc(consts_in, 16)

            def split_hi(v, it=0):
                n, c0, w, nk = units[v]
                step = 0 if isinstance(it, int) else landed_per_turn(n)
                act.wait_ge(raw_in[n % NR], landed[n] + step * it)
                if v >= NU:
                    act.wait_ge(unit_done, v - NU + 1 + LOOP_UNITS * it)
                nc.scalar.activation(whi[:, v % NU, 0:nk, 0:w], raw[:, n % NR, 0:nk, c0:c0 + w], ACT.Copy)\
                    .then_inc(w_hi, 1)

            def root(r):
                act.wait_ge(ms_done, r + 1)
                nc.scalar.activation(rms, ps[MS_BANK[r]][:, 0:N], ACT.Sqrt, bias=eps_col[:, 0:1]).then_inc(root_ready, 1)

            def norm_hi(r, k, it=0):
                act.wait_ge(scaled, KB * r + k + 1 + 4 * it)
                at = slice(k, k + 1) if isinstance(it, int) else bass.ds(4 * it + k, 1)
                nc.scalar.activation(nhi[:, at, :], tmp[:, k % 2, :, :], ACT.Copy).then_inc(n_hi, 1)

            for k in range(KB + 1):
                if k < KB:
                    act.wait_ge(xT_done, k + 1)
                    nc.scalar.activation(x[:, k, :], ps[4 + k % 4][:, 0:N], ACT.Copy).then_inc(x_ready, 1)
                if k:
                    norm_hi(0, k - 1)
                if k < AHEAD:
                    split_hi(k)
            act.wait_ge(masks_ready, 1)

            def pair(f, p, it=0):
                v = first[f"G{f}"][1] + 2 * p + 1
                gp = (f - 1) * FB + p
                w = units[v][2]
                if p == 0:
                    split_hi(v - 1 + AHEAD)
                    split_hi(v + AHEAD)
                    root(0 if f == 1 else 2)
                act.wait_ge(gate_scaled, gp + 1 + LOOP_PAIRS * it)
                nc.scalar.activation(act_tmp[0:w, p % 2, 0, :], act_tmp[0:w, p % 2, 0, :], ACT.Silu).then_inc(silu_done, 1)
                if p:
                    split_hi(v - 1 + AHEAD, it)
                    split_hi(v + AHEAD, it)
                act.wait_ge(prod_ready, gp + 1 + LOOP_PAIRS * it)
                at = slice(p, p + 1) if isinstance(it, int) else bass.ds(LOOP_PAIRS * it + p, 1)
                nc.scalar.activation(hhi[0:w, at, :], tmp[0:w, p % 2, :, :], ACT.Copy).then_inc(h_hi, 1)

            def gate_up(f):
                for p in range(G_HEAD):
                    pair(f, p)
                with act.Fori(0, G_LOOPS) as it:
                    for p in range(G_HEAD, G_HEAD + LOOP_PAIRS):
                        pair(f, p, it)
                for p in range(G_HEAD + G_LOOPS * LOOP_PAIRS, FB):
                    pair(f, p)

            def down_turn(it):
                v0 = first["D1"][1]
                for j in range(LOOP_UNITS):
                    if j % 6 >= 4:
                        norm_hi(1, 2 * (j // 6) + j % 6 - 4, it)
                    split_hi(v0 + j + AHEAD, it)

            gate_up(1)
            with act.Fori(0, D_LOOPS) as it:
                down_turn(it)
            for g in range(0, 12, 2):
                act.wait_ge(keysT_done, g + 1)
                dst = kt[:, g // 4, :, :].rearrange("p b k -> p (b k)")[:, (g % 4) * 512:(g % 4 + 1) * 512]
                nc.scalar.activation(dst, ps[1 + g % 3][:, :], ACT.Copy).then_inc(keysT_act, 1)

            vp = first["P"][1]

            def attend(m):
                if m < N_STEPS:
                    kind, form, i = step_kind(m)
                    nh, w = {1: (2, 2 * P), 0: (4, P), 2: (1, NK_S)}[form]
                    if m >= 2:
                        k2, f2, i2 = step_kind(m - 2)
                        if k2 != IDX:
                            act.wait_ge(probsT_done, m - 2 - 8 + 1)
                        elif f2 != 2:
                            act.wait_ge(idx_acc, m - 2 + 1)
                        else:
                            act.wait_ge(score_ps, i2 + 1)
                    act.wait_ge(logits_done, m + 1)
                    if kind == IDX:
                        nc.scalar.activation(probs[:, m % 2, 0:nh * w], ps[m % 2][:, 0:nh * w], ACT.Relu).then_inc(soft_done, 1)
                    else:
                        act.wait_ge(max_done, m - 7)
                        for h in range(nh):
                            ins = nc.scalar.activation(probs[:, m % 2, h * w:(h + 1) * w], ps[m % 2][:, h * w:(h + 1) * w],
                                                       ACT.Exp, bias=nmax[:, 4 * m + h:4 * m + h + 1],
                                                       accum_out=rsum[:, 4 * m + h:4 * m + h + 1])
                        ins.then_inc(soft_done, 1)
                if 8 <= m - 1 < N_STEPS:
                    n = m - 1 - 8
                    act.wait_ge(probsT_done, n + 1)
                    if n >= 2:
                        act.wait_ge(pv_done, n - 1)
                    if step_kind(m - 1)[1] == 2:
                        nc.scalar.activation(probsT[:, n % 2, 0:256], ps[2 + n % 2][:, 0:256], ACT.Copy)
                        nc.scalar.activation(probsT[0:NS_TOK, n % 2, 256:384], ps[2 + n % 2][0:NS_TOK, 256:384],
                                             ACT.Copy).then_inc(probsT_ready, 1)
                    else:
                        nc.scalar.activation(probsT[:, n % 2, :], ps[2 + n % 2][:, :], ACT.Copy).then_inc(probsT_ready, 1)
                if 8 <= m - 2 < N_STEPS and out_group(m - 2)[1]:
                    g = out_group(m - 2)[0]
                    kind, form, _ = step_kind(m - 2)
                    act.wait_ge(pv_done, m - 2 - 8 + 1)
                    dst_t = bhi if kind == MOBA else ahi
                    for dst, src in out_views(dst_t, ps[5 - g % 2], kind, form):
                        ins = nc.scalar.activation(dst, src, ACT.Copy)
                    ins.then_inc(out_hi, 1)

            for u in range(U_END):
                for m in STEPS_OF_SLOT.get(u, []):
                    attend(m)
                if u in NORMED:
                    i = index_among(u, NORMED)
                    z = zloc[u]
                    act.wait_ge(z_ready, u + 1)
                    if i >= 2:
                        act.wait_ge(zms_done, i - 1)
                    nc.scalar.activation(act_tmp[:, i % 2, 0, :], z, ACT.Square).then_inc(zsq_ready, 1)
                    act.wait_ge(zsq_ready, i + 1)
                    nc.scalar.activation(z, z, ACT.Copy, scale=gains[:, GAIN_OF[u]:GAIN_OF[u] + 1]).then_inc(zg_ready, 1)
                if u - 1 in NORMED:
                    i = index_among(u - 1, NORMED)
                    act.wait_ge(zms_done, i + 1)
                    if i >= 2:
                        act.wait_ge(zn_ready, i - 1)
                    nc.scalar.activation(roots[:, i % 2, :], ps[5][:, 0:N], ACT.Sqrt, bias=eps_col[:, 0:1]).then_inc(zroot_ready, 1)
                split_hi(vp + u + AHEAD)
                if u == 0:
                    root(1)
                if u == TOK_SLOT:
                    for t in range(3):
                        r = P if t < 2 else NS_TOK
                        act.wait_ge(tok_T, t + 1)
                        nc.scalar.activation(tok[0:r, t, :], ps[(2, 3, 0)[t]][0:r, 0:456], ACT.Copy).then_inc(tok_ready, 1)
                    act.wait_ge(tok_ready, 3)
                    for name, c0, w in (("k_a", 0, 64), ("kidx", 64, 64), ("k_b", 128, 128), ("v_b", 256, 128), ("v_a", 384, 64)):
                        act.dma_start(o[f"new_{name}_p"], tok[:, 0:2, c0:c0 + w]).then_inc(out_done, 16)
                        act.dma_start(o[f"new_{name}_s"], tok[0:NS_TOK, 2, c0:c0 + w]).then_inc(out_done, 16)
            for m in STEPS_AFTER:
                attend(m)
            vu = first["U"][1]
            act.wait_ge(z_ready, U_END)

            def gate(j):
                for b in (j, 8 + j):
                    nc.scalar.activation(gates[:, b, :], gates[:, b, :], ACT.Sigmoid,
                                         bias=gains[:, 24 + b:25 + b]).then_inc(sig_ready, 1)

            gate(0)
            for j in range(8):
                if j < 7:
                    gate(j + 1)
                split_hi(vu + j + AHEAD)
                act.wait_ge(m_scaled, j + 1)
                nc.scalar.activation(mhi[:, j, :], tmp[:, j % 2, 0, :], ACT.Copy).then_inc(m_hi, 1)
            vo = first["O"][1]
            for j in range(8):
                split_hi(vo + j + AHEAD)
                norm_hi(2, j)
            gate_up(2)
            vd = first["D2"][1]
            for j in range(2 * LOOP_UNITS):
                if vd + j + AHEAD < len(units):
                    split_hi(vd + j + AHEAD)

        @block.vector
        def _(dve):
            chained = [0]

            def link(ins):
                chained[0] += 1
                ins.then_inc(dve_chain, 1)
                dve.wait_ge(dve_chain, chained[0])

            def split_lo(v, it=0):
                n, c0, w, nk = units[v]
                dve.wait_ge(w_hi, v + 1 + LOOP_UNITS * it)
                nc.vector.tensor_tensor(wlo[:, v % NU, 0:nk, 0:w], raw[:, n % NR, 0:nk, c0:c0 + w],
                                        whi[:, v % NU, 0:nk, 0:w].bitcast(F32), ALU.subtract).then_inc(w_lo, 1)

            nc.vector.memset(eps_col[:, 0:1], EPS).then_inc(masks_ready, 1)
            nc.vector.memset(eps_col[:, 1:2], 0.0).then_inc(pair_free, BANKS_FREE)
            nc.vector.memset(eps_col[:, 2:3], 0.0).then_inc(down_evac, DOWN_FREE)
            dve.wait_ge(gains_T, 1)
            nc.vector.tensor_copy(gains[:], ps[0][:, 0:GAIN_ROWS]).then_inc(gains_ready, 1)
            dve.wait_ge(gains_ready, 1)
            for c in (40, 42):
                nc.vector.tensor_scalar(gains[:, c:c + 1], gains[:, c:c + 1], HD ** -0.5, None, ALU.mult).then_inc(scaled_gains, 1)

            def scale(r, k, ready, base, it=0):
                dve.wait_ge(ready, base + k + 1 + 4 * it)
                if isinstance(it, int):
                    at, g = slice(k, k + 1), slice(8 * r + k, 8 * r + k + 1)
                    if k >= 2:
                        dve.wait_ge(n_lo, KB * r + k - 1)
                else:
                    at, g = bass.ds(4 * it + k, 1), bass.ds(4 * it + 8 * r + k, 1)
                    dve.wait_ge(n_lo, KB * r + k - 1 + 4 * it)
                nc.vector.tensor_scalar(tmp[:, k % 2, :, :], x[:, at, :], gains[:, g], None, ALU.mult).then_inc(scaled, 1)

            def norm_lo(r, k, it=0):
                dve.wait_ge(n_hi, KB * r + k + 1 + 4 * it)
                at = slice(k, k + 1) if isinstance(it, int) else bass.ds(4 * it + k, 1)
                nc.vector.tensor_tensor(nlo[:, at, :], tmp[:, k % 2, :, :], nhi[:, at, :].bitcast(F32),
                                        ALU.subtract).then_inc(n_lo, 1)

            def inverse_rms(r):
                dve.wait_ge(root_ready, r + 1)
                link(nc.vector.reciprocal(rstd[:], rms))

            for k in range(KB + 1):
                if k < KB:
                    scale(0, k, x_ready, 0)
                if k:
                    norm_lo(0, k - 1)
                    if k <= AHEAD:
                        split_lo(k - 1)
            dve.wait_ge(consts_in, 16)
            nc.vector.tensor_copy(idb[:], c_(C_ID, P)).then_inc(masks_ready, 1)
            nc.vector.tensor_copy(causalb[:], c_(C_CAUSAL, 2 * P)).then_inc(masks_ready, 1)

            def pair(f, p, it=0):
                v = first[f"G{f}"][1] + 2 * p + 1
                gp = (f - 1) * FB + p
                w = units[v][2]
                if p == 0:
                    split_lo(v - 1 + AHEAD)
                    split_lo(v + AHEAD)
                    inverse_rms(0 if f == 1 else 2)
                dve.wait_ge(unit_done, v + 1 + LOOP_UNITS * it)
                nc.vector.tensor_tensor(act_tmp[0:w, p % 2, 0, :], ps[2 * (p % 3)][0:w, 0:N], rstd[0:w, :],
                                        ALU.mult).then_inc(gate_scaled, 1)
                if gp >= 2:
                    dve.wait_ge(h_lo, gp - 1 + LOOP_PAIRS * it)
                nc.vector.tensor_tensor(tmp[0:w, p % 2, 0, :], ps[2 * (p % 3) + 1][0:w, 0:N], rstd[0:w, :],
                                        ALU.mult).then_inc(pair_free, 1)
                if p:
                    split_lo(v - 1 + AHEAD, it)
                dve.wait_ge(silu_done, gp + 1 + LOOP_PAIRS * it)
                dve.wait_ge(pair_free, gp + 1 + BANKS_FREE + LOOP_PAIRS * it)
                nc.vector.tensor_tensor(tmp[0:w, p % 2, 0, :], act_tmp[0:w, p % 2, 0, :], tmp[0:w, p % 2, 0, :],
                                        ALU.mult).then_inc(prod_ready, 1)
                if p:
                    split_lo(v + AHEAD, it)
                dve.wait_ge(h_hi, gp + 1 + LOOP_PAIRS * it)
                at = slice(p, p + 1) if isinstance(it, int) else bass.ds(LOOP_PAIRS * it + p, 1)
                nc.vector.tensor_tensor(hlo[0:w, at, :], tmp[0:w, p % 2, :, :], hhi[0:w, at, :].bitcast(F32),
                                        ALU.subtract).then_inc(h_lo, 1)

            def gate_up(f):
                for p in range(G_HEAD):
                    pair(f, p)
                with dve.Fori(0, G_LOOPS) as it:
                    for p in range(G_HEAD, G_HEAD + LOOP_PAIRS):
                        pair(f, p, it)
                for p in range(G_HEAD + G_LOOPS * LOOP_PAIRS, FB):
                    pair(f, p)

            def down_turn(f, it, q0=0):
                v0 = first[f"D{f}"][1] + 6 * q0
                for j in range(LOOP_UNITS):
                    q, i = divmod(j, 6)
                    if i >= 4:
                        m = i - 4
                        dve.wait_ge(unit_done, v0 + j + 1 + LOOP_UNITS * it)
                        k = 2 * (q0 + q) + m
                        xk = x[:, k:k + 1, :] if isinstance(it, int) else x[:, bass.ds(4 * it + k, 1), :]
                        bank = ps[(6, 4)[q % 2] + m]
                        nc.vector.scalar_tensor_tensor(xk, bank[:, 0:N].unsqueeze(1), 0.5, xk, ALU.mult, ALU.add)\
                            .then_inc(down_evac, 1)
                        if f == 1:
                            scale(1, k, down_evac, DOWN_FREE, it)
                    if v0 + j + AHEAD < len(units):
                        split_lo(v0 + j + AHEAD, it)
                    if f == 1 and i >= 4:
                        norm_lo(1, k, it)

            gate_up(1)
            with dve.Fori(0, D_LOOPS) as it:
                down_turn(1, it)
            for g in range(1, 12, 2):
                dve.wait_ge(keysT_done, g + 1)
                dst = kt[:, g // 4, :, :].rearrange("p b k -> p (b k)")[:, (g % 4) * 512:(g % 4 + 1) * 512]
                nc.vector.tensor_copy(dst, ps[1 + g % 3][:, :]).then_inc(keysT_dve, 1)
            nc.vector.tensor_copy(masksb[:], c_(C_MASKS, NK_S, NS_TOK)).then_inc(masks_ready, 1)
            nc.vector.tensor_copy(expb[:], c_(C_EXP, 2 * P, NS_TOK)).then_inc(masks_ready, 1)

            vp = first["P"][1]

            def top_k(work, rounds, final, mask, kind_final):
                r = work.shape[0]

                def one_round(n):
                    link(nc.vector.max(best[0:r, :], work[:]))
                    if n == rounds - 1 and kind_final:
                        link(nc.vector.memset(best[0:r, kind_final:8], TAKEN))
                    link(nc.vector.match_replace(work[:], best[0:r, :], work[:], TAKEN))

                def finish():
                    link(nc.vector.tensor_scalar(work[:], work[:], TAKEN_LIMIT, NEG, ALU.is_gt, ALU.mult))
                    nc.vector.tensor_tensor(final[:], work[:], mask, ALU.add).then_inc(sel_ready, 1)

                return [lambda n=n: one_round(n) for n in range(rounds)] + [finish]

            chores = (top_k(acc1, TOPK_PROMPT // 8, sel1, c_(C_CAUSAL, 2 * P), 0)
                      + top_k(acc0, TOPK_PROMPT // 8, sel0, c_(C_CAUSAL + P, P), 0)
                      + top_k(acc_s, -(-TOPK_SAMPLE // 8), sel_s, c_(C_MASKS, NK_S, NS_TOK), TOPK_SAMPLE % 8))

            def attend(m):
                if 8 <= m < N_STEPS:
                    kind, form, i = step_kind(m)
                    nh, w = {1: (2, 2 * P), 0: (4, P), 2: (1, NK_S)}[form]
                    dve.wait_ge(logits_done, m + 1)
                    nc.vector.tensor_reduce(nmax[:, 4 * m:4 * m + nh], ps[m % 2][:, 0:nh * w].rearrange("p (h k) -> p h k", h=nh),
                                            AX, ALU.max, negate=True).then_inc(max_done, 1)
                if m == 8:
                    dve.wait_ge(score_ps, 2)
                    nc.vector.tensor_tensor(acc_s[:], ps[3][0:NS_TOK, 0:NK_S], c_(C_MASKS, NK_S, NS_TOK), ALU.add)\
                        .then_inc(score_ready, 1)
                    dve.wait_ge(score_ready, 1)
                if 8 <= m - 2 < N_STEPS and out_group(m - 2)[1]:
                    g = out_group(m - 2)[0]
                    kind, form, _ = step_kind(m - 2)
                    dve.wait_ge(out_hi, g + 1)
                    lo_t, hi_t = (blo, bhi) if kind == MOBA else (alo, ahi)
                    for (dst, src), (hi, _) in zip(out_views(lo_t, ps[5 - g % 2], kind, form),
                                                   out_views(hi_t, ps[5 - g % 2], kind, form)):
                        ins = nc.vector.tensor_tensor(dst, src, hi.bitcast(F32), ALU.subtract)
                    ins.then_inc(out_lo, 1)

            def attend_late(m):
                if m < 6:
                    kind, form, i = step_kind(m)
                    half, blocks, w = step_heads(form, i)
                    acc = acc1 if form == 1 else acc0
                    mask = c_(C_CAUSAL, 2 * P) if form == 1 else c_(C_CAUSAL + P, P)
                    dve.wait_ge(soft_done, m + 1)
                    for j, b in enumerate(blocks):
                        h = 2 * b + half
                        ins = nc.vector.scalar_tensor_tensor(
                            acc[:], probs[:, m % 2, j * w:(j + 1) * w], wi_p[:, form, h:h + 1],
                            mask if i == 0 and j == 0 else acc[:], ALU.mult, ALU.add)
                        if j == len(blocks) - 1:
                            ins.then_inc(idx_acc, 1)
                            dve.wait_ge(idx_acc, m + 1)
                        else:
                            link(ins)
                if 8 <= m < N_STEPS:
                    nh = {1: 2, 0: 4, 2: 1}[step_kind(m)[1]]
                    dve.wait_ge(soft_done, m + 1)
                    nc.vector.reciprocal(rinv[:, 4 * m:4 * m + nh], rsum[:, 4 * m:4 * m + nh]).then_inc(rinv_ready, 1)
            for u in range(U_END):
                for m in STEPS_OF_SLOT.get(u, []):
                    attend(m)
                for m in STEPS_OF_SLOT.get(u, []):
                    attend_late(m)
                if u >= CHORE_SLOT:
                    for _ in range(CHORES_PER_SLOT):
                        if chores:
                            chores.pop(0)()
                if u == 0:
                    split_lo(vp + AHEAD)
                    inverse_rms(1)
                dve.wait_ge(unit_done, vp + u + 1)
                bank = ps[6 + u % 2]
                if u < U_GATE:
                    w = units[vp + u][2]
                    nc.vector.tensor_tensor(zloc[u][0:w], bank[0:w, 0:N], rstd[0:w, :], ALU.mult).then_inc(z_ready, 1)
                else:
                    nc.vector.tensor_tensor(gates[:, u - U_GATE, :], bank[:, 0:N], rstd[:], ALU.mult).then_inc(z_ready, 1)
                if u - 1 in NORMED:
                    i = index_among(u - 1, NORMED)
                    dve.wait_ge(zroot_ready, i + 1)
                    nc.vector.reciprocal(roots[:, i % 2, :], roots[:, i % 2, :]).then_inc(zrstd_ready, 1)
                if u - 2 in ROTATED:
                    i = index_among(u - 2, ROTATED)
                    dve.wait_ge(swapped, i + 1)
                    if i >= 2:
                        dve.wait_ge(z_final, i - 1)
                    nc.vector.tensor_tensor(rot_tmp[:, i % 2, :], ps[4][:, 0:N], c_(C_SIN, N), ALU.mult).then_inc(rot_ready, 1)
                if u:
                    split_lo(vp + u + AHEAD)
                if u == WCOL_SLOT:
                    dve.wait_ge(tok_ready, 3)
                    nc.vector.tensor_scalar(wi_p[:], tok[:, 0:2, 448:456], HEADS ** -0.5, HD ** -0.5,
                                            ALU.mult, ALU.mult).then_inc(wi_ready, 1)
                    dve.wait_ge(wi_ready, 1)
                    dve.wait_ge(wexp_ps, 1)
                    hs = c_(C_HSEL, HEADS).unsqueeze(1).to_broadcast([P, 2, HEADS])
                    link(nc.vector.tensor_tensor(wsel[:], ps[3][:, 0:2 * HEADS].rearrange("p (g h) -> p g h", g=2), hs, ALU.mult))
                    link(nc.vector.tensor_reduce(wcol[:], wsel[:], AX, ALU.add))
                    link(nc.vector.tensor_scalar(wcol[:], wcol[:], HEADS ** -0.5, HD ** -0.5, ALU.mult, ALU.mult))
                    for g in range(2):
                        nc.vector.tensor_scalar(wexp[:, g, :], c_(C_EXPT + g * NS_TOK, NS_TOK), wcol[:, g:g + 1], None,
                                                ALU.mult).then_inc(wexp_ready, 1)
            for m in STEPS_AFTER:
                attend(m)
                attend_late(m)
            assert not chores

            vu = first["U"][1]

            def merged_lo(j):
                dve.wait_ge(m_hi, j + 1)
                nc.vector.tensor_tensor(mlo[:, j, :], tmp[:, j % 2, 0, :], mhi[:, j, :].bitcast(F32), ALU.subtract).then_inc(m_lo, 1)

            for j in range(8):
                dve.wait_ge(unit_done, vu + j + 1)
                dve.wait_ge(sig_ready, 2 * j + 2)
                ba, bb = (ps[6], ps[7]) if j % 2 == 0 else (ps[0], ps[1])
                nc.vector.tensor_tensor(gates[:, j, :], gates[:, j, :], ba[:, 0:N], ALU.mult)
                link(nc.vector.tensor_tensor(gates[:, 8 + j, :], gates[:, 8 + j, :], bb[:, 0:N], ALU.mult))
                nc.vector.tensor_tensor(tmp[:, j % 2, 0, :], gates[:, j, :], gates[:, 8 + j, :], ALU.add).then_inc(m_scaled, 1)
                split_lo(vu + j + AHEAD)
                merged_lo(j)
            vo = first["O"][1]
            for j in range(8):
                dve.wait_ge(unit_done, vo + j + 1)
                nc.vector.tensor_tensor(x[:, j, :], ps[2 + j % 2][:, 0:N], x[:, j, :], ALU.add).then_inc(o_evac, 1)
                scale(2, j, o_evac, 0)
                split_lo(vo + j + AHEAD)
                norm_lo(2, j)
            gate_up(2)

            def y_out(k):
                dve.wait_ge(yT_done, k + 1)
                bank = ps[k % 2]
                nc.vector.tensor_copy(ytok[:, 0:2, k * P:(k + 1) * P], bank[:, 0:2 * P].rearrange("p (t c) -> p t c", t=2))
                nc.vector.tensor_copy(ytok[0:NS_TOK, 2, k * P:(k + 1) * P], bank[0:NS_TOK, 2 * P:3 * P]).then_inc(y_ready, 1)

            for turn in range(D_LOOPS):
                down_turn(2, 0, 2 * turn)
                if turn == 0:
                    for k in range(2):
                        y_out(k)
            for k in range(2, KB):
                y_out(k)

        @block.tensor
        def _(pe):
            def unit(v, out, xs, it=0, kl=None, start=True, stop=True, wait_x=None, done=True):
                n, c0, w, nk = units[v]
                pe.wait_ge(w_lo, v + 1 + LOOP_UNITS * it)
                ks = range(nk) if kl is None else kl
                for i, k in enumerate(ks):
                    if wait_x:
                        wait_x(k)
                    hi, lo, r = xs(k)
                    h, l = whi[0:r, v % NU, k, 0:w], wlo[0:r, v % NU, k, 0:w]
                    nc.tensor.matmul(out[0:w, 0:N], h, hi, start=start and i == 0, stop=False)
                    nc.tensor.matmul(out[0:w, 0:N], h, lo, start=False, stop=False)
                    ins = nc.tensor.matmul(out[0:w, 0:N], l, hi, start=False, stop=stop and i == len(ks) - 1)
                if done:
                    ins.then_inc(unit_done, 1)

            ident = c_(C_ID, P)
            pe.wait_ge(const_in, 16)
            pe.wait_ge(rows_in, 16 * 12)
            nc.tensor.transpose(ps[0][:, 0:GAIN_ROWS], rows[:], cst[0:GAIN_ROWS, C_ID:C_ID + GAIN_ROWS]).then_inc(gains_T, 1)
            pe.wait_ge(x_in, 32)
            for k in range(KB):
                if k >= 4:
                    pe.wait_ge(x_ready, k - 3)
                for t in range(3):
                    r = P if t < 2 else NS_TOK
                    ins = nc.tensor.transpose(ps[4 + k % 4][:, t * P:t * P + r], xtok[0:r, t, k * P:(k + 1) * P],
                                              cst[0:r, C_ID:C_ID + r])
                ins.then_inc(xT_done, 1)

            def mean_square(r):
                if r == 0:
                    pe.wait_ge(consts_in, 16)
                pe.wait_ge(squares_ready, r + 1)
                nc.tensor.matmul(ps[MS_BANK[r]][:, 0:N], c_(C_ONE, P), ssq, start=True, stop=True).then_inc(ms_done, 1)

            normed = lambda k: (nhi[:, k, :], nlo[:, k, :], P)

            def pair(f, p, it=0, r=None):
                v = first[f"G{f}"][1] + 2 * p
                pe.wait_ge(pair_free, (f - 1) * FB + p + 1 + LOOP_PAIRS * it)
                for g in range(2):
                    wait_x = (lambda k: pe.wait_ge(n_lo, KB * r + k + 1)) if r is not None and g == 0 else None
                    unit(v + g, ps[2 * (p % 3) + g], normed, it, wait_x=wait_x)

            def gate_up(f, r):
                for p in range(G_HEAD):
                    pair(f, p, r=r if p == 0 else None)
                mean_square(r)
                with pe.Fori(0, G_LOOPS) as it:
                    for p in range(G_HEAD, G_HEAD + LOOP_PAIRS):
                        pair(f, p, it)
                for p in range(G_HEAD + G_LOOPS * LOOP_PAIRS, FB):
                    pair(f, p)

            def down_turn(f, it, q0=0, between=None):
                v = first[f"D{f}"][1] + 6 * q0
                for q in range(2):
                    pe.wait_ge(down_evac, KB * (f - 1) + 2 * (q0 + q) + DOWN_FREE - 2 + 4 * it)
                    for t in range(3):
                        pe.wait_ge(h_lo, (f - 1) * FB + min(FB, KB * (t + 1)))
                        for m in range(2):
                            xs = lambda k, t=t: (hhi[0:FTAIL if KB * t + k == FB - 1 else P, KB * t + k, :],
                                                 hlo[0:FTAIL if KB * t + k == FB - 1 else P, KB * t + k, :],
                                                 FTAIL if KB * t + k == FB - 1 else P)
                            unit(v + 6 * q + 2 * t + m, ps[(6, 4)[q] + m], xs, it, start=t == 0, stop=t == 2)
                    if between:
                        between(q0 + q)

            gate_up(1, 0)
            with pe.Fori(0, D_LOOPS) as it:
                down_turn(1, it)

            pe.wait_ge(pages_in, 16 * 7 * N_SEQ * NPG)
            for g in range(12):
                if g >= 3:
                    pe.wait_ge((keysT_act, keysT_dve)[(g - 3) % 2], (g - 3) // 2 + 1)
                for j in range(4):
                    ins = nc.tensor.transpose(ps[1 + g % 3][:, j * P:(j + 1) * P], kraw[:, g // 4, (g % 4) * 4 + j, :], ident)
                ins.then_inc(keysT_done, 1)

            def attend(m):
                if m < N_STEPS:
                    kind, form, i = step_kind(m)
                    bank = ps[m % 2]
                    if m >= 2:
                        pe.wait_ge(soft_done, m - 1)
                    if m == 0:
                        pe.wait_ge(tok_ready, 3)
                    if i == 0 and form == 1:
                        pe.wait_ge(z_final, index_among({IDX: U_KI, MOBA: U_QB + 3, DSA: U_QA + 3}[kind], ROTATED) + 1)
                    if form == 2 and i == 0:
                        pe.wait_ge(qz_ready, 2 * (kind + 1))
                        pe.wait_ge(keysT_act, 6)
                        pe.wait_ge(keysT_dve, 6)
                    if m == 8:
                        pe.wait_ge(masks_ready, 5)
                    if kind == DSA and i == 0:
                        pe.wait_ge(sel_ready, {1: 1, 0: 2, 2: 3}[form])
                    k_new = K_OF[kind]
                    if form == 2:
                        if kind != IDX:
                            nc.tensor.matmul(bank[:, 0:NK_S], expb[:, i * P:(i + 1) * P],
                                             masksb[:] if kind == MOBA else sel_s[:], start=True, stop=False)
                        for b in range(4):
                            s = 4 * i + b
                            nc.tensor.matmul(bank[32 * b:32 * b + 32, 0:PAST], qz[:, kind, 32 * s:32 * s + 32],
                                             kt[:, KT_OF[kind], s, :], start=kind == IDX, stop=kind == IDX)
                        ins = nc.tensor.matmul(bank[:, PAST:NK_S], qz[:, kind, i * P:(i + 1) * P], k_new[:, NP_TOK:N],
                                               start=kind == IDX, stop=True)
                    else:
                        half, blocks, w = step_heads(form, i)
                        if kind != IDX:
                            mask = ((causalb[:] if kind == MOBA else sel1[:]) if form == 1
                                    else (causalb[:, P:2 * P] if kind == MOBA else sel0[:]))
                            nh = len(blocks)
                            nc.tensor.matmul(bank[:, :].rearrange("p (h k) -> p h k", h=nh), idb[:],
                                             mask.unsqueeze(1).to_broadcast([P, nh, w]), start=True, stop=False)
                        rows_ = slice(half * HD, (half + 1) * HD)
                        for j, b in enumerate(blocks):
                            ins = nc.tensor.matmul(bank[:, j * w:(j + 1) * w], Q_OF[kind][rows_, b, form * P:(form + 1) * P],
                                                   k_new[rows_, 0:w], start=kind == IDX,
                                                   stop=kind == IDX or j == len(blocks) - 1)
                    ins.then_inc(logits_done, 1)
                if m - 1 in (6, 7):
                    g = m - 1 - 6
                    pe.wait_ge(soft_done, m)
                    pe.wait_ge(wexp_ready, 2)
                    nc.tensor.matmul(ps[3][0:NS_TOK, 0:NK_S], wexp[:, g, :], probs[:, (m - 1) % 2, 0:NK_S],
                                     start=g == 0, stop=g == 1).then_inc(score_ps, 1)
                if 8 <= m - 1 < N_STEPS:
                    n = m - 1 - 8
                    form = step_kind(m - 1)[1]
                    pr = probs[:, (m - 1) % 2, :]
                    pe.wait_ge(probs_ready, n + 1)
                    if n >= 2:
                        pe.wait_ge(probsT_ready, n - 1)
                    if n == 1:
                        pe.wait_ge(score_ready, 1)
                    bank = ps[2 + n % 2]
                    if form == 2:
                        for j in range(2):
                            nc.tensor.transpose(bank[:, j * P:(j + 1) * P], pr[:, j * P:(j + 1) * P], ident)
                        ins = nc.tensor.transpose(bank[0:NS_TOK, 2 * P:3 * P], pr[:, PAST:NK_S], ident)
                    else:
                        for j in range(4):
                            ins = nc.tensor.transpose(bank[:, j * P:(j + 1) * P], pr[:, j * P:(j + 1) * P], ident)
                    ins.then_inc(probsT_done, 1)
                if 8 <= m - 2 < N_STEPS:
                    n = m - 2 - 8
                    kind, form, i = step_kind(m - 2)
                    g, _ = out_group(m - 2)
                    bank = ps[5 - g % 2]
                    pe.wait_ge(probsT_ready, n + 1)
                    if i == 0 and g >= 2:
                        pe.wait_ge(out_lo, g - 1)
                    if n == 0:
                        pe.wait_ge(zroot_ready, len(NORMED))
                    if g == 1 and i == 0:
                        pe.wait_ge(rot_ready, len(ROTATED))
                    pT = probsT[:, n % 2, :]
                    if form == 2:
                        if kind == DSA and i == 0:
                            pe.wait_ge(va2_ready, 2)
                        v_new = va2[:, :] if kind == DSA else tok[0:NS_TOK, 2, 256:384]
                        cols = slice(i * P, (i + 1) * P)
                        nc.tensor.matmul(bank[:, cols], v_new, pT[0:NS_TOK, 2 * P:3 * P], start=True, stop=False)
                        for b in range(4):
                            for j in range(NPG):
                                pg = (4 * i + b) * NPG + j
                                last = b == 3 and j == NPG - 1
                                rhs = pT[:, j * P + 32 * b:j * P + 32 * b + 32]
                                dst = slice(i * P + 32 * b, i * P + 32 * b + 32)
                                if kind == MOBA:
                                    ins = nc.tensor.matmul(bank[:, dst], vb_pg[:, pg, :], rhs, start=False, stop=last)
                                else:
                                    for s in range(2):
                                        ins = nc.tensor.matmul(bank[s * HD:(s + 1) * HD, dst], va_pg[:, pg, :], rhs,
                                                               start=False, stop=last)
                    else:
                        half, blocks, w = step_heads(form, i)
                        vc = 384 if kind == DSA else 256 + half * HD
                        for j, b in enumerate(blocks):
                            for t in range(w // P):
                                ins = nc.tensor.matmul(bank[half * HD:(half + 1) * HD, b * P:(b + 1) * P],
                                                       tok[:, t, vc:vc + HD], pT[:, (j * (w // P) + t) * P:(j * (w // P) + t + 1) * P],
                                                       start=t == 0, stop=t == w // P - 1)
                    ins.then_inc(pv_done, 1)

            vp = first["P"][1]
            for u in range(U_END):
                for m in STEPS_OF_SLOT.get(u, []):
                    attend(m)
                if u >= 2:
                    pe.wait_ge(z_ready, u - 1)
                wait_x = (lambda k: pe.wait_ge(n_lo, KB + k + 1)) if u == 0 else None
                unit(vp + u, ps[6 + u % 2], normed, wait_x=wait_x)
                if u == 0:
                    mean_square(1)
                if u - 1 in NORMED:
                    i = index_among(u - 1, NORMED)
                    pe.wait_ge(zsq_ready, i + 1)
                    if i:
                        pe.wait_ge(zroot_ready, i)
                    nc.tensor.matmul(ps[5][:, 0:N], c_(C_BLK, P), act_tmp[:, i % 2, 0, :], start=True, stop=True).then_inc(zms_done, 1)
                if u - 2 in ROTATED:
                    i = index_among(u - 2, ROTATED)
                    if u - 2 in NORMED:
                        pe.wait_ge(zn_ready, index_among(u - 2, NORMED) + 1)
                    else:
                        pe.wait_ge(z_ready, u - 1)
                    if i:
                        pe.wait_ge(rot_ready, i)
                    nc.tensor.matmul(ps[4][:, 0:N], c_(C_SWAP, P), zloc[u - 2], start=True, stop=True).then_inc(swapped, 1)
                if u == TOK_SLOT:
                    pe.wait_ge(z_final, index_among(U_KB, ROTATED) + 1)
                    pe.wait_ge(z_ready, U_VW + 1)
                    for t in range(3):
                        r = P if t < 2 else NS_TOK
                        tc_ = slice(t * P, t * P + r)
                        for b, w, c0 in ((0, HD, 0), (1, HD, 64), (2, P, 128), (3, P, 256), (4, HD + HEADS, 384)):
                            ins = nc.tensor.transpose(ps[(2, 3, 0)[t]][0:r, c0:c0 + w], kv[0:w, b, tc_], cst[0:w, C_ID:C_ID + w])
                        ins.then_inc(tok_T, 1)
                if u == WCOL_SLOT:
                    pe.wait_ge(tok_ready, 3)
                    for g in range(2):
                        ins = nc.tensor.matmul(ps[3][:, g * HEADS:(g + 1) * HEADS], c_(C_EXP + g * P, P, NS_TOK),
                                               tok[0:NS_TOK, 2, 448:456], start=True, stop=True)
                    ins.then_inc(wexp_ps, 1)
            for m in STEPS_AFTER:
                attend(m)

            vu = first["U"][1]
            pe.wait_ge(out_lo, 6)
            pe.wait_ge(z_ready, U_END)
            for j in range(8):
                ba, bb = (ps[6], ps[7]) if j % 2 == 0 else (ps[0], ps[1])
                if j >= 2:
                    pe.wait_ge(m_scaled, j - 1)
                unit(vu + j, ba, lambda k: (ahi[:, k, :], alo[:, k, :], P), kl=range(4), done=False)
                unit(vu + j, bb, lambda k: (bhi[:, k - 4, :], blo[:, k - 4, :], P), kl=range(4, 8))
            vo = first["O"][1]
            for j in range(8):
                if j >= 2:
                    pe.wait_ge(o_evac, j - 1)
                wait_x = (lambda k: pe.wait_ge(m_lo, k + 1)) if j == 0 else None
                unit(vo + j, ps[2 + j % 2], lambda k: (mhi[:, k, :], mlo[:, k, :], P), wait_x=wait_x)
            gate_up(2, 2)

            def y_T(k):
                pe.wait_ge(down_evac, DOWN_FREE + KB + k + 1)
                if k >= 2:
                    pe.wait_ge(y_ready, k - 1)
                for t in range(3):
                    r = P if t < 2 else NS_TOK
                    ins = nc.tensor.transpose(ps[k % 2][0:r, t * P:(t + 1) * P], x[:, k, t * P:t * P + r], ident)
                ins.then_inc(yT_done, 1)

            down_turn(2, 0, 0, between=lambda q: [y_T(k) for k in range(2 * q - 2, 2 * q)] if q else None)
            down_turn(2, 0, 2, between=lambda q: [y_T(k) for k in range(2 * q - 2, 2 * q)])
            for k in range(KB - 2, KB):
                y_T(k)


INPUTS = ("x_prompt x_sample cache_k_a cache_v_a cache_kidx_a cache_k_b cache_v_b page_table ffn1_norm ffn1_w_in "
          "ffn1_w_out mix_norm w_in q_norm_a k_norm_a q_norm_b k_norm_b gate_bias w_up_a w_up_b w_out ffn2_norm "
          "ffn2_w_in ffn2_w_out").split()
LAYER_WEIGHTS = "ffn1_w_in ffn1_w_out w_in w_up_a w_up_b w_out ffn2_w_in ffn2_w_out".split()


def kernel(**inputs):
    import concourse.bacc as bacc
    from concourse.bass_utils import run_bass_kernel_spmd

    nc = bacc.Bacc("TRN2", target_bir_lowering=False, num_devices=1)
    arrays, a = {}, {}
    for name in INPUTS:
        v = np.ascontiguousarray(inputs[name])
        arrays[f"in_{name}"] = v
        a[name] = nc.dram_tensor(f"in_{name}", v.shape, mybir.dt.from_np(v.dtype), kind="ExternalInput").ap()
    for name in LAYER_WEIGHTS:
        a[name] = a[name].rearrange("l r c -> (l r) c")
    arrays["in_constants"] = shape_constants()
    a["constants"] = nc.dram_tensor("in_constants", (P, C_ALL), F32, kind="ExternalInput").ap()
    returned = [("y_prompt", (1, NP_TOK, D)), ("y_sample", (N_SEQ, N_NEW, D))]
    for g, lead in (("p", (1, 1, NP_TOK)), ("s", (1, N_SEQ, N_NEW))):
        returned += [(f"new_k_a_{g}", lead + (1, HD)), (f"new_v_a_{g}", lead + (1, HD)), (f"new_kidx_{g}", lead + (HD,)),
                     (f"new_k_b_{g}", lead + (2, HD)), (f"new_v_b_{g}", lead + (2, HD))]
    o = {}
    for name, shape in returned:
        t = nc.dram_tensor(f"out_{name}", shape, F32, kind="ExternalOutput").ap()
        if name.endswith("_p"):
            t = t.rearrange("l b (t p) d -> p (l b t) d" if len(shape) == 4 else "l b (t p) h d -> p (l b t) (h d)", p=P)
        elif name.endswith("_s"):
            t = t.rearrange("l b t d -> (l b t) d" if len(shape) == 4 else "l b t h d -> (l b t) (h d)")
        o[name] = t
    build(nc, a, o)
    r = run_bass_kernel_spmd(nc, [arrays], core_ids=[0])
    return tuple(r.results[0][f"out_{name}"] for name, _ in returned)
```

```python
from contextlib import ExitStack

import numpy as np

import concourse.bass as bass
from concourse import mybir

F32 = mybir.dt.float32
F32R = mybir.dt.float32r
BF16 = mybir.dt.bfloat16
I32 = mybir.dt.int32
ALU = mybir.AluOpType
ACT = mybir.ActivationFunctionType
AX = mybir.AxisListType.X

P = 128
EPS = 1e-6
ROPE_THETA = 10000.0
NEG = -float(2.0 ** 100)
TAKEN = -3.0e38
TAKEN_LIMIT = -2.0e38

NP_TOK, N_SEQ, N_NEW = 256, 8, 4
NS_TOK = N_SEQ * N_NEW
N = NP_TOK + NS_TOK
PAST = 256
PAGE = 128
NPG = PAST // PAGE
HD = 64
HEADS = 8
TOPK_PROMPT = NP_TOK // 4
TOPK_SAMPLE = (PAST + N_NEW) // 4
NK_S = PAST + NS_TOK
D = 1024
KB = D // P
DFF = 2752
FB = -(-DFF // P)
FTAIL = DFF - (FB - 1) * P
TC = 256
NR, NU = 3, 4
AHEAD = NU

C_ID, C_SWAP, C_BLK, C_ONE = 0, P, 2 * P, 3 * P
C_COS, C_SIN = 4 * P, 4 * P + N
C_CAUSAL = C_SIN + N
C_MASKS = C_CAUSAL + 2 * P
C_EXP = C_MASKS + NK_S
C_EXPT = C_EXP + 2 * P
C_HSEL = C_EXPT + 2 * NS_TOK
C_ALL = C_HSEL + HEADS


def shape_constants():
    c = np.zeros((P, C_ALL), np.float32)
    half = HD // 2
    inv = (np.float32(ROPE_THETA) ** (-np.arange(half, dtype=np.float32) / np.float32(half))).astype(np.float32)
    pos = np.concatenate([np.arange(NP_TOK), np.tile(PAST + np.arange(N_NEW), N_SEQ)]).astype(np.float32)
    ang = (pos[None, :] * inv[:, None]).astype(np.float32)
    c[:, C_COS:C_COS + N] = np.tile(np.cos(ang), (4, 1))
    c[:, C_SIN:C_SIN + N] = np.tile(np.concatenate([-np.sin(ang), np.sin(ang)]), (2, 1))
    p = np.arange(P)
    c[p ^ half, C_SWAP + p] = 1.0
    c[p, C_ID + p] = 1.0
    c[:, C_BLK:C_BLK + P] = (p[:, None] // HD == p[None, :] // HD) / HD
    c[:, C_ONE:C_ONE + P] = 1.0 / D
    keys = np.arange(2 * P)
    c[:, C_CAUSAL:C_CAUSAL + 2 * P] = np.where(keys[None, :] <= P + p[:, None], 0.0, NEG)
    b, t = np.arange(NS_TOK) // N_NEW, np.arange(NS_TOK) % N_NEW
    c[:NS_TOK, C_MASKS + PAST:C_MASKS + NK_S] = np.where(
        (b[:, None] == b[None, :]) & (t[None, :] <= t[:, None]), 0.0, NEG)
    rb, rh, rt = p // 32, p % 32 // N_NEW, p % N_NEW
    for g in range(2):
        e = (b[:, None] == 4 * g + rb[None, :]) & (t[:, None] == rt[None, :])
        c[:NS_TOK, C_EXP + g * P:C_EXP + (g + 1) * P] = e
        c[:, C_EXPT + g * NS_TOK:C_EXPT + (g + 1) * NS_TOK] = e.T
    c[:, C_HSEL:C_HSEL + HEADS] = rh[:, None] == np.arange(HEADS)[None, :]
    return c


def weight_plan():
    tiles, units, first = [], [], {}

    def ffn(f):
        first[f"G{f}"] = len(tiles), len(units)
        w = f"ffn{f}_w_in"
        for t in range(FB // 2 - 1):
            n = len(tiles)
            for c0 in (0, DFF):
                tiles.append([(0, P, 0, KB, 0, TC, w, 0, c0 + TC * t)])
            for m in range(2):
                for g in range(2):
                    units.append((n + g, m * P, P, KB))
        n = len(tiles)
        for c0, width in (((FB - 2) * P, P), ((FB - 1) * P, FTAIL)):
            tiles.append([(0, P, 0, KB, 0, 2 * width, w, 0, (c0, c0 + width))])
        for m in range(2):
            for g in range(2):
                units.append((n + g, m * P, P, KB))
        first[f"D{f}"] = len(tiles), len(units)
        w = f"ffn{f}_w_out"
        for c in range(D // TC):
            for k0 in range(0, FB, KB):
                kb = min(KB, FB - k0)
                n = len(tiles)
                full = kb - (k0 + kb == FB)
                tiles.append([(0, P, 0, full, 0, TC, w, k0 * P, c * TC)])
                if full < kb:
                    tiles[-1] += [(s * FTAIL, FTAIL, full, 1, 0, TC, w, (FB - 1) * P, c * TC) for s in range(2)]
                units.extend((n, m * P, P, kb) for m in range(2))

    def one(*cols):
        tiles.append([(0, P, 0, KB, a, w, "w_in", 0, s) for a, w, s in cols])

    ffn(1)
    first["P"] = len(tiles), len(units)
    wqa, wk, wq = 0, HD, HEADS * HD
    ka, va = wq, wq + wk
    qi = va + wk
    ki = qi + wq
    wi = ki + wk
    qb = wi + HEADS
    kb_ = qb + wq
    vb = kb_ + 2 * HD
    ga = vb + 2 * HD
    one((0, TC, qi))
    one((0, TC, qi + TC))
    one((0, HD, ka), (HD, HD, ka), (2 * HD, HD, ki), (3 * HD, HD, ki))
    one((0, TC, kb_))
    qbh = [((s * HD), HD, qb + (m + 4 * s) * HD) for m in range(4) for s in range(2)]
    at = lambda m, a: [(a + qbh[2 * m + s][0], HD, qbh[2 * m + s][2]) for s in range(2)]
    one((0, HD, va), (HD, HEADS, wi), *at(0, P))
    one(*at(1, 0), *at(2, P))
    one(*at(3, 0), (P, P, wqa))
    one((0, TC, wqa + P))
    one((0, P, wqa + 3 * P), (P, P, ga))
    for g in range(7):
        one((0, TC, ga + P + g * TC))
    one((0, P, ga + 15 * P))
    base = first["P"][0]
    for u in range(U_END):
        units.append((base + u // 2, (u % 2) * P, HD + HEADS if u == U_VW else P, KB))
    first["U"] = len(tiles), len(units)
    for c in range(D // TC):
        n = len(tiles)
        tiles.append([(0, P, 0, 4, 0, TC, "w_up_a", 0, c * TC)]
                     + [(s * HD, HD, 4, 4, 0, TC, "w_up_b", s * 4 * HD, c * TC) for s in range(2)])
        units.extend((n, m * P, P, KB) for m in range(2))
    first["O"] = len(tiles), len(units)
    for c in range(D // TC):
        n = len(tiles)
        tiles.append([(0, P, 0, KB, 0, TC, "w_out", 0, c * TC)])
        units.extend((n, m * P, P, KB) for m in range(2))
    ffn(2)
    return tiles, units, first


U_QI, U_KA, U_KI, U_KB, U_VB, U_VW, U_QB, U_QA, U_GATE, U_END = 0, 4, 5, 6, 7, 8, 9, 13, 17, 33
NORMED = [U_KA, U_KB] + list(range(U_QB, U_QA + 4))
LAST_QUERY = {U_KB: 0, U_QB + 3: 1, U_QA + 3: 2}
ROTATED = [u for u in range(U_GATE) if u not in (U_VB, U_VW)]
GAIN_OF = {U_KA: 41, U_KB: 43} | {u: 42 for u in range(U_QB, U_QB + 4)} | {u: 40 for u in range(U_QA, U_QA + 4)}
GAIN_ROWS = 44

IDX, MOBA, DSA = 0, 1, 2
N_STEPS = 24
STEPS_OF_SLOT = {12 + i: [2 * i, 2 * i + 1] for i in range(4)} | {u: [u - 9] for u in range(17, U_END)}
KEY_SLOTS = {u: (2 * u - 2, 2 * u - 1) for u in range(1, 7)}
TOK_SLOT = 11
ROT_DELAY = 3
SEARCH_SLOT, SEARCH_STEPS = 20, 3


def step_kind(m):
    kind, a = divmod(m, 8)
    return (kind, 1, a) if a < 4 else (kind, 0, a - 4) if a < 6 else (kind, 2, a - 6)


def step_heads(form, i):
    return (i // 2, [2 * (i % 2), 2 * (i % 2) + 1], 2 * P) if form == 1 else (i, [0, 1, 2, 3], P)


def out_group(m):
    kind, form, i = step_kind(m)
    g = (kind - 1) * 3 + {1: 0, 0: 1, 2: 2}[form]
    return g, i == {1: 3, 0: 1, 2: 1}[form]


def build(nc, a, o):
    tiles, units, first = weight_plan()
    landed, total = [], [0] * NR
    for n, t in enumerate(tiles):
        total[n % NR] += 16 * len(t)
        landed.append(total[n % NR])
    tile_split = [0] * len(tiles)
    for v, u in enumerate(units):
        tile_split[u[0]] = v + 1

    ctx = ExitStack()
    with ctx:
        sems = {}

        def sem(name):
            sems[name] = ctx.enter_context(nc.semaphore(name))
            return sems[name]

        here = [-(-nc.sbuf_base // 128) * 128]

        def sb(name, shape, dt=F32, at=None):
            size = int(np.prod(shape[1:])) * (2 if dt == BF16 else 4)
            where = here[0] if at is None else at
            t = nc.alloc_sbuf_tensor_at(name, shape, dt, offset=where)
            if at is None:
                here[0] += -(-size // 32) * 32
            return t, where

        def new(name, shape, dt=F32):
            return sb(name, shape, dt)[0]

        raw = new("raw", [P, NR, KB, TC])
        whi = new("whi", [P, NU, KB, P], F32R)
        wlo = new("wlo", [P, NU, KB, P], F32R)
        x = new("x", [P, KB, N])
        nhi = new("nhi", [P, KB, N], F32R)
        nlo = new("nlo", [P, KB, N], F32R)
        hhi, at_h = sb("hhi", [P, FB, N], F32R)
        hlo = new("hlo", [P, FB, N], F32R)
        blk = lambda i: at_h + i * N * 4
        xtok, _ = sb("xtok", [P, 3, D], at=at_h)
        qi, _ = sb("qi", [P, 4, N], at=blk(0))
        qb, _ = sb("qb", [P, 4, N], at=blk(4))
        qa, _ = sb("qa", [P, 4, N], at=blk(8))
        bhi, _ = sb("bhi", [P, 4, N], F32R, at=blk(0))
        blo, _ = sb("blo", [P, 4, N], F32R, at=blk(12))
        ahi, _ = sb("ahi", [P, 4, N], F32R, at=blk(4))
        alo, _ = sb("alo", [P, 4, N], F32R, at=blk(16))
        gates, _ = sb("gates", [P, 16, N], at=blk(20))
        kv, _ = sb("kv", [P, 5, N], at=blk(36))
        roots, _ = sb("roots", [P, 2, N], at=blk(41))
        masksb, _ = sb("masksb", [NS_TOK, NK_S], BF16, at=blk(43))
        expb, _ = sb("expb", [NS_TOK, 2 * P], BF16, at=blk(43) + 2 * NK_S)
        kt, at_kt = sb("kt", [P, 3, N_SEQ, PAST])
        ytok, _ = sb("ytok", [P, 3, D], at=at_kt)
        mhi, _ = sb("mhi", [P, KB, N], F32R, at=blk(36))
        mlo, _ = sb("mlo", [P, KB, N], F32R, at=at_kt)
        va_pg = new("va_pg", [P, N_SEQ * NPG, HD])
        vb_pg = new("vb_pg", [P, N_SEQ * NPG, P])
        cst = new("cst", [P, C_ALL])
        idb = new("idb", [P, P], BF16)
        causalb = new("causalb", [P, 2 * P], BF16)
        gains = new("gains", [P, GAIN_ROWS])
        ptab = new("ptab", [1, N_SEQ * NPG], I32)
        tmp = new("tmp", [P, 2, 1, N])
        act_tmp = new("act_tmp", [P, 2, 1, N])
        rms, ssq = act_tmp[:, 0, 0, :], act_tmp[:, 1, 0, :]
        rstd = new("rstd", [P, N])
        sq_block = (act_tmp[:, 0, 0, :], rstd[:, :])
        eps_col = new("eps_col", [P, 16])
        kraw, at_att = sb("kraw", [P, 3, N_SEQ * NPG, P])
        end_kraw = here[0]
        here[0] = at_att
        rows, _ = sb("rows", [GAIN_ROWS, P], at=at_att)
        rot_tmp = tmp[:, :, 0, :]
        va2 = new("va2", [NS_TOK, P])
        tok = new("tok", [P, 3, 456])
        probs = new("probs", [P, 2, 512])
        probsT = new("probsT", [P, 2, 512])
        qz = new("qz", [P, 3, 2 * P])
        acc1 = new("acc1", [P, 2 * P])
        acc0 = new("acc0", [P, P])
        acc_s = new("acc_s", [NS_TOK, NK_S])
        best = new("best", [P, 8])
        sel1 = new("sel1", [P, 2 * P], BF16)
        sel0 = new("sel0", [P, P], BF16)
        sel_s = new("sel_s", [NS_TOK, NK_S], BF16)
        nmax = new("nmax", [P, 4 * N_STEPS])
        rsum = new("rsum", [P, 4 * N_STEPS])
        rinv = new("rinv", [P, 4 * N_STEPS])
        wi_p = new("wi_p", [P, 2, HEADS])
        wsel = new("wsel", [P, 2, HEADS])
        wcol = new("wcol", [P, 2])
        wexp = new("wexp", [P, 2, NS_TOK])
        assert here[0] <= nc.sbuf_usable_end and end_kraw <= nc.sbuf_usable_end, (here, end_kraw, nc.sbuf_usable_end)
        ps = [ctx.enter_context(nc.psum_tensor(f"ps{i}", [P, 512], F32)) for i in range(8)]
        zloc = ([qi[:, i, :] for i in range(4)] + [kv[:, i, :] for i in range(5)]
                + [qb[:, i, :] for i in range(4)] + [qa[:, i, :] for i in range(4)])
        KT_OF = {IDX: 0, MOBA: 1, DSA: 2}
        Q_OF = {IDX: qi, MOBA: qb, DSA: qa}
        K_OF = {IDX: kv[:, 1, :], MOBA: kv[:, 2, :], DSA: kv[:, 0, :]}
        c_ = lambda at, n, rows_=P: cst[0:rows_, at:at + n]

        raw_in = [sem(f"raw_in{i}") for i in range(NR)]
        (tail_in, x_in, x_rest_in, const_in, consts_in, rows_in, ptab_in, pages_in, out_done) = [sem(s) for s in
            "tail_in x_in x_rest_in const_in consts_in rows_in ptab_in pages_in out_done".split()]
        (gains_T, gains_ready, scaled_gains, masks_ready) = [sem(s) for s in
            "gains_T gains_ready scaled_gains masks_ready".split()]
        (xT_done, x_ready, squares_ready, ms_done, root_ready, scaled, n_hi, n_lo) = [sem(s) for s in
            "xT_done x_ready squares_ready ms_done root_ready scaled n_hi n_lo".split()]
        w_hi, w_lo, unit_done = [sem(s) for s in "w_hi w_lo unit_done".split()]
        (gate_scaled, silu_done, pair_free, prod_ready, h_hi, h_lo, down_evac) = [sem(s) for s in
            "gate_scaled silu_done pair_free prod_ready h_hi h_lo down_evac".split()]
        keysT_done, keysT_act, keysT_dve = [sem(s) for s in "keysT_done keysT_act keysT_dve".split()]
        (z_ready, zsq_ready, zg_ready, zms_done, zroot_ready, zrstd_ready, zn_ready) = [sem(s) for s in
            "z_ready zsq_ready zg_ready zms_done zroot_ready zrstd_ready zn_ready".split()]
        swapped, rot_ready, rot_cos, z_final = [sem(s) for s in "swapped rot_ready rot_cos z_final".split()]
        (tok_T, tok_ready, va2_ready, wi_ready, wexp_ps, wexp_ready) = [sem(s) for s in
            "tok_T tok_ready va2_ready wi_ready wexp_ps wexp_ready".split()]
        qz_zero, qz_ready = [sem(s) for s in "qz_zero qz_ready".split()]
        (logits_done, max_done, soft_done, rinv_ready, probs_ready, probsT_done, probsT_ready) = [sem(s) for s in
            "logits_done max_done soft_done rinv_ready probs_ready probsT_done probsT_ready".split()]
        pv_done, out_hi, out_lo = [sem(s) for s in "pv_done out_hi out_lo".split()]
        idx_acc, score_ps, score_ready, sel_ready = [sem(s) for s in "idx_acc score_ps score_ready sel_ready".split()]
        (up_b_done, sig_ready, a_gated, b_gated, m_scaled, m_hi, m_lo, o_evac) = [sem(s) for s in
            "up_b_done sig_ready a_gated b_gated m_scaled m_hi m_lo o_evac".split()]
        yT_done, y_ready = [sem(s) for s in "yT_done y_ready".split()]
        dve_chain, pool_chain = [sem(s) for s in "dve_chain pool_chain".split()]

        LOOP_TILES, LOOP_UNITS, LOOP_PAIRS = 6, 12, 6
        G_LOOPS = FB // 2 // 3
        G_HEAD = 2
        D_LOOPS = D // TC // 2
        FIRST_SPLITS = {4: (0,), 7: (1,), 8: (2, 3)}
        MS_AFTER = (2, 1)
        MS_BANK = (7, 0, 7)
        BANKS_FREE = 3
        DOWN_FREE = 3
        TAIL_IN = 33
        UP_A_BANK = (0, 1, 4, 5)
        UP_B_BANK = (7, 6, 2, 3)
        KEYS_BANK = (3, 0)

        def landed_per_turn(n):
            return landed[n + LOOP_TILES] - landed[n]

        def keys_of(g):
            return kt[:, g // 4, :, :].rearrange("p b k -> p (b k)")[:, (g % 4) * 512:(g % 4 + 1) * 512]

        def index_among(u, those):
            return those.index(u)

        def sample_columns(ap, kind, s):
            order = "p (b s m t) -> p s m b t" if kind == MOBA else "p (b m s t) -> p s m b t"
            return ap.rearrange(order, b=N_SEQ, m=4, s=2, t=N_NEW)[:, s]

        def z_bank(u):
            return (6, 7, 1, 2)[u] if u < 4 else 6 + u % 2

        def last_of_bank(u):
            return u - 2 if u >= 6 else u - 4

        def out_views(t, bank, kind, form):
            if form < 2:
                return [(t[:, :, form * P:(form + 1) * P], bank[:, :].rearrange("p (m q) -> p m q", m=4))]
            halves = [slice(s * HD, (s + 1) * HD) for s in range(2)]
            return [(t[h, :, NP_TOK:N].rearrange("p m (b t) -> p m b t", t=N_NEW),
                     sample_columns(bank[h, 0:2 * P], kind, s)) for s, h in enumerate(halves)]

        block = ctx.enter_context(nc.Block())

        @block.sync
        def _(sp):
            def load(n, it=None, turns=1):
                if n >= NR:
                    free = max(tile_split[n - NR + LOOP_TILES * i] - LOOP_UNITS * i for i in range(turns))
                    free = free if it is None else free + LOOP_UNITS * it
                    sp.wait_ge(w_hi, free)
                    sp.wait_ge(w_lo, free)
                for p0, np_, k0, nk, c0, w, name, r0, s0 in tiles[n]:
                    if isinstance(s0, tuple):
                        for g, landed_sem in ((0, raw_in[n % NR]), (1, tail_in)):
                            src = a[name][:, g * DFF + s0[0]:g * DFF + s0[1]].rearrange("(k p) c -> p k c", p=P)
                            sp.dma_start(raw[:, n % NR, :, g * (w // 2):(g + 1) * (w // 2)], src).then_inc(landed_sem, 16)
                        continue
                    src = a[name][r0:r0 + nk * np_, :]
                    if it is None:
                        src = src[:, s0:s0 + w]
                    else:
                        step = tiles[n + LOOP_TILES][0][8] - tiles[n][0][8]
                        src = src[:, bass.ds(it * step + s0, w)]
                    sp.dma_start(raw[p0:p0 + np_, n % NR, k0:k0 + nk, c0:c0 + w],
                                 src.rearrange("(k p) c -> p k c", p=np_)).then_inc(raw_in[n % NR], 16)

            sp.dma_start(xtok[0:NS_TOK, 2, :], a["x_sample"].rearrange("b t d -> (b t) d")).then_inc(x_in, 16)
            for cols, x_part_in in ((slice(0, D // 2), x_in), (slice(D // 2, D), x_rest_in)):
                sp.dma_start(xtok[:, 0:2, cols], a["x_prompt"].rearrange("b (t p) d -> p (b t) d", p=P)[:, :, cols])\
                    .then_inc(x_part_in, 16)
            for f in (1, 2):
                g0, d0 = first[f"G{f}"][0], first[f"D{f}"][0]
                for n in range(LOOP_TILES):
                    load(g0 + n)
                with sp.Fori(0, G_LOOPS - 1) as it:
                    for n in range(LOOP_TILES):
                        load(g0 + LOOP_TILES + n, it, G_LOOPS - 1)
                for n in range(G_LOOPS * LOOP_TILES, 2 * (FB // 2)):
                    load(g0 + n)
                with sp.Fori(0, D_LOOPS) as it:
                    for n in range(LOOP_TILES):
                        load(d0 + n, it, D_LOOPS)
                if f == 1:
                    for n in range(first["P"][0], first["G2"][0]):
                        load(n)
            yp, ys = o["y_prompt"].rearrange("b (t p) d -> p (b t) d", p=P), o["y_sample"].rearrange("b t d -> (b t) d")
            for k0, k1 in ((0, 4), (4, 6), (6, KB)):
                sp.wait_ge(y_ready, k1)
                cols = slice(k0 * P, k1 * P)
                sp.dma_start(yp[:, :, cols], ytok[:, 0:2, cols]).then_inc(out_done, 16)
                sp.dma_start(ys[:, cols], ytok[0:NS_TOK, 2, cols]).then_inc(out_done, 16)
            sp.wait_ge(out_done, 16 * 16)

        @block.gpsimd
        def _(pool):
            pool_ops = [0]

            def squares(r, ready, base):
                n = pool_ops[0]
                for k in range(KB + 1):
                    if k < KB:
                        pool.wait_ge(ready, base + k + 1)
                        if k >= 3:
                            pool.wait_ge(pool_chain, n + 2 * k - 2)
                        dst = sq_block[k % 2] if k else ssq
                        nc.gpsimd.tensor_tensor(dst, x[:, k, :], x[:, k, :], ALU.mult).then_inc(pool_chain, 1)
                    if k >= 2:
                        pool.wait_ge(pool_chain, n + 2 * k - 2)
                        ins = nc.gpsimd.tensor_tensor(ssq, ssq, sq_block[(k - 1) % 2], ALU.add)
                        ins.then_inc(*((pool_chain, 1) if k < KB else (squares_ready, 1)))
                pool_ops[0] += 2 * KB - 2

            squares(0, x_ready, 0)
            nc.gpsimd.dma_start(ptab[:], a["page_table"].rearrange("a b -> (a b)")[None, :]).then_inc(ptab_in, 16)
            pool.wait_ge(ptab_in, 16)
            n_pool = a["cache_k_a"].shape[1]
            flat = {n: a[n].rearrange("l n p h d -> (l n) p (h d)") for n in
                    ("cache_k_a", "cache_v_a", "cache_k_b", "cache_v_b")}
            flat["cache_kidx_a"] = a["cache_kidx_a"].rearrange("l n p d -> (l n) p d")
            with pool.Fori(0, N_SEQ * NPG) as i:
                page = pool.value_load(ptab[0:1, bass.ds(i, 1)], min_val=0, max_val=n_pool - 1)
                for name, dst in (("cache_kidx_a", kraw[:, 0, bass.ds(i, 1), 0:HD]),
                                  ("cache_kidx_a", kraw[:, 0, bass.ds(i, 1), HD:P]),
                                  ("cache_k_b", kraw[:, 1, bass.ds(i, 1), :]),
                                  ("cache_k_a", kraw[:, 2, bass.ds(i, 1), 0:HD]),
                                  ("cache_k_a", kraw[:, 2, bass.ds(i, 1), HD:P]),
                                  ("cache_v_a", va_pg[:, bass.ds(i, 1), :]),
                                  ("cache_v_b", vb_pg[:, bass.ds(i, 1), :])):
                    nc.gpsimd.dma_start(dst, flat[name][bass.ds(page, 1), :, :].rearrange("o p d -> p o d"))\
                        .then_inc(pages_in, 16)

            squares(1, down_evac, DOWN_FREE)
            def sample_queries(kind):
                if kind == IDX:
                    pool.wait_ge(keysT_done, 12)
                    nc.gpsimd.memset(qz[:], 0.0).then_inc(qz_zero, 1)
                    pool.wait_ge(qz_zero, 1)
                for s in range(2):
                    half = slice(s * HD, (s + 1) * HD)
                    dst = sample_columns(qz[half, kind, :], kind, s)
                    src = Q_OF[kind][half, :, NP_TOK:N].rearrange("p m (b t) -> p m b t", t=N_NEW)
                    nc.gpsimd.tensor_copy(dst, src).then_inc(qz_ready, 1)
                    pool.wait_ge(qz_ready, 2 * kind + s + 1)

            def weigh(m):
                kind, form, i = step_kind(m)
                nh, w = {1: (2, 2 * P), 0: (4, P), 2: (1, NK_S)}[form]
                pool.wait_ge(rinv_ready, m - 7)
                pool.wait_ge(soft_done, m + 1)
                pv = probs[:, m % 2, 0:nh * w].rearrange("p (h k) -> p h k", h=nh)
                r = rinv[:, 4 * m:4 * m + nh].unsqueeze(2).to_broadcast([P, nh, w])
                nc.gpsimd.tensor_tensor(pv, pv, r, ALU.mult).then_inc(probs_ready, 1)

            for u in range(U_END):
                if u - 1 != NORMED[-1]:
                    for m in STEPS_OF_SLOT.get(u, []):
                        if 8 <= m:
                            weigh(m)
                if u - ROT_DELAY in ROTATED:
                    i = index_among(u - ROT_DELAY, ROTATED)
                    z = zloc[u - ROT_DELAY]
                    pool.wait_ge(swapped, i + 1)
                    nc.gpsimd.tensor_tensor(z, z, c_(C_COS, N), ALU.mult).then_inc(rot_cos, 1)
                    pool.wait_ge(rot_cos, i + 1)
                    pool.wait_ge(rot_ready, i + 1)
                    nc.gpsimd.tensor_tensor(z, z, rot_tmp[:, i % 2, :], ALU.add).then_inc(z_final, 1)
                    if u - ROT_DELAY in LAST_QUERY:
                        pool.wait_ge(z_final, i + 1)
                        sample_queries(LAST_QUERY[u - ROT_DELAY])
                if u - 1 == NORMED[-1]:
                    for m in STEPS_OF_SLOT.get(u, []):
                        weigh(m)
                if u - 1 in NORMED:
                    i = index_among(u - 1, NORMED)
                    pool.wait_ge(zg_ready, i + 1)
                    pool.wait_ge(zrstd_ready, i + 1)
                    nc.gpsimd.tensor_tensor(zloc[u - 1], zloc[u - 1], roots[:, i % 2, :], ALU.mult).then_inc(zn_ready, 1)
                if u == TOK_SLOT:
                    pool.wait_ge(tok_ready, 3)
                    for s in range(2):
                        nc.gpsimd.tensor_copy(va2[:, s * HD:(s + 1) * HD], tok[0:NS_TOK, 2, 384:448]).then_inc(va2_ready, 1)
                        pool.wait_ge(va2_ready, s + 1)
            squares(2, o_evac, 0)

        @block.scalar
        def _(act):
            act.dma_start(cst[:, 0:P], a["constants"][:, 0:P]).then_inc(const_in, 16)
            act.dma_start(rows[:], a["gain_rows"]).then_inc(rows_in, 16)

            def split_hi(v, it=0):
                n, c0, w, nk = units[v]
                step = 0 if isinstance(it, int) else landed_per_turn(n)
                act.wait_ge(raw_in[n % NR], landed[n] + step * it)
                if v >= NU:
                    act.wait_ge(unit_done, v - NU + 1 + LOOP_UNITS * it)
                nc.scalar.activation(whi[:, v % NU, 0:nk, 0:w], raw[:, n % NR, 0:nk, c0:c0 + w], ACT.Copy)\
                    .then_inc(w_hi, 1)

            preloads = [0]

            def preload(function):
                c = 5 + preloads[0]
                preloads[0] += 1
                nc.scalar.activation(eps_col[:, c:c + 1], eps_col[:, 0:1], function)

            def root(r):
                act.wait_ge(ms_done, r + 1)
                nc.scalar.activation(rms, ps[MS_BANK[r]][:, 0:N], ACT.Sqrt, bias=eps_col[:, 0:1]).then_inc(root_ready, 1)

            def norm_hi(r, k, it=0):
                act.wait_ge(scaled, KB * r + k + 1 + 4 * it)
                at = slice(k, k + 1) if isinstance(it, int) else bass.ds(4 * it + k, 1)
                nc.scalar.activation(nhi[:, at, :], tmp[:, k % 2, :, :], ACT.Copy).then_inc(n_hi, 1)

            for k in range(KB + 1):
                if k < KB:
                    act.wait_ge(xT_done, k + 1)
                    nc.scalar.activation(x[:, k, :], ps[4 + k % 4][:, 0:N], ACT.Copy).then_inc(x_ready, 1)
                if k:
                    norm_hi(0, k - 1)
                for v in FIRST_SPLITS.get(k, ()):
                    split_hi(v)
                if k == 3:
                    act.dma_start(cst[:, P:], a["constants"][:, P:]).then_inc(consts_in, 16)
            act.wait_ge(masks_ready, 1)

            def pair(f, p, it=0):
                v = first[f"G{f}"][1] + 2 * p + 1
                gp = (f - 1) * FB + p
                w = P if p < FB - 1 else FTAIL
                if p == 0:
                    split_hi(v - 1 + AHEAD)
                    split_hi(v + AHEAD)
                    preload(ACT.Sqrt)
                    root(0 if f == 1 else 2)
                    preload(ACT.Silu)
                if p == FB - 2:
                    split_hi(v - 1 + AHEAD)
                    split_hi(v + AHEAD)
                act.wait_ge(gate_scaled, gp + 1 + LOOP_PAIRS * it)
                nc.scalar.activation(act_tmp[0:w, p % 2, 0, :], act_tmp[0:w, p % 2, 0, :], ACT.Silu).then_inc(silu_done, 1)
                if p not in (0, FB - 2):
                    split_hi(v - 1 + AHEAD, it)
                    if p == LOOP_PAIRS:
                        act.wait_ge(tail_in, 32 * (f - 1) + 1 + 32 * it)
                    split_hi(v + AHEAD, it)
                act.wait_ge(prod_ready, gp + 1 + LOOP_PAIRS * it)
                at = slice(p, p + 1) if isinstance(it, int) else bass.ds(LOOP_PAIRS * it + p, 1)
                nc.scalar.activation(hhi[0:w, at, :], tmp[0:w, p % 2, :, :], ACT.Copy).then_inc(h_hi, 1)

            def gate_up(f):
                for p in range(G_HEAD):
                    pair(f, p)
                with act.Fori(0, G_LOOPS) as it:
                    for p in range(G_HEAD, G_HEAD + LOOP_PAIRS):
                        pair(f, p, it)
                for p in range(G_HEAD + G_LOOPS * LOOP_PAIRS, FB):
                    pair(f, p)

            def down_turn(it):
                v0 = first["D1"][1]
                for j in range(LOOP_UNITS):
                    if j % 6 >= 4:
                        norm_hi(1, 2 * (j // 6) + j % 6 - 4, it)
                    split_hi(v0 + j + AHEAD, it)

            gate_up(1)
            with act.Fori(0, D_LOOPS) as it:
                down_turn(it)
            vp = first["P"][1]

            def attend(m):
                if 8 <= m - 2 < N_STEPS:
                    n = m - 2 - 8
                    act.wait_ge(probsT_done, n + 1)
                    if n >= 2:
                        act.wait_ge(pv_done, n - 1)
                    if step_kind(m - 2)[1] == 2:
                        nc.scalar.activation(probsT[:, n % 2, 0:256], ps[2 + n % 2][:, 0:256], ACT.Copy)
                        nc.scalar.activation(probsT[0:NS_TOK, n % 2, 256:384], ps[2 + n % 2][0:NS_TOK, 256:384],
                                             ACT.Copy).then_inc(probsT_ready, 1)
                    else:
                        nc.scalar.activation(probsT[:, n % 2, :], ps[2 + n % 2][:, :], ACT.Copy).then_inc(probsT_ready, 1)
                if m < N_STEPS:
                    kind, form, i = step_kind(m)
                    nh, w = {1: (2, 2 * P), 0: (4, P), 2: (1, NK_S)}[form]
                    if m >= 2:
                        k2, f2, i2 = step_kind(m - 2)
                        if k2 != IDX:
                            act.wait_ge(probsT_done, m - 2 - 8 + 1)
                        elif f2 != 2:
                            act.wait_ge(idx_acc, m - 2 + 1)
                        else:
                            act.wait_ge(score_ps, i2 + 1)
                    act.wait_ge(logits_done, m + 1)
                    if kind == IDX:
                        nc.scalar.activation(probs[:, m % 2, 0:nh * w], ps[m % 2][:, 0:nh * w], ACT.Relu).then_inc(soft_done, 1)
                    else:
                        act.wait_ge(max_done, m - 7)
                        for h in range(nh):
                            ins = nc.scalar.activation(probs[:, m % 2, h * w:(h + 1) * w], ps[m % 2][:, h * w:(h + 1) * w],
                                                       ACT.Exp, bias=nmax[:, 4 * m + h:4 * m + h + 1],
                                                       accum_out=rsum[:, 4 * m + h:4 * m + h + 1])
                        ins.then_inc(soft_done, 1)

            def outputs_hi(m):
                if 8 <= m - 2 < N_STEPS and out_group(m - 2)[1]:
                    g = out_group(m - 2)[0]
                    kind, form, _ = step_kind(m - 2)
                    act.wait_ge(pv_done, m - 2 - 8 + 1)
                    dst_t = bhi if kind == MOBA else ahi
                    for dst, src in out_views(dst_t, ps[5 - g % 2], kind, form):
                        ins = nc.scalar.activation(dst, src, ACT.Copy)
                    ins.then_inc(out_hi, 1)

            for u in range(U_END):
                last_root = u - 1 == NORMED[-1]
                for m in STEPS_OF_SLOT.get(u, []):
                    if not last_root:
                        attend(m)
                if u == TOK_SLOT:
                    for t in range(3):
                        r = P if t < 2 else NS_TOK
                        act.wait_ge(tok_T, t + 1)
                        nc.scalar.activation(tok[0:r, t, :], ps[(2, 3, 0)[t]][0:r, 0:456], ACT.Copy).then_inc(tok_ready, 1)
                    act.wait_ge(tok_ready, 3)
                    for name, c0, w in (("k_a", 0, 64), ("kidx", 64, 64), ("k_b", 128, 128), ("v_b", 256, 128), ("v_a", 384, 64)):
                        act.dma_start(o[f"new_{name}_p"], tok[:, 0:2, c0:c0 + w]).then_inc(out_done, 16)
                        act.dma_start(o[f"new_{name}_s"], tok[0:NS_TOK, 2, c0:c0 + w]).then_inc(out_done, 16)
                split_hi(vp + u + AHEAD)
                for m in STEPS_OF_SLOT.get(u, []):
                    outputs_hi(m)
                if u == 0:
                    preload(ACT.Sqrt)
                    root(1)
                if u - 1 in NORMED:
                    i = index_among(u - 1, NORMED)
                    act.wait_ge(zms_done, i + 1)
                    if i >= 2:
                        act.wait_ge(zn_ready, i - 1)
                    nc.scalar.activation(roots[:, i % 2, :], ps[5][:, 0:N], ACT.Sqrt, bias=eps_col[:, 0:1]).then_inc(zroot_ready, 1)
                    if i == len(NORMED) - 1:
                        preload(ACT.Exp)
                if u in NORMED:
                    i = index_among(u, NORMED)
                    z = zloc[u]
                    act.wait_ge(z_ready, u + 1)
                    if i >= 2:
                        act.wait_ge(zms_done, i - 1)
                    nc.scalar.activation(act_tmp[:, i % 2, 0, :], z, ACT.Square).then_inc(zsq_ready, 1)
                    act.wait_ge(zsq_ready, i + 1)
                    nc.scalar.activation(z, z, ACT.Copy, scale=gains[:, GAIN_OF[u]:GAIN_OF[u] + 1]).then_inc(zg_ready, 1)
                for g in KEY_SLOTS.get(u, ())[0:1]:
                    act.wait_ge(keysT_done, g + 1)
                    nc.scalar.activation(keys_of(g), ps[KEYS_BANK[0]][:, :], ACT.Copy).then_inc(keysT_act, 1)
                if last_root:
                    for m in STEPS_OF_SLOT.get(u, []):
                        attend(m)
            attend(N_STEPS)
            preload(ACT.Sigmoid)
            vu = first["U"][1]

            def gate(j):
                for b in (j, 8 + j):
                    act.wait_ge(z_ready, U_GATE + b + 1)
                    nc.scalar.activation(gates[:, b, :], gates[:, b, :], ACT.Sigmoid,
                                         bias=gains[:, 24 + b:25 + b]).then_inc(sig_ready, 1)

            gate(0)
            attend(N_STEPS + 1)
            gate(1)
            gate(2)
            outputs_hi(N_STEPS + 1)
            gate(3)
            for j in range(8):
                split_hi(vu + j + AHEAD)
                act.wait_ge(m_scaled, j + 1)
                nc.scalar.activation(mhi[:, j, :], tmp[:, j % 2, 0, :], ACT.Copy).then_inc(m_hi, 1)
                if j < 4:
                    gate(j + 4)
            vo = first["O"][1]
            for j in range(8):
                split_hi(vo + j + AHEAD)
                norm_hi(2, j)
            gate_up(2)
            vd = first["D2"][1]
            for j in range(2 * LOOP_UNITS):
                if vd + j + AHEAD < len(units):
                    split_hi(vd + j + AHEAD)

        @block.vector
        def _(dve):
            chained = [0]

            def link(ins):
                chained[0] += 1
                ins.then_inc(dve_chain, 1)
                dve.wait_ge(dve_chain, chained[0])

            def split_lo(v, it=0):
                n, c0, w, nk = units[v]
                dve.wait_ge(w_hi, v + 1 + LOOP_UNITS * it)
                nc.vector.tensor_tensor(wlo[:, v % NU, 0:nk, 0:w], raw[:, n % NR, 0:nk, c0:c0 + w],
                                        whi[:, v % NU, 0:nk, 0:w].bitcast(F32), ALU.subtract).then_inc(w_lo, 1)

            nc.vector.memset(eps_col[:, 0:1], EPS).then_inc(masks_ready, 1)
            nc.vector.memset(eps_col[:, 1:2], 0.0).then_inc(pair_free, BANKS_FREE)
            nc.vector.memset(eps_col[:, 2:3], 0.0).then_inc(down_evac, DOWN_FREE)
            nc.vector.memset(eps_col[:, 3:4], 0.0).then_inc(tail_in, TAIL_IN)
            dve.wait_ge(gains_T, 1)
            nc.vector.tensor_copy(gains[:], ps[0][:, 0:GAIN_ROWS]).then_inc(gains_ready, 1)
            dve.wait_ge(gains_ready, 1)
            for c in (40, 42):
                nc.vector.tensor_scalar(gains[:, c:c + 1], gains[:, c:c + 1], HD ** -0.5, None, ALU.mult).then_inc(scaled_gains, 1)

            def scale(r, k, ready, base, it=0):
                dve.wait_ge(ready, base + k + 1 + 4 * it)
                if isinstance(it, int):
                    at, g = slice(k, k + 1), slice(8 * r + k, 8 * r + k + 1)
                    if k >= 2:
                        dve.wait_ge(n_lo, KB * r + k - 1)
                else:
                    at, g = bass.ds(4 * it + k, 1), bass.ds(4 * it + 8 * r + k, 1)
                    dve.wait_ge(n_lo, KB * r + k - 1 + 4 * it)
                nc.vector.tensor_scalar(tmp[:, k % 2, :, :], x[:, at, :], gains[:, g], None, ALU.mult).then_inc(scaled, 1)

            def norm_lo(r, k, it=0):
                dve.wait_ge(n_hi, KB * r + k + 1 + 4 * it)
                at = slice(k, k + 1) if isinstance(it, int) else bass.ds(4 * it + k, 1)
                nc.vector.tensor_tensor(nlo[:, at, :], tmp[:, k % 2, :, :], nhi[:, at, :].bitcast(F32),
                                        ALU.subtract).then_inc(n_lo, 1)

            def inverse_rms(r):
                dve.wait_ge(root_ready, r + 1)
                link(nc.vector.reciprocal(rstd[:], rms))

            for k in range(KB + 1):
                if k < KB:
                    scale(0, k, x_ready, 0)
                if k:
                    norm_lo(0, k - 1)
                for v in FIRST_SPLITS.get(k, ()):
                    split_lo(v)
            dve.wait_ge(consts_in, 16)
            nc.vector.tensor_copy(idb[:], c_(C_ID, P)).then_inc(masks_ready, 1)
            nc.vector.tensor_copy(causalb[:], c_(C_CAUSAL, 2 * P)).then_inc(masks_ready, 1)

            def pair(f, p, it=0):
                v = first[f"G{f}"][1] + 2 * p + 1
                gp = (f - 1) * FB + p
                bank, up_bank, w, up = ps[2 * (p % 3)], ps[2 * (p % 3) + 1], P, slice(0, P)
                if p == FB - 1:
                    up_bank, w, up = bank, FTAIL, slice(FTAIL, 2 * FTAIL)
                if p == 0:
                    split_lo(v - 1 + AHEAD)
                    split_lo(v + AHEAD)
                    inverse_rms(0 if f == 1 else 2)
                if p == FB - 2:
                    split_lo(v - 1 + AHEAD)
                    split_lo(v + AHEAD)
                dve.wait_ge(unit_done, v + 1 + LOOP_UNITS * it if p != FB - 2 else v + 3)
                nc.vector.tensor_tensor(act_tmp[0:w, p % 2, 0, :], bank[0:w, 0:N], rstd[0:w, :],
                                        ALU.mult).then_inc(gate_scaled, 1)
                if gp >= 2:
                    dve.wait_ge(h_lo, gp - 1 + LOOP_PAIRS * it)
                nc.vector.tensor_tensor(tmp[0:w, p % 2, 0, :], up_bank[up, 0:N], rstd[up, :],
                                        ALU.mult).then_inc(pair_free, 1)
                if p not in (0, FB - 2):
                    split_lo(v - 1 + AHEAD, it)
                dve.wait_ge(silu_done, gp + 1 + LOOP_PAIRS * it)
                dve.wait_ge(pair_free, gp + 1 + BANKS_FREE + LOOP_PAIRS * it)
                nc.vector.tensor_tensor(tmp[0:w, p % 2, 0, :], act_tmp[0:w, p % 2, 0, :], tmp[0:w, p % 2, 0, :],
                                        ALU.mult).then_inc(prod_ready, 1)
                if p not in (0, FB - 2):
                    split_lo(v + AHEAD, it)
                dve.wait_ge(h_hi, gp + 1 + LOOP_PAIRS * it)
                at = slice(p, p + 1) if isinstance(it, int) else bass.ds(LOOP_PAIRS * it + p, 1)
                dst = hlo[:, at, :] if p < FB - 1 else hhi[FTAIL:2 * FTAIL, at, :]
                nc.vector.tensor_tensor(dst, tmp[0:w, p % 2, :, :], hhi[0:w, at, :].bitcast(F32),
                                        ALU.subtract).then_inc(h_lo, 1)

            def gate_up(f):
                for p in range(G_HEAD):
                    pair(f, p)
                with dve.Fori(0, G_LOOPS) as it:
                    for p in range(G_HEAD, G_HEAD + LOOP_PAIRS):
                        pair(f, p, it)
                for p in range(G_HEAD + G_LOOPS * LOOP_PAIRS, FB):
                    pair(f, p)

            def down_turn(f, it, q0=0):
                v0 = first[f"D{f}"][1] + 6 * q0
                for j in range(LOOP_UNITS):
                    q, i = divmod(j, 6)
                    if i >= 4:
                        m = i - 4
                        dve.wait_ge(unit_done, v0 + j + 1 + LOOP_UNITS * it)
                        k = 2 * (q0 + q) + m
                        xk = x[:, k:k + 1, :] if isinstance(it, int) else x[:, bass.ds(4 * it + k, 1), :]
                        bank = ps[(6, 4)[q % 2] + m]
                        nc.vector.scalar_tensor_tensor(xk, bank[:, 0:N].unsqueeze(1), 0.5, xk, ALU.mult, ALU.add)\
                            .then_inc(down_evac, 1)
                        if f == 1:
                            scale(1, k, down_evac, DOWN_FREE, it)
                            norm_lo(1, k, it)
                    if f == 1 and i == 4:
                        continue
                    if f == 1 and i == 5:
                        split_lo(v0 + j - 1 + AHEAD, it)
                    if v0 + j + AHEAD < len(units):
                        split_lo(v0 + j + AHEAD, it)
                    if f == 2 and i == 2 and q0 + q:
                        for k in (2 * (q0 + q) - 2, 2 * (q0 + q) - 1):
                            y_out(k)

            gate_up(1)
            with dve.Fori(0, D_LOOPS) as it:
                down_turn(1, it)
            nc.vector.tensor_copy(masksb[:], c_(C_MASKS, NK_S, NS_TOK)).then_inc(masks_ready, 1)
            nc.vector.tensor_copy(expb[:], c_(C_EXP, 2 * P, NS_TOK)).then_inc(masks_ready, 1)

            vp = first["P"][1]

            searches = ((acc1, TOPK_PROMPT // 8, sel1, c_(C_CAUSAL, 2 * P), 0),
                        (acc0, TOPK_PROMPT // 8, sel0, c_(C_CAUSAL + P, P), 0),
                        (acc_s, -(-TOPK_SAMPLE // 8), sel_s, c_(C_MASKS, NK_S, NS_TOK), TOPK_SAMPLE % 8))

            def search_step(c):
                for work, rounds, final, mask, last_count in searches:
                    r = work.shape[0]
                    if 0 <= c < rounds:
                        link(nc.vector.max(best[0:r, :], work[:]))
                        if c == rounds - 1 and last_count:
                            link(nc.vector.memset(best[0:r, last_count:8], TAKEN))
                        link(nc.vector.match_replace(work[:], best[0:r, :], work[:], TAKEN))
                    if c == rounds:
                        link(nc.vector.tensor_scalar(work[:], work[:], TAKEN_LIMIT, NEG, ALU.is_gt, ALU.mult))
                        nc.vector.tensor_tensor(final[:], work[:], mask, ALU.add).then_inc(sel_ready, 1)
                    c -= rounds + 1

            def attend(m):
                if 8 <= m < N_STEPS:
                    kind, form, i = step_kind(m)
                    nh, w = {1: (2, 2 * P), 0: (4, P), 2: (1, NK_S)}[form]
                    dve.wait_ge(logits_done, m + 1)
                    nc.vector.tensor_reduce(nmax[:, 4 * m:4 * m + nh], ps[m % 2][:, 0:nh * w].rearrange("p (h k) -> p h k", h=nh),
                                            AX, ALU.max, negate=True).then_inc(max_done, 1)
                if m == 8:
                    dve.wait_ge(score_ps, 2)
                    nc.vector.tensor_tensor(acc_s[:], ps[3][0:NS_TOK, 0:NK_S], c_(C_MASKS, NK_S, NS_TOK), ALU.add)\
                        .then_inc(score_ready, 1)
                    dve.wait_ge(score_ready, 1)

            def attend_late(m):
                if m < 6:
                    kind, form, i = step_kind(m)
                    half, blocks, w = step_heads(form, i)
                    acc = acc1 if form == 1 else acc0
                    mask = c_(C_CAUSAL, 2 * P) if form == 1 else c_(C_CAUSAL + P, P)
                    dve.wait_ge(soft_done, m + 1)
                    for j, b in enumerate(blocks):
                        h = 2 * b + half
                        ins = nc.vector.scalar_tensor_tensor(
                            acc[:], probs[:, m % 2, j * w:(j + 1) * w], wi_p[:, form, h:h + 1],
                            mask if i == 0 and j == 0 else acc[:], ALU.mult, ALU.add)
                        if j == len(blocks) - 1:
                            ins.then_inc(idx_acc, 1)
                            dve.wait_ge(idx_acc, m + 1)
                        else:
                            link(ins)
                if 8 <= m < N_STEPS:
                    nh = {1: 2, 0: 4, 2: 1}[step_kind(m)[1]]
                    dve.wait_ge(soft_done, m + 1)
                    nc.vector.reciprocal(rinv[:, 4 * m:4 * m + nh], rsum[:, 4 * m:4 * m + nh]).then_inc(rinv_ready, 1)

            def outputs_lo(m):
                if 8 <= m - 2 < N_STEPS and out_group(m - 2)[1]:
                    g = out_group(m - 2)[0]
                    kind, form, _ = step_kind(m - 2)
                    dve.wait_ge(out_hi, g + 1)
                    lo_t, hi_t = (blo, bhi) if kind == MOBA else (alo, ahi)
                    for (dst, src), (hi, _) in zip(out_views(lo_t, ps[5 - g % 2], kind, form),
                                                   out_views(hi_t, ps[5 - g % 2], kind, form)):
                        ins = nc.vector.tensor_tensor(dst, src, hi.bitcast(F32), ALU.subtract)
                    ins.then_inc(out_lo, 1)

            for u in range(U_END):
                for m in STEPS_OF_SLOT.get(u, []):
                    attend(m)
                if u >= SEARCH_SLOT:
                    for c in range(SEARCH_STEPS * (u - SEARCH_SLOT), SEARCH_STEPS * (u - SEARCH_SLOT + 1)):
                        search_step(c)
                late = [m for m in STEPS_OF_SLOT.get(u, []) if m < 8 or u - 1 == NORMED[-1]]
                for m in STEPS_OF_SLOT.get(u, []):
                    if m not in late:
                        attend_late(m)
                if u == 0:
                    split_lo(vp + AHEAD)
                    inverse_rms(1)
                dve.wait_ge(unit_done, vp + u + 1)
                bank = ps[z_bank(u)]
                if u < U_GATE:
                    w = units[vp + u][2]
                    nc.vector.tensor_tensor(zloc[u][0:w], bank[0:w, 0:N], rstd[0:w, :], ALU.mult).then_inc(z_ready, 1)
                else:
                    nc.vector.tensor_tensor(gates[:, u - U_GATE, :], bank[:, 0:N], rstd[:], ALU.mult).then_inc(z_ready, 1)
                if u:
                    split_lo(vp + u + AHEAD)
                for m in STEPS_OF_SLOT.get(u, []):
                    outputs_lo(m)
                if u - ROT_DELAY in ROTATED:
                    i = index_among(u - ROT_DELAY, ROTATED)
                    dve.wait_ge(swapped, i + 1)
                    if i >= 2:
                        dve.wait_ge(z_final, i - 1)
                    nc.vector.tensor_tensor(rot_tmp[:, i % 2, :], ps[4][:, 0:N], c_(C_SIN, N), ALU.mult).then_inc(rot_ready, 1)
                for m in late:
                    attend_late(m)
                if u - 1 in NORMED:
                    i = index_among(u - 1, NORMED)
                    dve.wait_ge(zroot_ready, i + 1)
                    nc.vector.reciprocal(roots[:, i % 2, :], roots[:, i % 2, :]).then_inc(zrstd_ready, 1)
                for g in KEY_SLOTS.get(u, ())[1:2]:
                    dve.wait_ge(keysT_done, g + 1)
                    nc.vector.tensor_copy(keys_of(g), ps[KEYS_BANK[1]][:, :]).then_inc(keysT_dve, 1)
                if u == TOK_SLOT:
                    dve.wait_ge(tok_ready, 3)
                    nc.vector.tensor_scalar(wi_p[:], tok[:, 0:2, 448:456], HEADS ** -0.5, HD ** -0.5,
                                            ALU.mult, ALU.mult).then_inc(wi_ready, 1)
                    dve.wait_ge(wi_ready, 1)
                    dve.wait_ge(wexp_ps, 1)
                    hs = c_(C_HSEL, HEADS).unsqueeze(1).to_broadcast([P, 2, HEADS])
                    link(nc.vector.tensor_tensor(wsel[:], ps[3][:, 0:2 * HEADS].rearrange("p (g h) -> p g h", g=2), hs, ALU.mult))
                    link(nc.vector.tensor_reduce(wcol[:], wsel[:], AX, ALU.add))
                    link(nc.vector.tensor_scalar(wcol[:], wcol[:], HEADS ** -0.5, HD ** -0.5, ALU.mult, ALU.mult))
                    for g in range(2):
                        nc.vector.tensor_scalar(wexp[:, g, :], c_(C_EXPT + g * NS_TOK, NS_TOK), wcol[:, g:g + 1], None,
                                                ALU.mult).then_inc(wexp_ready, 1)

            vu = first["U"][1]

            def merged_lo(j):
                dve.wait_ge(m_hi, j + 1)
                nc.vector.tensor_tensor(mlo[:, j, :], tmp[:, j % 2, 0, :], mhi[:, j, :].bitcast(F32), ALU.subtract).then_inc(m_lo, 1)

            def gate_b(j):
                dve.wait_ge(sig_ready, 2 * j + 2)
                dve.wait_ge(up_b_done, j + 1)
                nc.vector.tensor_tensor(gates[:, 8 + j, :], gates[:, 8 + j, :], ps[UP_B_BANK[j % 4]][:, 0:N],
                                        ALU.mult).then_inc(b_gated, 1)

            gate_b(0)
            gate_b(1)
            outputs_lo(N_STEPS + 1)
            gate_b(2)
            gate_b(3)
            for j in range(8):
                dve.wait_ge(unit_done, vu + j + 1)
                nc.vector.tensor_tensor(gates[:, j, :], gates[:, j, :], ps[UP_A_BANK[j % 4]][:, 0:N],
                                        ALU.mult).then_inc(a_gated, 1)
                dve.wait_ge(a_gated, j + 1)
                dve.wait_ge(b_gated, j + 1)
                nc.vector.tensor_tensor(tmp[:, j % 2, 0, :], gates[:, j, :], gates[:, 8 + j, :], ALU.add).then_inc(m_scaled, 1)
                if j < 6:
                    split_lo(vu + j + AHEAD)
                merged_lo(j)
                if 4 <= j + 1 < 8:
                    gate_b(j + 1)
            for j in (6, 7):
                split_lo(vu + j + AHEAD)
            vo = first["O"][1]
            for j in range(8):
                dve.wait_ge(unit_done, vo + j + 1)
                nc.vector.tensor_tensor(x[:, j, :], ps[7 - j % 2][:, 0:N], x[:, j, :], ALU.add).then_inc(o_evac, 1)
                scale(2, j, o_evac, 0)
                if j < 6:
                    split_lo(vo + j + AHEAD)
                norm_lo(2, j)
            for j in (6, 7):
                split_lo(vo + j + AHEAD)
            gate_up(2)

            def y_out(k):
                dve.wait_ge(yT_done, k + 1)
                bank = ps[k % 2]
                nc.vector.tensor_copy(ytok[:, 0:2, k * P:(k + 1) * P], bank[:, 0:2 * P].rearrange("p (t c) -> p t c", t=2))
                nc.vector.tensor_copy(ytok[0:NS_TOK, 2, k * P:(k + 1) * P], bank[0:NS_TOK, 2 * P:3 * P]).then_inc(y_ready, 1)

            for turn in range(D_LOOPS):
                down_turn(2, 0, 2 * turn)
            for k in range(KB - 2, KB):
                y_out(k)

        @block.tensor
        def _(pe):
            def unit(v, out, xs, it=0, kl=None, start=True, stop=True, x_sem=None, x_base=0, done=None, count=1):
                n, c0, w, nk = units[v]
                pe.wait_ge(w_lo, v + 1 + LOOP_UNITS * it)
                ks = range(nk) if kl is None else kl
                for i, k in enumerate(ks):
                    if x_sem:
                        pe.wait_ge(x_sem, x_base + k + 1)
                    hi, lo, r = xs(k)
                    h, l = whi[0:r, v % NU, k, 0:w], wlo[0:r, v % NU, k, 0:w]
                    nc.tensor.matmul(out[0:w, 0:N], h, hi, start=start and i == 0, stop=False)
                    nc.tensor.matmul(out[0:w, 0:N], h, lo, start=False, stop=False)
                    ins = nc.tensor.matmul(out[0:w, 0:N], l, hi, start=False, stop=stop and done is not False and i == len(ks) - 1)
                if done is not False:
                    ins.then_inc(unit_done if done is None else done, count)

            def tail_block(v, out):
                n, _, _, nk = units[v]
                nc.tensor.matmul(out[:, 0:N], whi[:, v % NU, nk - 1, :], hhi[:, FB - 1, :], start=False, stop=False)
                nc.tensor.matmul(out[:, 0:N], wlo[0:FTAIL, v % NU, nk - 1, :], hhi[0:FTAIL, FB - 1, :],
                                 start=False, stop=True).then_inc(unit_done, 1)

            ident = c_(C_ID, P)
            pe.wait_ge(const_in, 16)
            pe.wait_ge(rows_in, 16)
            nc.tensor.transpose(ps[0][:, 0:GAIN_ROWS], rows[:], cst[0:GAIN_ROWS, C_ID:C_ID + GAIN_ROWS]).then_inc(gains_T, 1)
            for k in range(KB):
                if k == 0:
                    pe.wait_ge(x_in, 32)
                if k == KB // 2:
                    pe.wait_ge(x_rest_in, 16)
                if k >= 4:
                    pe.wait_ge(x_ready, k - 3)
                for t in range(3):
                    r = P if t < 2 else NS_TOK
                    ins = nc.tensor.transpose(ps[4 + k % 4][:, t * P:t * P + r], xtok[0:r, t, k * P:(k + 1) * P],
                                              cst[0:r, C_ID:C_ID + r])
                ins.then_inc(xT_done, 1)

            def mean_square(r):
                if r == 0:
                    pe.wait_ge(consts_in, 16)
                pe.wait_ge(squares_ready, r + 1)
                nc.tensor.matmul(ps[MS_BANK[r]][:, 0:N], c_(C_ONE, P), ssq, start=True, stop=True).then_inc(ms_done, 1)

            normed = lambda k: (nhi[:, k, :], nlo[:, k, :], P)

            def pair(f, p, it=0, r=None):
                v = first[f"G{f}"][1] + 2 * p
                pe.wait_ge(pair_free, (f - 1) * FB + p + 1 + LOOP_PAIRS * it)
                for g in range(2):
                    if r is not None and g == 0:
                        unit(v + g, ps[2 * (p % 3) + g], normed, it, x_sem=n_lo, x_base=KB * r)
                    else:
                        unit(v + g, ps[2 * (p % 3) + g], normed, it)
                    if p < G_HEAD and 2 * p + g == MS_AFTER[f - 1]:
                        mean_square((0, 2)[f - 1])

            def gate_up(f, r):
                for p in range(G_HEAD):
                    pair(f, p, r=r if p == 0 else None)
                with pe.Fori(0, G_LOOPS) as it:
                    for p in range(G_HEAD, G_HEAD + LOOP_PAIRS):
                        pair(f, p, it)
                v = first[f"G{f}"][1] + 2 * (FB - 2)
                for i, (p, g) in enumerate(((FB - 2, 0), (FB - 1, 0), (FB - 2, 1))):
                    if g == 0:
                        pe.wait_ge(pair_free, (f - 1) * FB + p + 1)
                    unit(v + i, ps[2 * (p % 3) + g], normed, count=1 if i < 2 else 2)

            def down_turn(f, it, q0=0, y_blocks={}):
                v = first[f"D{f}"][1] + 6 * q0
                for q in range(2):
                    pe.wait_ge(down_evac, KB * (f - 1) + 2 * (q0 + q) + DOWN_FREE - 2 + 4 * it)
                    for t in range(3):
                        pe.wait_ge(h_lo, (f - 1) * FB + min(FB, KB * (t + 1)))
                        for m in range(2):
                            hidden = lambda k, t=t: (hhi[:, KB * t + k, :], hlo[:, KB * t + k, :], P)
                            unit(v + 6 * q + 2 * t + m, ps[(6, 4)[q] + m], hidden, it, start=t == 0, stop=t == 2,
                                 kl=range(KB if t < 2 else FB - 1 - 2 * KB), done=None if t < 2 else False)
                            if t == 2:
                                tail_block(v + 6 * q + 2 * t + m, ps[(6, 4)[q] + m])
                        for k in y_blocks.get(3 * q + t, ()):
                            y_T(k)

            def keys_T(g):
                if g == 0:
                    pe.wait_ge(pages_in, 16 * 7 * N_SEQ * NPG)
                if g == 1:
                    pe.wait_ge(root_ready, 2)
                if g >= 2:
                    pe.wait_ge((keysT_act, keysT_dve)[g % 2], g // 2)
                for j in range(4):
                    ins = nc.tensor.transpose(ps[KEYS_BANK[g % 2]][:, j * P:(j + 1) * P], kraw[:, g // 4, (g % 4) * 4 + j, :], ident)
                ins.then_inc(keysT_done, 1)

            gate_up(1, 0)
            with pe.Fori(0, D_LOOPS) as it:
                down_turn(1, it)

            def logits(m):
                if m < N_STEPS:
                    kind, form, i = step_kind(m)
                    bank = ps[m % 2]
                    if m >= 2:
                        pe.wait_ge(soft_done, m - 1)
                    if m == 0:
                        pe.wait_ge(tok_ready, 3)
                    if i == 0 and form == 1:
                        pe.wait_ge(z_final, index_among({IDX: U_KI, MOBA: U_QB + 3, DSA: U_QA + 3}[kind], ROTATED) + 1)
                    if form == 2 and i == 0:
                        pe.wait_ge(qz_ready, 2 * (kind + 1))
                        pe.wait_ge(keysT_act, 6)
                        pe.wait_ge(keysT_dve, 6)
                    if m == 8:
                        pe.wait_ge(masks_ready, 5)
                    if kind == DSA and i == 0:
                        pe.wait_ge(sel_ready, {1: 1, 0: 2, 2: 3}[form])
                    k_new = K_OF[kind]
                    if form == 2:
                        if kind != IDX:
                            nc.tensor.matmul(bank[:, 0:NK_S], expb[:, i * P:(i + 1) * P],
                                             masksb[:] if kind == MOBA else sel_s[:], start=True, stop=False)
                        for b in range(4):
                            s = 4 * i + b
                            nc.tensor.matmul(bank[32 * b:32 * b + 32, 0:PAST], qz[:, kind, 32 * s:32 * s + 32],
                                             kt[:, KT_OF[kind], s, :], start=kind == IDX, stop=kind == IDX)
                        ins = nc.tensor.matmul(bank[:, PAST:NK_S], qz[:, kind, i * P:(i + 1) * P], k_new[:, NP_TOK:N],
                                               start=kind == IDX, stop=True)
                    else:
                        half, blocks, w = step_heads(form, i)
                        if kind != IDX:
                            mask = ((causalb[:] if kind == MOBA else sel1[:]) if form == 1
                                    else (causalb[:, P:2 * P] if kind == MOBA else sel0[:]))
                            nh = len(blocks)
                            nc.tensor.matmul(bank[:, :].rearrange("p (h k) -> p h k", h=nh), idb[:],
                                             mask.unsqueeze(1).to_broadcast([P, nh, w]), start=True, stop=False)
                        rows_ = slice(half * HD, (half + 1) * HD)
                        for j, b in enumerate(blocks):
                            ins = nc.tensor.matmul(bank[:, j * w:(j + 1) * w], Q_OF[kind][rows_, b, form * P:(form + 1) * P],
                                                   k_new[rows_, 0:w], start=kind == IDX,
                                                   stop=kind == IDX or j == len(blocks) - 1)
                    ins.then_inc(logits_done, 1)

            def sample_scores():
                pe.wait_ge(wexp_ready, 2)
                for g in range(2):
                    pe.wait_ge(soft_done, 6 + g + 1)
                    nc.tensor.matmul(ps[3][0:NS_TOK, 0:NK_S], wexp[:, g, :], probs[:, g, 0:NK_S],
                                     start=g == 0, stop=g == 1).then_inc(score_ps, 1)

            def probs_T(m):
                if 8 <= m < N_STEPS:
                    n = m - 8
                    form = step_kind(m)[1]
                    pr = probs[:, m % 2, :]
                    pe.wait_ge(probs_ready, n + 1)
                    if n >= 2:
                        pe.wait_ge(probsT_ready, n - 1)
                    if n == 1:
                        pe.wait_ge(score_ready, 1)
                    bank = ps[2 + n % 2]
                    if form == 2:
                        for j in range(2):
                            nc.tensor.transpose(bank[:, j * P:(j + 1) * P], pr[:, j * P:(j + 1) * P], ident)
                        ins = nc.tensor.transpose(bank[0:NS_TOK, 2 * P:3 * P], pr[:, PAST:NK_S], ident)
                    else:
                        for j in range(4):
                            ins = nc.tensor.transpose(bank[:, j * P:(j + 1) * P], pr[:, j * P:(j + 1) * P], ident)
                    ins.then_inc(probsT_done, 1)

            def outputs(m):
                if 8 <= m < N_STEPS:
                    n = m - 8
                    kind, form, i = step_kind(m)
                    g, _ = out_group(m)
                    bank = ps[5 - g % 2]
                    pe.wait_ge(probsT_ready, n + 1)
                    if i == 0 and g >= 2:
                        pe.wait_ge(out_lo, g - 1)
                    if n == 0:
                        pe.wait_ge(zroot_ready, len(NORMED))
                    if g == 1 and i == 0:
                        pe.wait_ge(rot_ready, len(ROTATED))
                    pT = probsT[:, n % 2, :]
                    if form == 2:
                        if kind == DSA and i == 0:
                            pe.wait_ge(va2_ready, 2)
                        v_new = va2[:, :] if kind == DSA else tok[0:NS_TOK, 2, 256:384]
                        cols = slice(i * P, (i + 1) * P)
                        nc.tensor.matmul(bank[:, cols], v_new, pT[0:NS_TOK, 2 * P:3 * P], start=True, stop=False)
                        for b in range(4):
                            for j in range(NPG):
                                pg = (4 * i + b) * NPG + j
                                last = b == 3 and j == NPG - 1
                                rhs = pT[:, j * P + 32 * b:j * P + 32 * b + 32]
                                dst = slice(i * P + 32 * b, i * P + 32 * b + 32)
                                if kind == MOBA:
                                    ins = nc.tensor.matmul(bank[:, dst], vb_pg[:, pg, :], rhs, start=False, stop=last)
                                else:
                                    for s in range(2):
                                        ins = nc.tensor.matmul(bank[s * HD:(s + 1) * HD, dst], va_pg[:, pg, :], rhs,
                                                               start=False, stop=last)
                    else:
                        half, blocks, w = step_heads(form, i)
                        vc = 384 if kind == DSA else 256 + half * HD
                        for j, b in enumerate(blocks):
                            for t in range(w // P):
                                ins = nc.tensor.matmul(bank[half * HD:(half + 1) * HD, b * P:(b + 1) * P],
                                                       tok[:, t, vc:vc + HD], pT[:, (j * (w // P) + t) * P:(j * (w // P) + t + 1) * P],
                                                       start=t == 0, stop=t == w // P - 1)
                    ins.then_inc(pv_done, 1)

            vp = first["P"][1]
            for u in range(U_END):
                for m in STEPS_OF_SLOT.get(u, []):
                    logits(m)
                if u == TOK_SLOT:
                    pe.wait_ge(z_final, index_among(U_KB, ROTATED) + 1)
                    pe.wait_ge(z_ready, U_VW + 1)
                    for t in range(3):
                        r = P if t < 2 else NS_TOK
                        tc_ = slice(t * P, t * P + r)
                        for b, w, c0 in ((0, HD, 0), (1, HD, 64), (2, P, 128), (3, P, 256), (4, HD + HEADS, 384)):
                            ins = nc.tensor.transpose(ps[(2, 3, 0)[t]][0:r, c0:c0 + w], kv[0:w, b, tc_], cst[0:w, C_ID:C_ID + w])
                        ins.then_inc(tok_T, 1)
                if u >= 4:
                    pe.wait_ge(z_ready, last_of_bank(u) + 1)
                unit(vp + u, ps[z_bank(u)], normed, x_sem=n_lo if u == 0 else None, x_base=KB)
                if u == 0:
                    mean_square(1)
                if u - 1 in NORMED:
                    i = index_among(u - 1, NORMED)
                    pe.wait_ge(zsq_ready, i + 1)
                    if i:
                        pe.wait_ge(zroot_ready, i)
                    nc.tensor.matmul(ps[5][:, 0:N], c_(C_BLK, P), act_tmp[:, i % 2, 0, :], start=True, stop=True).then_inc(zms_done, 1)
                if u - ROT_DELAY in ROTATED:
                    i = index_among(u - ROT_DELAY, ROTATED)
                    if u - ROT_DELAY in NORMED:
                        pe.wait_ge(zn_ready, index_among(u - ROT_DELAY, NORMED) + 1)
                    if i:
                        pe.wait_ge(rot_ready, i)
                    nc.tensor.matmul(ps[4][:, 0:N], c_(C_SWAP, P), zloc[u - ROT_DELAY], start=True, stop=True).then_inc(swapped, 1)
                if u == TOK_SLOT:
                    pe.wait_ge(tok_ready, 3)
                    for g in range(2):
                        ins = nc.tensor.matmul(ps[3][:, g * HEADS:(g + 1) * HEADS], c_(C_EXP + g * P, P, NS_TOK),
                                               tok[0:NS_TOK, 2, 448:456], start=True, stop=True)
                    ins.then_inc(wexp_ps, 1)
                for g in KEY_SLOTS.get(u, ()):
                    keys_T(g)
                for m in STEPS_OF_SLOT.get(u, []):
                    if m == 7:
                        sample_scores()
                    outputs(m - 2)
                    probs_T(m - 1)

            vu = first["U"][1]
            up_a = lambda j: unit(vu + j, ps[UP_A_BANK[j % 4]], lambda k: (ahi[:, k, :], alo[:, k, :], P), kl=range(4))
            up_b = lambda j: unit(vu + j, ps[UP_B_BANK[j % 4]], lambda k: (bhi[:, k - 4, :], blo[:, k - 4, :], P),
                                  kl=range(4, 8), done=up_b_done)
            pe.wait_ge(out_lo, 3)
            pe.wait_ge(z_ready, U_END - 1)
            up_b(0)
            outputs(N_STEPS - 2)
            probs_T(N_STEPS - 1)
            pe.wait_ge(z_ready, U_END)
            up_b(1)
            outputs(N_STEPS - 1)
            up_b(2)
            up_b(3)
            pe.wait_ge(out_lo, 6)
            for j in range(8):
                if j >= 4:
                    pe.wait_ge(b_gated, j - 3)
                    up_b(j)
                    pe.wait_ge(a_gated, j - 3)
                up_a(j)
            vo = first["O"][1]
            for j in range(8):
                if j >= 2:
                    pe.wait_ge(o_evac, j - 1)
                else:
                    pe.wait_ge(b_gated, 5 + j)
                unit(vo + j, ps[7 - j % 2], lambda k: (mhi[:, k, :], mlo[:, k, :], P), x_sem=m_lo if j == 0 else None)
            gate_up(2, 2)

            def y_T(k):
                pe.wait_ge(down_evac, DOWN_FREE + KB + k + 1)
                if k >= 2:
                    pe.wait_ge(y_ready, k - 1)
                for t in range(3):
                    r = P if t < 2 else NS_TOK
                    ins = nc.tensor.transpose(ps[k % 2][0:r, t * P:(t + 1) * P], x[:, k, t * P:t * P + r], ident)
                ins.then_inc(yT_done, 1)

            down_turn(2, 0, 0, y_blocks={3: (0, 1)})
            down_turn(2, 0, 2, y_blocks={0: (2, 3), 3: (4, 5)})
            for k in range(KB - 2, KB):
                y_T(k)


INPUTS = ("x_prompt x_sample cache_k_a cache_v_a cache_kidx_a cache_k_b cache_v_b page_table ffn1_w_in "
          "ffn1_w_out w_in w_up_a w_up_b w_out ffn2_w_in ffn2_w_out").split()
WIDE_GAINS = "ffn1_norm mix_norm ffn2_norm gate_bias".split()
HEAD_GAINS = "q_norm_a k_norm_a q_norm_b k_norm_b".split()
LAYER_WEIGHTS = "ffn1_w_in ffn1_w_out w_in w_up_a w_up_b w_out ffn2_w_in ffn2_w_out".split()


def kernel(**inputs):
    import concourse.bacc as bacc
    from concourse.bass_utils import run_bass_kernel_spmd

    nc = bacc.Bacc("TRN2", target_bir_lowering=False, num_devices=1)
    arrays, a = {}, {}
    for name in INPUTS:
        v = np.ascontiguousarray(inputs[name])
        arrays[f"in_{name}"] = v
        a[name] = nc.dram_tensor(f"in_{name}", v.shape, mybir.dt.from_np(v.dtype), kind="ExternalInput").ap()
    for name in LAYER_WEIGHTS:
        a[name] = a[name].rearrange("l r c -> (l r) c")
    rows = [np.asarray(inputs[n]).reshape(-1, P) for n in WIDE_GAINS]
    rows += [np.tile(np.asarray(inputs[n]).reshape(1, HD), (1, 2)) for n in HEAD_GAINS]
    arrays["in_gain_rows"] = np.ascontiguousarray(np.concatenate(rows))
    a["gain_rows"] = nc.dram_tensor("in_gain_rows", (GAIN_ROWS, P), F32, kind="ExternalInput").ap()
    arrays["in_constants"] = shape_constants()
    a["constants"] = nc.dram_tensor("in_constants", (P, C_ALL), F32, kind="ExternalInput").ap()
    returned = [("y_prompt", (1, NP_TOK, D)), ("y_sample", (N_SEQ, N_NEW, D))]
    for g, lead in (("p", (1, 1, NP_TOK)), ("s", (1, N_SEQ, N_NEW))):
        returned += [(f"new_k_a_{g}", lead + (1, HD)), (f"new_v_a_{g}", lead + (1, HD)), (f"new_kidx_{g}", lead + (HD,)),
                     (f"new_k_b_{g}", lead + (2, HD)), (f"new_v_b_{g}", lead + (2, HD))]
    o = {}
    for name, shape in returned:
        t = nc.dram_tensor(f"out_{name}", shape, F32, kind="ExternalOutput").ap()
        if name.endswith("_p"):
            t = t.rearrange("l b (t p) d -> p (l b t) d" if len(shape) == 4 else "l b (t p) h d -> p (l b t) (h d)", p=P)
        elif name.endswith("_s"):
            t = t.rearrange("l b t d -> (l b t) d" if len(shape) == 4 else "l b t h d -> (l b t) (h d)")
        o[name] = t
    build(nc, a, o)
    r = run_bass_kernel_spmd(nc, [arrays], core_ids=[0])
    return tuple(r.results[0][f"out_{name}"] for name, _ in returned)
```
